# Optimizing a Trainium2 kernel written in Bass

```python
import jax, jax.numpy as jnp
from jax import lax
import numpy as np

D_MODEL = 1024
BATCH = 1
SEQ = 1024
DEPTH = 1

HEAD_DIM = 64
N_HEADS_DIL = 8
N_HEADS_SB = 8
DIL_WIDTH = N_HEADS_DIL * HEAD_DIM
SB_WIDTH = N_HEADS_SB * HEAD_DIM
DIL_PATTERNS = ((128, 1), (512, 4), (2048, 16))
BLOCK = 128
ROPE_THETA = 500000.0
ROPE_DIM = HEAD_DIM // 4
N_MEM = 256
N_HEADS_MEM = 4
MEM_HEAD_DIM = 128
MEM_WIDTH = N_HEADS_MEM * MEM_HEAD_DIM
D_FF = -(-(8 * D_MODEL) // (3 * 256)) * 256
IN_COLS = 3 * DIL_WIDTH + 3 * SB_WIDTH + 2 * D_MODEL
RMS_EPS = 1e-6
MAX_POS_OFFSET = 1024

kernel_name = "hybrid_dilated_stickbreak_gated_block"

def _rmsnorm(x, g):
    xf = x.astype(jnp.float32)
    y = xf * lax.rsqrt(jnp.mean(xf * xf, axis=-1, keepdims=True) + RMS_EPS)
    return (y * g.astype(jnp.float32)).astype(x.dtype)

def _partial_rope(x, positions):
    half = ROPE_DIM // 2
    inv_freq = ROPE_THETA ** (-jnp.arange(half, dtype=jnp.float32) / half)
    ang = positions.astype(jnp.float32)[:, None, :, None] * inv_freq
    cos, sin = jnp.cos(ang), jnp.sin(ang)
    xf = x.astype(jnp.float32)
    x1, x2 = xf[..., :half], xf[..., half:ROPE_DIM]
    out = jnp.concatenate([x1 * cos - x2 * sin, x2 * cos + x1 * sin, xf[..., ROPE_DIM:]], axis=-1)
    return out.astype(x.dtype)

def _dilated_pattern(q, k, v, window, dilation):
    B, H, S, hd = q.shape
    L = S // dilation
    n_back = window // dilation
    C = BLOCK
    nb = -(-L // C)
    Lp = nb * C

    def to_stream(t):
        t = t.reshape(B, H, L, dilation, hd).transpose(0, 1, 3, 2, 4)
        t = jnp.pad(t, ((0, 0), (0, 0), (0, 0), (0, Lp - L), (0, 0)))
        return t.reshape(B, H, dilation, nb, C, hd)

    def with_prev(t):
        prev = jnp.pad(t, ((0, 0), (0, 0), (0, 0), (1, 0), (0, 0), (0, 0)))[:, :, :, :-1]
        return jnp.concatenate([prev, t], axis=4)

    qs = to_stream(q)
    kb = with_prev(to_stream(k))
    vb = with_prev(to_stream(v)).astype(jnp.float32)
    s = jnp.einsum('bhrnqd,bhrnkd->bhrnqk', qs, kb,
                   preferred_element_type=jnp.float32) * (hd ** -0.5)
    i = jnp.arange(C)[:, None]
    j = jnp.arange(2 * C)[None, :]
    dist = C + i - j
    band = (dist >= 0) & (dist <= n_back)
    in_cur = j >= C
    blk = jnp.arange(nb)[:, None, None]
    valid = band[None] & ((blk > 0) | in_cur[None])
    s = jnp.where(valid, s, -jnp.inf)
    m = jnp.max(s, axis=-1, keepdims=True)
    p = jnp.exp(s - m)
    den = jnp.sum(p, axis=-1)
    o = jnp.einsum('bhrnqk,bhrnkd->bhrnqd', p, vb) / den[..., None]
    lse = m[..., 0] + jnp.log(den)

    def from_stream(t):
        rest = t.shape[5:]
        t = t.reshape((B, H, dilation, Lp) + rest)[:, :, :, :L]
        t = jnp.moveaxis(t, 2, 3)
        return t.reshape((B, H, S) + rest)

    return from_stream(o), from_stream(lse)

def _dilated_attention(q, k, v):
    outs, lses = [], []
    for window, dilation in DIL_PATTERNS:
        o, lse = _dilated_pattern(q, k, v, window, dilation)
        outs.append(o)
        lses.append(lse)
    alpha = jax.nn.softmax(jnp.stack(lses, axis=0), axis=0)
    return jnp.einsum('gbhs,gbhsd->bhsd', alpha, jnp.stack(outs, axis=0))

def _stick_breaking(q, k, v):
    B, H, S, hd = q.shape
    nb = S // BLOCK
    qb = q.reshape(B, H, nb, BLOCK, hd).transpose(2, 0, 1, 3, 4)
    vf = v.astype(jnp.float32)
    kpos = jnp.arange(S)

    def block(args):
        qi, bi = args
        z = jnp.einsum('bhqd,bhkd->bhqk', qi, k,
                       preferred_element_type=jnp.float32) * (hd ** -0.5)
        qpos = bi * BLOCK + jnp.arange(BLOCK)
        strict = kpos[None, :] < qpos[:, None]
        log1m = jnp.where(strict, jax.nn.log_sigmoid(-z), 0.0)
        between = lax.cumsum(log1m, axis=3, reverse=True) - log1m
        a = jnp.where(strict, jnp.exp(jax.nn.log_sigmoid(z) + between), 0.0)
        return jnp.einsum('bhqk,bhkd->bhqd', a, vf)

    o = lax.map(block, (qb, jnp.arange(nb)))
    return o.transpose(1, 2, 0, 3, 4).reshape(B, H, S, hd)

def _memory_attention(hn, mem_n, w_q, w_kv, w_o):
    B, S, _ = hn.shape
    q = (hn @ w_q).reshape(B, S, N_HEADS_MEM, MEM_HEAD_DIM)
    kv = mem_n @ w_kv
    k = kv[..., :MEM_WIDTH].reshape(B, N_MEM, N_HEADS_MEM, MEM_HEAD_DIM)
    v = kv[..., MEM_WIDTH:].reshape(B, N_MEM, N_HEADS_MEM, MEM_HEAD_DIM)
    s = jnp.einsum('bshd,bmhd->bhsm', q, k,
                   preferred_element_type=jnp.float32) * (MEM_HEAD_DIM ** -0.5)
    p = jax.nn.softmax(s, axis=-1)
    o = jnp.einsum('bhsm,bmhd->bshd', p, v.astype(jnp.float32))
    return o.reshape(B, S, MEM_WIDTH).astype(hn.dtype) @ w_o

def _swiglu(n, w_gate, w_up, w_down):
    return (jax.nn.silu(n @ w_gate) * (n @ w_up)) @ w_down

def setup_inputs(seed: int = 0) -> dict:
    key = jax.random.key(seed)
    ks = jax.random.split(key, 20)

    def w(k, shape):
        return jax.random.normal(k, shape, jnp.float32) * (shape[-2] ** -0.5)

    def gain(k, shape):
        return 1.0 + 0.01 * jax.random.normal(k, shape, jnp.float32)

    x = jax.random.normal(ks[0], (BATCH, SEQ, D_MODEL), jnp.float32)
    mem = jax.random.normal(ks[1], (BATCH, N_MEM, D_MODEL), jnp.float32)
    offs = jax.random.randint(ks[2], (BATCH, 1), 0, MAX_POS_OFFSET, dtype=jnp.int32)
    positions = offs + jnp.arange(SEQ, dtype=jnp.int32)[None, :]
    return {
        "x": x,
        "mem": mem,
        "positions": positions,
        "g_mix": gain(ks[3], (DEPTH, D_MODEL)),
        "w_in": w(ks[4], (DEPTH, D_MODEL, IN_COLS)),
        "w_up_a": w(ks[5], (DEPTH, DIL_WIDTH, D_MODEL)),
        "w_up_b": w(ks[6], (DEPTH, SB_WIDTH, D_MODEL)),
        "w_out": w(ks[7], (DEPTH, D_MODEL, D_MODEL)),
        "g_mem_q": gain(ks[8], (DEPTH, D_MODEL)),
        "g_mem_kv": gain(ks[9], (DEPTH, D_MODEL)),
        "w_q_mem": w(ks[10], (DEPTH, D_MODEL, MEM_WIDTH)),
        "w_kv_mem": w(ks[11], (DEPTH, D_MODEL, 2 * MEM_WIDTH)),
        "w_o_mem": w(ks[12], (DEPTH, MEM_WIDTH, D_MODEL)),
        "g_ffn": gain(ks[13], (DEPTH, D_MODEL)),
        "w_ffn_gate": w(ks[14], (DEPTH, D_MODEL, D_FF)),
        "w_ffn_up": w(ks[15], (DEPTH, D_MODEL, D_FF)),
        "w_ffn_down": w(ks[16], (DEPTH, D_FF, D_MODEL)),
        "g_final": gain(ks[17], (D_MODEL,)),
    }

def reference(x, mem, positions, g_mix, w_in, w_up_a, w_up_b, w_out, g_mem_q, g_mem_kv,
              w_q_mem, w_kv_mem, w_o_mem, g_ffn, w_ffn_gate, w_ffn_up, w_ffn_down, g_final):
    B, S, _ = x.shape
    split_at = list(np.cumsum([DIL_WIDTH, DIL_WIDTH, DIL_WIDTH,
                               SB_WIDTH, SB_WIDTH, SB_WIDTH, D_MODEL]))

    def heads(t, nh):
        return t.reshape(B, S, nh, HEAD_DIM).transpose(0, 2, 1, 3)

    def merge(t):
        return t.transpose(0, 2, 1, 3).reshape(B, S, -1).astype(x.dtype)

    h = x
    for l in range(DEPTH):
        n = _rmsnorm(h, g_mix[l])
        proj = n @ w_in[l]
        qa, ka, va, qb, kb, vb, gate_a, gate_b = jnp.split(proj, split_at, axis=-1)
        qa = _partial_rope(heads(qa, N_HEADS_DIL), positions)
        ka = _partial_rope(heads(ka, N_HEADS_DIL), positions)
        o_a = merge(_dilated_attention(qa, ka, heads(va, N_HEADS_DIL)))
        o_b = merge(_stick_breaking(heads(qb, N_HEADS_SB), heads(kb, N_HEADS_SB),
                                    heads(vb, N_HEADS_SB)))
        mixed = (jax.nn.sigmoid(gate_a) * (o_a @ w_up_a[l])
                 + jax.nn.sigmoid(gate_b) * (o_b @ w_up_b[l]))
        h = h + mixed @ w_out[l]
        h = h + _memory_attention(_rmsnorm(h, g_mem_q[l]), _rmsnorm(mem, g_mem_kv[l]),
                                  w_q_mem[l], w_kv_mem[l], w_o_mem[l])
        h = h + _swiglu(_rmsnorm(h, g_ffn[l]), w_ffn_gate[l], w_ffn_up[l], w_ffn_down[l])
    return _rmsnorm(h, g_final)


_drawn_inputs = setup_inputs


def setup_inputs(seed=0):
    import zlib

    import numpy as np

    out = dict(_drawn_inputs(seed))
    spreads = {}
    factors = {'g_mix': 8.0, 'g_mem_q': 8.0, 'g_mem_kv': 8.0, 'g_ffn': 7.79, 'g_final': 5.751}
    for name, (base, spread) in spreads.items():
        noise = np.random.default_rng([zlib.crc32(name.encode()), seed]).standard_normal(out[name].shape)
        drawn = base * np.exp(spread * noise) if base else spread * noise
        out[name] = __import__('jax').numpy.asarray(drawn.astype(out[name].dtype))
    for name, factor in factors.items():
        out[name] = (out[name] * factor).astype(out[name].dtype)
    return out
```

```python
from contextlib import ExitStack

import concourse.bass as bass
from concourse import mybir

ALU = mybir.AluOpType
ACT = mybir.ActivationFunctionType
F32 = mybir.dt.float32
F32R = mybir.dt.float32r
I32 = mybir.dt.int32
AX_X = mybir.AxisListType.X

P = 128
T = 1024
D = 1024
KT = D // P
HALF = 512
NB = T // P
HD = 64
PAIRS = 4
NM = 256
MH = 4
FF = 2816
FPAIRS = FF // P // 2
EPS = 1e-6
TINY = -1.0e30
NEG_MAX = -3.0e38

TILES_IN = 10
N_TILES = PAIRS * TILES_IN + KT + KT + MH + 2 * MH + KT // 2 + 6 * FPAIRS

G_MIX, G_MEMQ, G_MEMKV, G_FFN, G_FINAL = (KT * n for n in range(5))

UNITS = 32
ORDER = [(h, (b if h == 0 else NB - 1 - b)) for b in range(NB) for h in range(2)]
QA, KA, VA, KB, TA, QB, VB, TB, GATE = 0, 2, 4, 6, 8, 10, 12, 14, 16
BANKS_ROUND = 24
SLOTS = UNITS + 4


def filler_plan():
    plan = [[] for _ in range(SLOTS)]
    for n in range(12):
        plan[n].append((QB + n // 3, n % 3))
    plan[12] += [(TB, None), (TB + 1, None)]
    slots = list(range(13, 34)) + [18, 22, 26]
    for n, s in enumerate(sorted(slots)):
        plan[s].append((GATE + n // 3, n % 3))
    return plan


FILLERS = filler_plan()


def finished_in(slot):
    if slot == 0:
        return [TA, TA + 1]
    if slot > SLOTS:
        return []
    return [u for u, p in FILLERS[slot - 1] if p in (2, None)]


def tile_of(unit):
    return {QA: 0, KA: 1, VA: 2, KB: 3, QB: 4, VB: 5}.get(unit - unit % 2, 6 + (unit - GATE) // 2)


def blk(n, size=P):
    return slice(n * size, (n + 1) * size)


def build(nc, xT, memT, positions, gains, weights, ident_d, rope_d, bias_d, mask_d, outT):
    with ExitStack() as ctx:
        gates_d = nc.dram_tensor("gates_scratch", [2 * KT, P, T], F32, kind="Internal").ap()
        o_d = nc.dram_tensor("o_scratch", [KT, P, T], F32, kind="Internal").ap()

        def sem(name):
            return ctx.enter_context(nc.semaphore(name))

        def keep(name, shape, dt):
            return ctx.enter_context(nc.sbuf_tensor(name, shape, dt))

        stage = keep("w_stage", [P, 2, KT * P], F32)
        w_hi = keep("w_hi", [P, 2, KT * P], F32R)
        w_lo = keep("w_lo", [P, 2, KT * P], F32R)
        n_hi = keep("n_hi", [P, KT, T], F32R)
        n_lo = keep("n_lo", [P, KT, T], F32R)
        rms = keep("rms", [P, T], F32)
        ident = keep("ident", [P, P], F32)
        mean_w = keep("mean_w", [P, P], F32)
        gain = keep("gain", [P, 5 * KT], F32)
        eps_col = keep("eps_col", [P, 1], F32)
        rope_c = keep("rope_c", [P, 2], F32)
        stat = keep("stat", [P, 4, 4], F32)

        def phase(*tensors):
            with ExitStack() as p:
                return [p.enter_context(nc.sbuf_tensor(n, s, d)) for n, s, d in tensors]

        (x_f,) = phase(("x_f", [P, KT, T], F32))
        (sin_t, cos_t, pad0, sq0, pos_i, ang, rnd) = phase(
            ("sin_t", [P, T], F32), ("cos_t", [P, T], F32), ("pad0", [P, KT - 2, T], F32),
            ("sq0", [P, 2, T], F32), ("pos_i", [P, T], I32), ("ang", [P, T], F32),
            ("rnd", [P, 2, T], F32))
        (sin_t, cos_t, qkA_q_hi, qkA_q_lo, qkA_k_hi, qkA_k_lo, qkB_q_hi, qkB_q_lo, qkB_k_hi,
         qkB_k_lo, vA, vB, pt_hi, pt_lo, rows, e_row, r_row, raw, swap, bias_A, mask_B,
         o_low, o_sum) = phase(
            ("sin_m", [P, T], F32), ("cos_m", [P, T], F32),
            *[(f"qk{n}", [P, T], F32R) for n in range(8)],
            ("vA", [P, NB, 2, 2, HD], F32R), ("vB", [P, NB, 2, 2, HD], F32R),
            ("pt_hi", [P, T], F32R), ("pt_lo", [P, T], F32R),
            ("rows", [P, 3, T], F32), ("e_row", [P, T], F32), ("r_row", [P, T], F32),
            ("raw", [P, 3, T], F32), ("swap", [P, T], F32),
            ("bias_A", [P, T], F32), ("mask_B", [P, P], F32),
            ("o_low", [HD, 2, P], F32), ("o_sum", [HD, 2, P], F32))
        qk = {"A": (qkA_q_hi, qkA_q_lo, qkA_k_hi, qkA_k_lo), "B": (qkB_q_hi, qkB_q_lo, qkB_k_hi, qkB_k_lo)}
        v_of = {"A": vA, "B": vB}
        (m_hi, m_lo, o_stage, g_a, g_b, y_a, y_b) = phase(
            ("m_hi", [P, KT, T], F32R), ("m_lo", [P, KT, T], F32R), ("o_stage", [P, 2, T], F32),
            ("g_a", [P, 2, T], F32), ("g_b", [P, 2, T], F32),
            ("y_a", [P, 2, HALF], F32), ("y_b", [P, 2, HALF], F32))
        (_, h, sq, q_t, mem_f, mem_r) = phase(
            ("pad_m", [P, 2 * KT, T], F32), ("h", [P, KT, T], F32), ("sq", [P, T], F32),
            ("q_t", [P, T], F32), ("mem_f", [P, KT, NM], F32), ("mem_r", [P, NM], F32))
        (qm_hi, qm_lo, km_hi, km_lo, vm_hi, vm_lo, mg_hi, mg_lo, _, p_m, pm_hi, pm_lo) = phase(
            ("qm_hi", [P, MH, T], F32R), ("qm_lo", [P, MH, T], F32R),
            ("km_hi", [P, MH, NM], F32R), ("km_lo", [P, MH, NM], F32R),
            ("vm_hi", [P, 2, MH * P], F32R), ("vm_lo", [P, 2, MH * P], F32R),
            ("mg_hi", [P, KT, NM], F32R), ("mg_lo", [P, KT, NM], F32R),
            ("pad_e", [P, KT + 2, T], F32),
            ("p_m", [P, 3, NM], F32), ("pm_hi", [P, 2, P], F32R), ("pm_lo", [P, 2, P], F32R))
        (a_hi, a_lo, g_f, u_f) = phase(
            ("a_hi", [P, 2, T], F32R), ("a_lo", [P, 2, T], F32R),
            ("g_f", [P, 2, T], F32), ("u_f", [P, 2, T], F32))

        ps = ctx.enter_context(nc.psum_tensor("ps", [P, 8, HALF], F32))
        ps_rows = ps[:, 2:4, :].rearrange("p b n -> p (b n)")
        ps_t = ps[:, 4:6, :].rearrange("p b n -> p (b n)")

        const_in, bias_in, pos_in = sem("const_in"), sem("bias_in"), sem("pos_in")
        x_tile = [sem(f"x_tile{k}") for k in range(KT)]
        w_in_s = [sem("w_stage0_in"), sem("w_stage1_in")]
        w_rounded, w_split, w_begun = sem("w_rounded"), sem("w_split"), sem("w_begun")
        bank_full, bank_free = sem("bank_full"), sem("bank_free")
        act_step, dve_step = sem("act_step"), sem("dve_step")
        squared, summed, mean_full, rms_raw, rms_ready = (
            sem("squared"), sem("summed"), sem("mean_full"), sem("rms_raw"), sem("rms_ready"))
        nhi_ready, nlo_ready = sem("nhi_ready"), sem("nlo_ready")
        ang_ready, sin_ready = sem("ang_ready"), sem("sin_ready")
        swap_in, rope_done = [sem("swap_q"), sem("swap_k")], sem("rope_done")
        qk_hi_s, qk_lo_s, vt_hi_s = sem("qk_hi"), sem("qk_lo"), sem("vt_hi")
        gate_out = [sem("gate_out0"), sem("gate_out1")]
        logits_full, logits_free = sem("logits_full"), sem("logits_free")
        max_ready, exp_ready, pA_ready, pB_ready = sem("max_ready"), sem("exp_ready"), sem("pA_ready"), sem("pB_ready")
        abs_ready, soft_ready, arg_ready = sem("abs_ready"), sem("soft_ready"), sem("arg_ready")
        pt_full, pt_hi_s, pt_lo_s, av_full = sem("pt_full"), sem("pt_hi_s"), sem("pt_lo_s"), sem("av_full")
        o_low_s, o_sum_s, o_out = sem("o_low_s"), sem("o_sum_s"), [sem("o_out0"), sem("o_out1")]
        o_in, o_hi_s, o_lo_s = [sem("o_in0"), sem("o_in1")], sem("o_hi_s"), sem("o_lo_s")
        g_in, g_ready = [sem("g_in0"), sem("g_in1")], sem("g_ready")
        y_ready, m_hi_s, m_lo_s = sem("y_ready"), sem("m_hi_s"), sem("m_lo_s")
        h_in, mem_in = sem("h_in"), sem("mem_in")
        qm_hi_s, qm_lo_s = sem("qm_hi_s"), sem("qm_lo_s")
        msq, mmean, mrms_raw, mrms, mg_f, mg_hi_s, mg_lo_s = (
            sem("msq"), sem("mmean"), sem("mrms_raw"), sem("mrms"), sem("mg_f"), sem("mg_hi_s"), sem("mg_lo_s"))
        kv_hi_s = sem("kv_hi_s")
        ms_full, mx_ready, mp_exp, mr_ready, mp_ready = (
            sem("ms_full"), sem("mx_ready"), sem("mp_exp"), sem("mr_ready"), sem("mp_ready"))
        mt_full, mt_hi, mt_lo, mav_full, om_hi, om_lo = (
            sem("mt_full"), sem("mt_hi"), sem("mt_lo"), sem("mav_full"), sem("om_hi"), sem("om_lo"))
        silu_ready, hidden_ready, a_hi_s, a_lo_s = sem("silu_ready"), sem("hidden_ready"), sem("a_hi_s"), sem("a_lo_s")
        out_ready, out_done = sem("out_ready"), sem("out_done")

        B_MIX = 2
        B_GATED = B_MIX + PAIRS * BANKS_ROUND
        B_OUT = B_GATED + 4 * KT
        B_QM = B_OUT + 2 * KT
        B_KV = B_QM + 2 * MH
        B_OM = B_KV + 2 * MH
        B_FF = B_OM + 2 * KT
        B_FF_LOOP = B_FF + 8
        B_END = B_FF_LOOP + 24 * (FPAIRS - 1)
        W_GATED = PAIRS * TILES_IN
        W_OUT = W_GATED + KT
        W_QM = W_OUT + KT
        W_KV = W_QM + MH
        W_OM = W_KV + 2 * MH
        W_FF = W_OM + KT // 2
        W_FF_LOOP = W_FF + 4
        W_END = W_FF_LOOP + 6 * (FPAIRS - 1)
        assert W_END + 2 == N_TILES

        def apart(eng):
            eng.nop(nofuse=True)

        block = ctx.enter_context(nc.Block())

        @block.sync
        def _(sp):
            sp.dma_start(ident[:], ident_d).then_inc(const_in, 16)
            sp.dma_start(gain[:], gains).then_inc(const_in, 16)
            sp.dma_start(rope_c[:], rope_d).then_inc(const_in, 16)
            for k in range(0, KT, 2):
                sp.dma_start(x_f[:, k, :], xT[k]).then_inc(x_tile[k], 16)
            sp.dma_start(pos_i[:], positions.partition_broadcast(P)).then_inc(pos_in, 16)
            for b in range(2):
                sp.dma_start(stage[:, b, :], weights[b]).then_inc(w_in_s[b], 16)
            with sp.Fori(1, N_TILES // 2) as i:
                for b in range(2):
                    sp.wait_ge(w_split, i * 2 + (b - 1))
                    src = weights[bass.ds(i * 2 + b, 1), :, :].rearrange("o p n -> p (o n)")
                    sp.dma_start(stage[:, b, :], src).then_inc(w_in_s[b], 16)

        @block.gpsimd
        def _(pool):
            def split(b, loaded, tile_free, number):
                pool.wait_ge(w_in_s[b], loaded)
                if tile_free is not None:
                    pool.wait_ge(w_begun, tile_free)
                apart(pool)
                pool.tensor_scalar(w_hi[:, b, :], stage[:, b, :], 1.0, 1.0, ALU.mult, ALU.mult).then_inc(w_rounded, 1)
                pool.wait_ge(w_rounded, number)
                pool.tensor_tensor(w_lo[:, b, :], stage[:, b, :], w_hi[:, b, :].bitcast(F32),
                                   ALU.subtract).then_inc(w_split, 1)

            for b in range(2):
                split(b, 16, None, b + 1)
            with pool.Fori(1, N_TILES // 2) as i:
                for b in range(2):
                    split(b, i * 16 + 16, i * 2 + b, i * 2 + (b + 1))

        @block.tensor
        def _(pe):
            def passes(bank, units, mv_hi, mv_lo, which, ks, first, last):
                n = 0
                total = len(which) * len(ks)
                for p in which:
                    w = w_lo if p == 2 else w_hi
                    mv = mv_lo if p == 1 else mv_hi
                    for k in ks:
                        b, c = units(k)
                        ins = pe.matmul(bank, w[:, b, c:c + P], mv(k), start=(first and n == 0),
                                        stop=(last and n == total - 1))
                        if n == 0:
                            lead = ins
                        n += 1
                return lead, ins

            def begin_tile(number):
                pe.wait_ge(w_split, number)

            def product(bank, b, half, which=(0, 1, 2), hi=None, lo=None):
                hi, lo = hi or n_hi, lo or n_lo
                return passes(bank, lambda k: (b, k * P), lambda k: hi[:, k, blk(half, HALF)],
                              lambda k: lo[:, k, blk(half, HALF)], which, range(KT), which[0] == 0, which[-1] == 2)

            def mean(number):
                pe.wait_ge(summed, number)
                for half in range(2):
                    pe.matmul(ps[:, 6 + half, :], mean_w[:], rms[:, blk(half, HALF)], start=True,
                              stop=True).then_inc(mean_full, 1)

            pe.wait_ge(const_in, 48)
            pe.wait_ge(summed, KT)
            for half in range(2):
                pe.matmul(ps[:, half, :], mean_w[:], rms[:, blk(half, HALF)], start=True, stop=True
                          ).then_inc(bank_full, 1)
            pe.wait_ge(nlo_ready, KT)

            def round_(i):
                def unit_pass(u, p):
                    t = tile_of(u)
                    if p == 0:
                        if u % 2 == 0:
                            begin_tile(i * TILES_IN + (t + 1))
                        order = B_MIX + i * BANKS_ROUND + (u - 1)
                        pe.wait_ge(bank_free, order if u >= 1 else B_MIX + i * BANKS_ROUND)
                    lead, last = product(ps[:, u % 2, :], t % 2, u % 2, (p,))
                    if p == 0 and u % 2 == 0:
                        lead.then_inc(w_begun, 1)
                    if p == 2:
                        last.then_inc(bank_full, 1)

                def v_transposes(u):
                    pe.wait_ge(bank_free, B_MIX + i * BANKS_ROUND + (u - 1))
                    pe.wait_ge(bank_free, B_MIX + i * BANKS_ROUND + ((VA if u < QB else VB) + 2))
                    for n in range(4):
                        ins = pe.transpose(ps[:, u % 2, blk(n)], raw[:, 2, blk((u % 2) * 4 + n)], ident[:])
                    ins.then_inc(bank_full, 1)

                def logits(u):
                    m = "AB"[u // 16]
                    hd, qb = ORDER[u % 16]
                    q_hi, q_lo, k_hi, k_lo = qk[m]
                    if u == 0:
                        pe.wait_ge(qk_lo_s, i * 4 + 2)
                    if u == 16:
                        pe.wait_ge(qk_lo_s, i * 4 + 4)
                    if u:
                        pe.wait_ge(logits_free, i * UNITS + u)
                    hs = slice(hd * HD, (hd + 1) * HD)
                    width = (qb + 1) * P
                    for c in range(0, width, HALF):
                        w = min(HALF, width - c)
                        for n, (a, b) in enumerate(((q_hi, k_hi), (q_hi, k_lo), (q_lo, k_hi))):
                            ins = pe.matmul(ps[:, 2 + c // HALF, 0:w], a[hs, blk(qb)], b[hs, c:c + w],
                                            start=(n == 0), stop=(n == 2))
                    ins.then_inc(logits_full, 1)

                def transposes(u):
                    if u < 16:
                        pe.wait_ge(pA_ready, i * 16 + (u + 1))
                    else:
                        pe.wait_ge(pB_ready, i * 16 + (u - 15))
                    if u:
                        pe.wait_ge(pt_lo_s, i * UNITS + u)
                    for kb in range(ORDER[u % 16][1] + 1):
                        ins = pe.transpose(ps_t[:, blk(kb)], rows[:, u % 3, blk(kb)], ident[:])
                    ins.then_inc(pt_full, 1)

                def attend(u):
                    hd, qb = ORDER[u % 16]
                    v = v_of["AB"[u // 16]]
                    if u % 16 == 0:
                        pe.wait_ge(bank_free, B_MIX + i * BANKS_ROUND + ((TA if u == 0 else TB) + 2))
                    pe.wait_ge(pt_lo_s, i * UNITS + (u + 1))
                    if u >= 2:
                        pe.wait_ge(o_sum_s, i * UNITS + (u - 1))
                    n = 0
                    for kb in range(qb + 1):
                        for part in (pt_hi, pt_lo):
                            ins = pe.matmul(ps[:, 6 + u % 2, 0:P], v[:, kb, hd, :, :].rearrange("p a d -> p (a d)"),
                                            part[:, blk(kb)], start=(n == 0), stop=(n == 2 * qb + 1))
                            n += 1
                    ins.then_inc(av_full, 1)

                for u in range(QA, TA):
                    for p in range(3):
                        unit_pass(u, p)
                v_transposes(TA)
                v_transposes(TA + 1)
                for s in range(SLOTS):
                    if 0 <= s - 2 < UNITS:
                        transposes(s - 2)
                    if s < UNITS:
                        logits(s)
                    for u, p in FILLERS[s]:
                        if p is None:
                            v_transposes(u)
                        else:
                            unit_pass(u, p)
                    if 0 <= s - 2 < UNITS:
                        attend(s - 2)

            with pe.Fori(0, PAIRS) as i:
                round_(i)

            pe.wait_ge(o_lo_s, KT)
            pe.wait_ge(bank_free, B_GATED)
            with pe.Fori(0, KT // 2) as i:
                for b in range(2):
                    begin_tile(i * 2 + (W_GATED + b + 1))
                    for c in range(4):
                        half, m = c // 2, c % 2
                        n = 4 * b + c
                        pe.wait_ge(bank_free, i * 8 + (B_GATED + n - 3))
                        lead, last = passes(
                            ps[:, n % 4, :], lambda k: (b, k * P), lambda k: n_hi[:, k, blk(half, HALF)],
                            lambda k: n_lo[:, k, blk(half, HALF)], (0, 1, 2), range(4 * m, 4 * m + 4), True, True)
                        if c == 0:
                            lead.then_inc(w_begun, 1)
                        last.then_inc(bank_full, 1)

            pe.wait_ge(m_lo_s, 2 * KT)
            with pe.Fori(0, KT // 2) as i:
                for b in range(2):
                    begin_tile(i * 2 + (W_OUT + b + 1))
                    for half in range(2):
                        n = 2 * b + half
                        pe.wait_ge(bank_free, i * 4 + (B_OUT + n - 3))
                        lead, last = product(ps[:, n, :], b, half, hi=m_hi, lo=m_lo)
                        if half == 0:
                            lead.then_inc(w_begun, 1)
                        last.then_inc(bank_full, 1)

            pe.wait_ge(nlo_ready, 2 * KT)
            for t in range(MH):
                begin_tile(W_QM + t + 1)
                for half in range(2):
                    n = 2 * t + half
                    pe.wait_ge(bank_free, B_QM + n - 3)
                    lead, last = product(ps[:, n % 4, :], t % 2, half)
                    if half == 0:
                        lead.then_inc(w_begun, 1)
                    last.then_inc(bank_full, 1)
                if t == 0:
                    mean(2 * KT)
            for k in range(KT):
                pe.wait_ge(msq, k // 4 + 1)
                ins = pe.matmul(ps[:, 5, 0:NM], mean_w[:], sq[:, blk(k % 4, NM)], start=(k == 0), stop=(k == KT - 1))
                if k % 4 == 3:
                    ins.then_inc(mmean, 1)
            pe.wait_ge(mg_lo_s, 1)
            for t in range(2 * MH):
                begin_tile(W_KV + t + 1)
                pe.wait_ge(bank_free, B_KV + t - 3)
                bank = ps[:, t % 4, :]
                if t < MH:
                    lead, last = passes(bank[:, 0:NM], lambda k: (t % 2, k * P), lambda k: mg_hi[:, k, :],
                                        lambda k: mg_lo[:, k, :], (0, 1, 2), range(KT), True, True)
                else:
                    for mt in range(2):
                        n = 0
                        for a, w in ((mg_hi, w_hi), (mg_lo, w_hi), (mg_hi, w_lo)):
                            for k in range(KT):
                                last = pe.matmul(bank[:, blk(mt)], a[:, k, blk(mt)], w[:, t % 2, blk(k)],
                                                 start=(n == 0), stop=(n == 3 * KT - 1))
                                if mt == 0 and n == 0:
                                    lead = last
                                n += 1
                lead.then_inc(w_begun, 1)
                last.then_inc(bank_full, 1)
            pe.wait_ge(qm_lo_s, MH)
            pe.wait_ge(bank_free, B_OM)
            pe.wait_ge(rms_ready, 2)
            MU = MH * NB
            for s in range(MU + 3):
                if s < MU:
                    hd, qb = divmod(s, NB)
                    if s >= 2:
                        pe.wait_ge(mp_exp, s - 1)
                    for n, (a, b) in enumerate(((qm_hi, km_hi), (qm_hi, km_lo), (qm_lo, km_hi))):
                        ins = pe.matmul(ps[:, 2 + s % 2, 0:NM], a[:, hd, blk(qb)], b[:, hd, :],
                                        start=(n == 0), stop=(n == 2))
                    ins.then_inc(ms_full, 1)
                u = s - 2
                if 0 <= u < MU:
                    pe.wait_ge(mp_ready, u + 1)
                    if u >= 2:
                        pe.wait_ge(mt_lo, u - 1)
                    for mt in range(2):
                        ins = pe.transpose(ps[:, 4 + u % 2, blk(mt)], p_m[:, u % 3, blk(mt)], ident[:])
                    ins.then_inc(mt_full, 1)
                u = s - 3
                if 0 <= u < MU:
                    hd, qb = divmod(u, NB)
                    pe.wait_ge(mt_lo, u + 1)
                    if u >= 2:
                        pe.wait_ge(om_lo, u - 1)
                    n = 0
                    for a, b in ((vm_hi, pm_hi), (vm_hi, pm_lo), (vm_lo, pm_hi)):
                        for mt in range(2):
                            ins = pe.matmul(ps[:, 6 + u % 2, 0:P], a[:, mt, blk(hd)], b[:, mt, :],
                                            start=(n == 0), stop=(n == 5))
                            n += 1
                    ins.then_inc(mav_full, 1)
            pe.wait_ge(om_lo, MU)
            with pe.Fori(0, KT // 4) as i:
                for b in range(2):
                    begin_tile(i * 2 + (W_OM + b + 1))
                    for c in range(4):
                        n = 4 * b + c
                        pe.wait_ge(bank_free, i * 8 + (B_OM + n - 3))
                        lead, last = passes(
                            ps[:, n % 4, :], lambda k: (b, (4 * (c // 2) + k) * P),
                            lambda k: qm_hi[:, k, blk(c % 2, HALF)], lambda k: qm_lo[:, k, blk(c % 2, HALF)],
                            (0, 1, 2), range(4), True, True)
                        if c == 0:
                            lead.then_inc(w_begun, 1)
                        last.then_inc(bank_full, 1)

            def wide(b, start, ring_at):
                for half in range(2):
                    pe.wait_ge(bank_free, start + (half - 3))
                    lead, last = product(ps[:, ring_at + half, :], b, half)
                    if half == 0:
                        lead.then_inc(w_begun, 1)
                    last.then_inc(bank_full, 1)

            def down(tile, buffer, start, ring_at):
                for n in range(KT):
                    if n % 4 == 0:
                        begin_tile(tile + (n // 4 + 1))
                    b = (n // 4 + buffer) % 2
                    for half in range(2):
                        c = 2 * n + half
                        pe.wait_ge(bank_free, start + (c - 3))
                        lead, last = passes(
                            ps[:, (c + ring_at) % 4, :],
                            lambda k: (b, k * HALF + (n % 4) * P),
                            lambda k: a_hi[:, k, blk(half, HALF)], lambda k: a_lo[:, k, blk(half, HALF)],
                            (0, 1, 2), range(2), True, True)
                        if n % 4 == 0 and half == 0:
                            lead.then_inc(w_begun, 1)
                        last.then_inc(bank_full, 1)

            pe.wait_ge(nlo_ready, 3 * KT)
            for t in range(4):
                begin_tile(W_FF + t + 1)
                wide(t % 2, B_FF + 2 * t, (2 * t) % 4)
                if t == 0:
                    mean(3 * KT)
            with pe.Fori(0, FPAIRS - 1) as i:
                tile, start = i * 6 + W_FF_LOOP, i * 24 + B_FF_LOOP
                begin_tile(tile + 1)
                wide(0, start, 0)
                pe.wait_ge(a_lo_s, i * 2 + 2)
                down(tile + 1, 1, start + 2, 2)
                for t in range(3, 6):
                    begin_tile(tile + (t + 1))
                    wide(t % 2, start + (12 + 2 * t), (12 + 2 * t) % 4)
            pe.wait_ge(a_lo_s, 2 * FPAIRS)
            down(W_END, 0, B_END, 0)
            mean(4 * KT)

        @block.scalar
        def _(act):
            steps = [0]

            def step(ins, base=0):
                steps[0] += 1
                ins.then_inc(act_step, 1)
                act.wait_ge(act_step, base + steps[0])

            for k in range(1, KT, 2):
                act.dma_start(x_f[:, k, :], xT[k]).then_inc(x_tile[k], 16)
            act.preload_act_table_set("natural_log_exp_and_others")

            def factors(number):
                if number == 1:
                    act.wait_ge(bank_free, B_MIX)
                else:
                    act.wait_ge(rms_raw, number - 1)
                step(act.activation(rms[:], rms[:], ACT.Ln))
                act.activation(rms[:], rms[:], ACT.Exp, scale=-0.5).then_inc(rms_ready, 1)

            act.wait_ge(const_in, 48)
            for k in range(KT):
                act.wait_ge(x_tile[k], 16)
                act.activation(n_hi[:, k, :], x_f[:, k, :], ACT.Copy, scale=gain[:, G_MIX + k:G_MIX + k + 1]
                               ).then_inc(nhi_ready, 1)
                if k >= 2:
                    act.wait_ge(summed, k - 1)
                act.activation(sq0[:, k % 2, :], x_f[:, k, :], ACT.Square).then_inc(squared, 1)
            factors(1)
            act.wait_ge(ang_ready, 1)
            act.activation(sin_t[:], rnd[:, 0, :], ACT.Sin).then_inc(sin_ready, 1)
            act.wait_ge(ang_ready, 2)
            act.activation(cos_t[:], rnd[:, 1, :], ACT.Sin).then_inc(sin_ready, 1)
            act.wait_ge(sin_ready, 2)
            act.dma_start(bias_A[:], bias_d).then_inc(bias_in, 16)
            act.dma_start(mask_B[:], mask_d).then_inc(bias_in, 16)
            act.preload_act_table_set("natural_log_exp_and_others")

            def round_(i):
                base = i * UNITS

                def swap_dma(n, src):
                    for head in (0, HD):
                        for to, of in ((0, 8), (8, 0)):
                            act.dma_start(swap[head + to:head + to + 8, :], raw[head + of:head + of + 8, src, :]
                                          ).then_inc(swap_in[n], 16)

                def round_hi(dst, src, number):
                    act.activation(dst[:], raw[:, src, :], ACT.Copy).then_inc(qk_hi_s, 1)

                act.wait_ge(bank_free, i * BANKS_ROUND + (B_MIX + QA + 2))
                swap_dma(0, 0)
                act.wait_ge(rope_done, i * 2 + 1)
                round_hi(qk["A"][0], 0, 1)
                act.wait_ge(bank_free, i * BANKS_ROUND + (B_MIX + KA + 2))
                swap_dma(1, 1)
                act.wait_ge(rope_done, i * 2 + 2)
                round_hi(qk["A"][2], 1, 2)
                act.wait_ge(bank_free, i * BANKS_ROUND + (B_MIX + KB + 2))
                round_hi(qk["B"][2], 0, 3)

                def v_hi(u):
                    v = v_of["A" if u < QB else "B"]
                    act.wait_ge(bank_full, B_MIX + i * BANKS_ROUND + (u + 1))
                    act.activation(v[:, blk(u % 2, 4), :, 0, :],
                                   ps[:, u % 2, :].rearrange("p (n h d) -> p n h d", n=4, h=2), ACT.Copy
                                   ).then_inc(vt_hi_s, 1)

                for s in range(SLOTS):
                    u = s - 2
                    if 0 <= u < UNITS:
                        width = (ORDER[u % 16][1] + 1) * P
                        act.wait_ge(pt_full, base + (u + 1))
                        if u:
                            act.wait_ge(av_full, base + u)
                        act.activation(pt_hi[:, 0:width], ps_t[:, 0:width], ACT.Copy).then_inc(pt_hi_s, 1)
                    u = s - 1
                    if 0 <= u < UNITS:
                        width = (ORDER[u % 16][1] + 1) * P
                        row = rows[:, u % 3, 0:width]
                        c = u % 4
                        if u < 16:
                            act.wait_ge(max_ready, i * 16 + (u + 1))
                            act.activation(row, row, ACT.Exp, scale=HD ** -0.5, bias=stat[:, 1, c:c + 1],
                                           accum_out=stat[:, 2, c:c + 1]).then_inc(exp_ready, 1)
                        else:
                            act.wait_ge(arg_ready, i * 16 + (u - 15))
                            act.activation(row, row, ACT.Exp).then_inc(pB_ready, 1)
                    u = s - 3
                    if 0 <= u < UNITS:
                        act.wait_ge(av_full, base + (u + 1))
                        if u >= 2:
                            act.wait_ge(o_sum_s, base + (u - 1))
                        act.activation(o_low[:, u % 2, :], ps[HD:P, 6 + u % 2, 0:P], ACT.Copy).then_inc(o_low_s, 1)
                    u = s
                    if 16 <= u < UNITS:
                        width = (ORDER[u % 16][1] + 1) * P
                        act.wait_ge(abs_ready, i * 16 + (u - 15))
                        act.activation(e_row[:, 0:width], e_row[:, 0:width], ACT.Exp).then_inc(act_step, 1)
                        act.wait_ge(act_step, i * 16 + (STEPS_ACT + u - 15))
                        act.activation(e_row[:, 0:width], e_row[:, 0:width], ACT.Ln, bias=1.0).then_inc(soft_ready, 1)
                    for u in finished_in(s):
                        if u in (TA, TA + 1, TB, TB + 1):
                            v_hi(u)
                        if u == QB + 1:
                            act.wait_ge(bank_free, i * BANKS_ROUND + (B_MIX + QB + 2))
                            round_hi(qk["B"][0], 1, 4)
                        if u >= GATE and u % 2 == 1:
                            m = (u - GATE) // 2
                            act.wait_ge(bank_free, i * BANKS_ROUND + (B_MIX + u + 1))
                            act.dma_start(gates_d[bass.ds(i * 4 + m, 1), :, :].rearrange("o p n -> p (o n)"),
                                          raw[:, m % 2, :]).then_inc(gate_out[m % 2], 16)
                    u = s - 4
                    if 0 <= u < UNITS:
                        store_o(i, u)

            def store_o(i, u):
                hd, qb = ORDER[u % 16]
                act.wait_ge(o_sum_s, i * UNITS + (u + 1))
                dst = o_d[bass.ds(i + 4 * (u // 16), 1), hd * HD:(hd + 1) * HD, blk(qb)].rearrange("o p n -> p (o n)")
                act.dma_start(dst, o_sum[:, u % 2, :]).then_inc(o_out[u % 2], 16)

            STEPS_ACT = steps[0]
            with act.Fori(0, PAIRS) as i:
                round_(i)
            steps[0] += PAIRS * 16

            for b in range(2):
                act.wait_ge(o_out[b], PAIRS * UNITS // 2 * 16)
                act.wait_ge(gate_out[b], PAIRS * 2 * 16)
            act.wait_ge(o_sum_s, PAIRS * UNITS)
            act.wait_ge(bank_full, B_GATED)
            act.wait_ge(bank_free, B_GATED)

            def load_o(k):
                act.dma_start(o_stage[:, k % 2, :], o_d[k]).then_inc(o_in[k % 2], 16)

            def load_gates(j, b):
                for g, at in ((g_a, 0), (g_b, KT)):
                    act.dma_start(g[:, b, :], gates_d[bass.ds(j + at, 1), :, :].rearrange("o p n -> p (o n)")
                                  ).then_inc(g_in[b], 16)

            load_o(0)
            load_o(1)
            load_gates(0, 0)
            load_gates(1, 1)
            for k in range(KT):
                act.wait_ge(o_in[k % 2], 16 * (k // 2 + 1))
                act.activation(n_hi[:, k, :], o_stage[:, k % 2, :], ACT.Copy).then_inc(o_hi_s, 1)
                if 1 <= k < KT - 1:
                    act.wait_ge(o_lo_s, k)
                    load_o(k + 1)
            act.preload_act_table(ACT.Sigmoid)

            def gated(i, more):
                for b in range(2):
                    act.wait_ge(g_in[b], i * 32 + 32)
                    for g in (g_a, g_b):
                        act.activation(g[:, b, :], g[:, b, :], ACT.Sigmoid).then_inc(g_ready, 1)
                    for half in range(2):
                        act.wait_ge(y_ready, i * 4 + (2 * b + half + 1))
                        apart(act)
                        act.activation(m_hi[:, bass.ds(i * 2 + b, 1), blk(half, HALF)].rearrange("p o n -> p (o n)"),
                                       y_a[:, half, :], ACT.Copy).then_inc(m_hi_s, 1)
                    if more:
                        load_gates(i * 2 + (b + 2), b)

            with act.Fori(0, KT // 2 - 1) as i:
                gated(i, True)
            gated(KT // 2 - 1, False)

            act.wait_ge(y_ready, 2 * KT)
            act.wait_ge(m_lo_s, 2 * KT)
            for k in range(KT):
                act.dma_start(h[:, k, :], xT[k]).then_inc(h_in, 16)
            act.dma_start(mem_f[:], memT).then_inc(mem_in, 16)
            act.preload_act_table_set("natural_log_exp_and_others")

            def next_operand(j, number, g, banks):
                act.wait_ge(bank_free, banks)
                hj = h[:, j, :] if isinstance(j, int) else h[:, bass.ds(j, 1), :].rearrange("p o n -> p (o n)")
                nj = n_hi[:, j, :] if isinstance(j, int) else n_hi[:, bass.ds(j, 1), :].rearrange("p o n -> p (o n)")
                gj = gain[:, g + j:g + j + 1] if isinstance(j, int) else gain[:, bass.ds(j + g, 1)]
                apart(act)
                act.activation(nj, hj, ACT.Copy, scale=gj).then_inc(nhi_ready, 1)
                act.wait_ge(summed, number + KT)
                apart(act)
                act.activation(sq[:], hj, ACT.Square).then_inc(squared, 1)

            with act.Fori(0, KT // 2) as i:
                for b in range(2):
                    next_operand(i * 2 + b, i * 2 + b, G_MEMQ, i * 4 + (B_OUT + 2 * b + 2))

            factors(2)
            def q_round(t):
                act.wait_ge(bank_free, B_QM + 2 * t + 2)
                act.activation(qm_hi[:, t, :], q_t[:], ACT.Copy).then_inc(qm_hi_s, 1)

            q_round(0)
            act.wait_ge(mem_in, 16)
            act.wait_ge(summed, 2 * KT)
            for c in range(2):
                if c:
                    act.wait_ge(mmean, c)
                act.activation(sq[:].rearrange("p (k n) -> p k n", k=4), mem_f[:, blk(c, 4), :], ACT.Square).then_inc(msq, 1)
            for t in range(1, MH):
                q_round(t)
            act.wait_ge(mrms_raw, 1)
            step(act.activation(mem_r[:], mem_r[:], ACT.Ln))
            act.activation(mem_r[:], mem_r[:], ACT.Exp, scale=-0.5).then_inc(mrms, 1)
            act.wait_ge(mg_f, 1)
            act.activation(mg_hi[:], mem_f[:], ACT.Copy).then_inc(mg_hi_s, 1)
            for t in range(2 * MH):
                act.wait_ge(bank_full, B_KV + t + 1)
                if t < MH:
                    act.activation(km_hi[:, t, :], ps[:, t % 4, 0:NM], ACT.Copy).then_inc(kv_hi_s, 1)
                else:
                    act.activation(vm_hi[:, :, blk(t - MH)], ps[:, t % 4, 0:NM].rearrange("p (m n) -> p m n", m=2),
                                   ACT.Copy).then_inc(kv_hi_s, 1)
            MU = MH * NB
            for s in range(MU + 4):
                u = s - 2
                if 0 <= u < MU:
                    act.wait_ge(mt_full, u + 1)
                    act.wait_ge(mav_full, u)
                    act.activation(pm_hi[:], ps[:, 4 + u % 2, 0:NM].rearrange("p (m n) -> p m n", m=2), ACT.Copy
                                   ).then_inc(mt_hi, 1)
                u = s - 3
                if 0 <= u < MU:
                    hd, qb = divmod(u, NB)
                    act.wait_ge(mav_full, u + 1)
                    act.activation(qm_hi[:, hd, blk(qb)], ps[:, 6 + u % 2, 0:P], ACT.Copy).then_inc(om_hi, 1)
                if s < MU:
                    c = s % 4
                    act.wait_ge(mx_ready, s + 1)
                    act.activation(p_m[:, s % 3, :], ps[:, 2 + s % 2, 0:NM], ACT.Exp, scale=P ** -0.5,
                                   bias=stat[:, 1, c:c + 1], accum_out=stat[:, 2, c:c + 1]).then_inc(mp_exp, 1)
            with act.Fori(0, KT // 4) as i:
                for b in range(4):
                    next_operand(i * 4 + b, i * 4 + (b + KT), G_FFN, i * 8 + (B_OM + 2 * b + 2))

            factors(3)
            act.preload_act_table(ACT.Silu)

            def hidden(f, gate_out_of_psum, number):
                act.wait_ge(bank_free, gate_out_of_psum)
                act.activation(g_f[:, f, :], g_f[:, f, :], ACT.Silu).then_inc(silu_ready, 1)
                act.wait_ge(hidden_ready, number)
                act.activation(a_hi[:, f, :], u_f[:, f, :], ACT.Copy).then_inc(a_hi_s, 1)

            for f in range(2):
                hidden(f, B_FF + 4 * f + 2, f + 1)
            with act.Fori(0, FPAIRS - 1) as i:
                for f in range(2):
                    hidden(f, i * 24 + (B_FF_LOOP + (2, 22)[f]), i * 2 + (f + 3))
            for j in range(KT):
                act.wait_ge(bank_free, B_END + 2 * j + 2)
                act.wait_ge(summed, 3 * KT + j)
                act.activation(sq[:], h[:, j, :], ACT.Square).then_inc(squared, 1)
            factors(4)
            for k in range(KT):
                act.wait_ge(out_ready, k + 1)
                act.dma_start(outT[k], h[:, k, :]).then_inc(out_done, 16)
            act.wait_ge(out_done, 16 * KT)

        @block.vector
        def _(dve):
            steps = [0]

            def step(ins, base=0):
                steps[0] += 1
                ins.then_inc(dve_step, 1)
                dve.wait_ge(dve_step, base + steps[0])

            def flat(ap):
                return ap.rearrange("p o n -> p (o n)")

            def raw_factors(number):
                dve.wait_ge(mean_full, 2 * number - 2)
                dve.tensor_scalar(rms[:], flat(ps[:, 6:8, :]), EPS, None, ALU.add).then_inc(rms_raw, 1)

            dve.memset(mean_w[:], 1.0 / D)
            step(dve.memset(rms[:], 0.0))
            dve.wait_ge(const_in, 48)
            for k in range(KT):
                dve.wait_ge(nhi_ready, k + 1)
                dve.scalar_tensor_tensor(n_lo[:, k, :], x_f[:, k, :], gain[:, G_MIX + k:G_MIX + k + 1],
                                         n_hi[:, k, :].bitcast(F32), ALU.mult, ALU.subtract).then_inc(nlo_ready, 1)
                dve.wait_ge(squared, k + 1)
                if k:
                    dve.wait_ge(summed, k)
                dve.tensor_tensor(rms[:], rms[:], sq0[:, k % 2, :], ALU.add).then_inc(summed, 1)
            dve.wait_ge(bank_full, 2)
            for half in range(2):
                dve.tensor_scalar(rms[:, blk(half, HALF)], ps[:, half, :], EPS, None, ALU.add).then_inc(bank_free, 1)
            dve.wait_ge(pos_in, 16)
            step(dve.tensor_copy(ang[:], pos_i[:]))
            step(dve.tensor_scalar(ang[:], ang[:], rope_c[:, 0:1], None, ALU.mult))
            big = 12582912.0
            step(dve.tensor_scalar(rnd[:, 0, :], ang[:], 0.15915494309189535, big, ALU.mult, ALU.add))
            step(dve.tensor_scalar(rnd[:, 0, :], rnd[:, 0, :], -big, None, ALU.add))
            for part in (6.28125, 0.0019350051879882812, 3.0199159819390456e-07):
                step(dve.scalar_tensor_tensor(ang[:], rnd[:, 0, :], -part, ang[:], ALU.mult, ALU.add))
            pi = 3.1415925
            step(dve.tensor_scalar(ang[:], ang[:], pi, -pi, ALU.min, ALU.max))
            step(dve.scalar_tensor_tensor(rnd[:, 1, :], ang[:], -1.0, ang[:], ALU.mult, ALU.max))
            dve.tensor_scalar(rnd[:, 0, :], ang[:], rope_c[:, 1:2], None, ALU.mult).then_inc(ang_ready, 1)
            dve.tensor_scalar(rnd[:, 1, :], rnd[:, 1, :], -1.0, pi / 2, ALU.mult, ALU.add).then_inc(ang_ready, 1)
            dve.wait_ge(sin_ready, 2)
            step(dve.memset(swap[:], 0.0))
            dve.wait_ge(bias_in, 32)
            dve.wait_ge(rms_ready, 1)

            LINKS = 4 + 16 + 16 + 14 + 16

            def round_(i):
                base = i * UNITS
                bank = B_MIX + i * BANKS_ROUND
                local = [0]

                def link(ins):
                    local[0] += 1
                    ins.then_inc(dve_step, 1)
                    dve.wait_ge(dve_step, i * LINKS + (steps[0] + local[0]))

                def read_out(u, to):
                    dve.wait_ge(bank_full, bank + (u + 1))
                    half = u % 2
                    dve.tensor_tensor(raw[:, to, blk(half, HALF)], ps[:, half, :], rms[:, blk(half, HALF)],
                                      ALU.mult).then_inc(bank_free, 1)
                    if half:
                        dve.wait_ge(bank_free, bank + (u + 1))

                def lo_part(dst, hi, src, number):
                    dve.wait_ge(qk_hi_s, i * 4 + number)
                    dve.tensor_tensor(dst[:], raw[:, src, :], hi[:].bitcast(F32), ALU.subtract).then_inc(qk_lo_s, 1)

                def rope(n, src):
                    dve.wait_ge(swap_in[n], i * 64 + 64)
                    link(dve.tensor_tensor(swap[:], swap[:], sin_t[:], ALU.mult))
                    link(dve.tensor_tensor(raw[:, src, :], raw[:, src, :], cos_t[:], ALU.mult))
                    dve.tensor_tensor(raw[:, src, :], raw[:, src, :], swap[:], ALU.add).then_inc(rope_done, 1)

                def v_lo(u):
                    v = v_of["A" if u < QB else "B"]
                    dve.wait_ge(vt_hi_s, i * 4 + ((0 if u < QB else 2) + u % 2 + 1))
                    dve.tensor_tensor(v[:, blk(u % 2, 4), :, 1, :],
                                      ps[:, u % 2, :].rearrange("p (n h d) -> p n h d", n=4, h=2),
                                      v[:, blk(u % 2, 4), :, 0, :].bitcast(F32), ALU.subtract).then_inc(bank_free, 1)

                read_out(QA, 0)
                read_out(QA + 1, 0)
                read_out(KA, 1)
                rope(0, 0)
                read_out(KA + 1, 1)
                lo_part(qk["A"][1], qk["A"][0], 0, 1)
                read_out(VA, 2)
                rope(1, 1)
                read_out(VA + 1, 2)
                lo_part(qk["A"][3], qk["A"][2], 1, 2)
                read_out(KB, 0)
                read_out(KB + 1, 0)
                lo_part(qk["B"][3], qk["B"][2], 0, 3)

                for s in range(SLOTS):
                    u = s - 1
                    if 16 <= u < UNITS:
                        width = (ORDER[u % 16][1] + 1) * P
                        c_row, e = r_row[:, 0:width], e_row[:, 0:width]
                        dve.wait_ge(soft_ready, i * 16 + (u - 15))
                        link(dve.tensor_tensor_scan(c_row[:, ::-1], c_row[:, ::-1], e[:, ::-1], 0.0, ALU.add, ALU.add))
                        row = rows[:, u % 3, 0:width]
                        dve.tensor_tensor(row, row, c_row, ALU.subtract).then_inc(arg_ready, 1)
                    u = s - 2
                    if 0 <= u < UNITS:
                        width = (ORDER[u % 16][1] + 1) * P
                        dve.wait_ge(pt_hi_s, base + (u + 1))
                        dve.tensor_tensor(pt_lo[:, 0:width], ps_t[:, 0:width], pt_hi[:, 0:width].bitcast(F32),
                                          ALU.subtract).then_inc(pt_lo_s, 1)
                    u = s - 1
                    if 0 <= u < 16:
                        width = (ORDER[u % 16][1] + 1) * P
                        c = u % 4
                        dve.wait_ge(exp_ready, i * 16 + (u + 1))
                        link(dve.reciprocal(stat[:, 3, c:c + 1], stat[:, 2, c:c + 1]))
                        row = rows[:, u % 3, 0:width]
                        dve.tensor_scalar(row, row, stat[:, 3, c:c + 1], None, ALU.mult).then_inc(pA_ready, 1)
                    u = s
                    if u < UNITS:
                        width = (ORDER[u % 16][1] + 1) * P
                        row = rows[:, u % 3, 0:width]
                        c = u % 4
                        dve.wait_ge(logits_full, base + (u + 1))
                        if u < 16:
                            apart(dve)
                            dve.tensor_tensor_reduce(
                                out=row, in0=ps_rows[:, 0:width], in1=bias_A[:, T - width:T], scale=1.0,
                                scalar=NEG_MAX, op0=ALU.add, op1=ALU.max, accum_out=stat[:, 0, c:c + 1]
                            ).then_inc(logits_free, 1)
                            dve.wait_ge(logits_free, base + (u + 1))
                            dve.tensor_scalar(stat[:, 1, c:c + 1], stat[:, 0, c:c + 1], -HD ** -0.5, None, ALU.mult
                                              ).then_inc(max_ready, 1)
                        else:
                            if width > P:
                                link(dve.tensor_scalar(row[:, 0:width - P], ps_rows[:, 0:width - P], HD ** -0.5, None,
                                                       ALU.mult))
                            dve.scalar_tensor_tensor(row[:, width - P:width], ps_rows[:, width - P:width], HD ** -0.5,
                                                     mask_B[:], ALU.mult, ALU.add).then_inc(logits_free, 1)
                            dve.wait_ge(logits_free, base + (u + 1))
                            if u > 16:
                                dve.wait_ge(arg_ready, i * 16 + (u - 16))
                            dve.scalar_tensor_tensor(e_row[:, 0:width], row, -1.0, row, ALU.mult, ALU.min
                                                     ).then_inc(abs_ready, 1)
                            link(dve.tensor_scalar(r_row[:, 0:width], row, 0.0, None, ALU.max))
                    u = s - 3
                    if 0 <= u < UNITS:
                        dve.wait_ge(o_low_s, base + (u + 1))
                        if u >= 2:
                            dve.wait_ge(o_out[u % 2], i * (UNITS // 2 * 16) + (u // 2) * 16)
                        dve.tensor_tensor(o_sum[:, u % 2, :], ps[0:HD, 6 + u % 2, 0:P], o_low[:, u % 2, :],
                                          ALU.add).then_inc(o_sum_s, 1)
                    for u in finished_in(s):
                        if u in (TA, TA + 1, TB, TB + 1):
                            v_lo(u)
                        elif u < VB:
                            read_out(u, 1)
                            if u % 2:
                                lo_part(qk["B"][1], qk["B"][0], 1, 4)
                        elif u < TB:
                            read_out(u, 2)
                        else:
                            m = (u - GATE) // 2
                            if u % 2 == 0 and m >= 2:
                                dve.wait_ge(gate_out[m % 2], i * 32 + 16)
                            read_out(u, m % 2)
                assert local[0] == LINKS
                for b in range(2):
                    dve.wait_ge(gate_out[b], i * 32 + 32)
                    dve.wait_ge(o_out[b], i * (UNITS // 2 * 16) + UNITS // 2 * 16)

            with dve.Fori(0, PAIRS) as i:
                round_(i)
            steps[0] += PAIRS * LINKS

            for k in range(KT):
                dve.wait_ge(o_hi_s, k + 1)
                dve.tensor_tensor(n_lo[:, k, :], o_stage[:, k % 2, :], n_hi[:, k, :].bitcast(F32), ALU.subtract
                                  ).then_inc(o_lo_s, 1)

            def column(t, j):
                return t[:, j, :] if isinstance(j, int) else flat(t[:, bass.ds(j, 1), :])

            GATED_LINKS = 4
            with dve.Fori(0, KT // 2) as i:
                for b in range(2):
                    j = i * 2 + b
                    for half in range(2):
                        n = 4 * b + 2 * half
                        ya, yb = y_a[:, half, :], y_b[:, half, :]
                        count = i * 4 + (2 * b + half + 1)
                        if half == 0:
                            dve.wait_ge(g_ready, i * 4 + (2 * b + 2))
                        dve.wait_ge(bank_full, i * 8 + (B_GATED + n + 1))
                        dve.tensor_tensor(ya, ps[:, n % 4, :], g_a[:, b, blk(half, HALF)], ALU.mult).then_inc(bank_free, 1)
                        dve.wait_ge(bank_full, i * 8 + (B_GATED + n + 2))
                        dve.tensor_tensor(yb, ps[:, (n + 1) % 4, :], g_b[:, b, blk(half, HALF)], ALU.mult).then_inc(bank_free, 1)
                        dve.wait_ge(bank_free, i * 8 + (B_GATED + n + 2))
                        dve.tensor_tensor(ya, ya, yb, ALU.add).then_inc(y_ready, 1)
                        dve.wait_ge(m_hi_s, count)
                        hi = flat(m_hi[:, bass.ds(j, 1), blk(half, HALF)])
                        lo = flat(m_lo[:, bass.ds(j, 1), blk(half, HALF)])
                        dve.tensor_tensor(lo, ya, hi.bitcast(F32), ALU.subtract).then_inc(m_lo_s, 1)

            def add_product(j, bank, start):
                for half in range(2):
                    dve.wait_ge(bank_full, start + (half + 1))
                    hj = (h[:, j, blk(half, HALF)] if isinstance(j, int)
                          else flat(h[:, bass.ds(j, 1), blk(half, HALF)]))
                    dve.tensor_tensor(hj, ps[:, bank + half, :], hj, ALU.add).then_inc(bank_free, 1)

            def next_operand(j, number, g, start):
                dve.wait_ge(bank_free, start + 2)
                dve.wait_ge(nhi_ready, number + (KT + 1))
                gj = gain[:, bass.ds(j + g, 1)]
                dve.scalar_tensor_tensor(column(n_lo, j), column(h, j), gj, column(n_hi, j).bitcast(F32),
                                         ALU.mult, ALU.subtract).then_inc(nlo_ready, 1)
                dve.wait_ge(squared, number + (KT + 1))
                dve.wait_ge(summed, number + KT)
                dve.tensor_tensor(rms[:], rms[:], sq[:], ALU.add).then_inc(summed, 1)

            dve.wait_ge(h_in, 16 * KT)
            step(dve.memset(rms[:], 0.0))
            with dve.Fori(0, KT // 2) as i:
                for b in range(2):
                    start = i * 4 + (B_OUT + 2 * b)
                    add_product(i * 2 + b, 2 * b, start)
                    next_operand(i * 2 + b, i * 2 + b, G_MEMQ, start)

            raw_factors(2)
            dve.wait_ge(rms_ready, 2)
            for t in range(MH):
                if t:
                    dve.wait_ge(qm_lo_s, t)
                for half in range(2):
                    n = 2 * t + half
                    dve.wait_ge(bank_full, B_QM + n + 1)
                    dve.tensor_tensor(q_t[:, blk(half, HALF)], ps[:, n % 4, :], rms[:, blk(half, HALF)], ALU.mult
                                      ).then_inc(bank_free, 1)
                dve.wait_ge(bank_free, B_QM + 2 * t + 2)
                dve.wait_ge(qm_hi_s, t + 1)
                dve.tensor_tensor(qm_lo[:, t, :], q_t[:], qm_hi[:, t, :].bitcast(F32), ALU.subtract).then_inc(qm_lo_s, 1)
            dve.wait_ge(mmean, 2)
            dve.tensor_scalar(mem_r[:], ps[:, 5, 0:NM], EPS, None, ALU.add).then_inc(mrms_raw, 1)
            dve.wait_ge(mrms, 1)
            for k in range(KT):
                last = dve.scalar_tensor_tensor(mem_f[:, k, :], mem_f[:, k, :], gain[:, G_MEMKV + k:G_MEMKV + k + 1],
                                                mem_r[:], ALU.mult, ALU.mult)
            last.then_inc(mg_f, 1)
            dve.wait_ge(mg_f, 1)
            dve.wait_ge(mg_hi_s, 1)
            dve.tensor_tensor(mg_lo[:], mem_f[:], mg_hi[:].bitcast(F32), ALU.subtract).then_inc(mg_lo_s, 1)
            for t in range(2 * MH):
                dve.wait_ge(kv_hi_s, t + 1)
                if t < MH:
                    dve.tensor_tensor(km_lo[:, t, :], ps[:, t % 4, 0:NM], km_hi[:, t, :].bitcast(F32), ALU.subtract
                                      ).then_inc(bank_free, 1)
                else:
                    c = blk(t - MH)
                    dve.tensor_tensor(vm_lo[:, :, c], ps[:, t % 4, 0:NM].rearrange("p (m n) -> p m n", m=2),
                                      vm_hi[:, :, c].bitcast(F32), ALU.subtract).then_inc(bank_free, 1)
            MU = MH * NB
            for s in range(MU + 4):
                u = s - 2
                if 0 <= u < MU:
                    dve.wait_ge(mt_hi, u + 1)
                    dve.tensor_tensor(pm_lo[:], ps[:, 4 + u % 2, 0:NM].rearrange("p (m n) -> p m n", m=2),
                                      pm_hi[:].bitcast(F32), ALU.subtract).then_inc(mt_lo, 1)
                u = s - 1
                if 0 <= u < MU:
                    c = u % 4
                    dve.wait_ge(mp_exp, u + 1)
                    dve.reciprocal(stat[:, 3, c:c + 1], stat[:, 2, c:c + 1]).then_inc(mr_ready, 1)
                    dve.wait_ge(mr_ready, u + 1)
                    dve.tensor_scalar(p_m[:, u % 3, :], p_m[:, u % 3, :], stat[:, 3, c:c + 1], None, ALU.mult
                                      ).then_inc(mp_ready, 1)
                if s < MU:
                    c = s % 4
                    dve.wait_ge(ms_full, s + 1)
                    step(dve.reduce_max(stat[:, 0, c:c + 1], ps[:, 2 + s % 2, 0:NM], AX_X))
                    dve.tensor_scalar(stat[:, 1, c:c + 1], stat[:, 0, c:c + 1], -P ** -0.5, None, ALU.mult
                                      ).then_inc(mx_ready, 1)
                u = s - 3
                if 0 <= u < MU:
                    hd, qb = divmod(u, NB)
                    dve.wait_ge(om_hi, u + 1)
                    dve.tensor_tensor(qm_lo[:, hd, blk(qb)], ps[:, 6 + u % 2, 0:P],
                                      qm_hi[:, hd, blk(qb)].bitcast(F32), ALU.subtract).then_inc(om_lo, 1)
            step(dve.memset(rms[:], 0.0))
            with dve.Fori(0, KT // 4) as i:
                for b in range(4):
                    start = i * 8 + (B_OM + 2 * b)
                    add_product(i * 4 + b, (2 * b) % 4, start)
                    next_operand(i * 4 + b, i * 4 + (b + KT), G_FFN, start)

            raw_factors(3)
            dve.wait_ge(rms_ready, 3)

            def half_out(dst, unit, bank):
                for half in range(2):
                    dve.wait_ge(bank_full, unit + (half + 1))
                    dve.tensor_tensor(dst[:, blk(half, HALF)], ps[:, bank + half, :], rms[:, blk(half, HALF)],
                                      ALU.mult).then_inc(bank_free, 1)

            def hidden(f, unit, bank, number):
                half_out(u_f[:, f, :], unit, bank)
                dve.wait_ge(bank_free, unit + 2)
                dve.wait_ge(silu_ready, number)
                dve.tensor_tensor(u_f[:, f, :], u_f[:, f, :], g_f[:, f, :], ALU.mult).then_inc(hidden_ready, 1)
                dve.wait_ge(a_hi_s, number)
                dve.tensor_tensor(a_lo[:, f, :], u_f[:, f, :], a_hi[:, f, :].bitcast(F32), ALU.subtract
                                  ).then_inc(a_lo_s, 1)

            for f in range(2):
                half_out(g_f[:, f, :], B_FF + 4 * f, 0)
                hidden(f, B_FF + 4 * f + 2, 2, f + 1)
            with dve.Fori(0, FPAIRS - 1) as i:
                start = i * 24 + B_FF_LOOP
                half_out(g_f[:, 0, :], start, 0)
                for n in range(KT):
                    add_product(n, (2 * n + 2) % 4, start + (2 + 2 * n))
                hidden(0, start + 18, 2, i * 2 + 3)
                half_out(g_f[:, 1, :], start + 20, 0)
                hidden(1, start + 22, 2, i * 2 + 4)

            step(dve.memset(rms[:], 0.0))
            for j in range(KT):
                add_product(j, (2 * j) % 4, B_END + 2 * j)
                dve.wait_ge(squared, 3 * KT + j + 1)
                dve.wait_ge(summed, 3 * KT + j)
                dve.tensor_tensor(rms[:], rms[:], sq[:], ALU.add).then_inc(summed, 1)
            raw_factors(4)
            dve.wait_ge(rms_ready, 4)
            for k in range(KT):
                dve.scalar_tensor_tensor(h[:, k, :], h[:, k, :], gain[:, G_FINAL + k:G_FINAL + k + 1], rms[:],
                                         ALU.mult, ALU.mult).then_inc(out_ready, 1)


def tiles(w, cols):
    k, n = w.shape
    return w.reshape(k // P, P, n // cols, cols).transpose(2, 1, 0, 3).reshape(n // cols, P, k // P * cols)


def weight_stream(np, w_in, w_up_a, w_up_b, w_out, w_q_mem, w_kv_mem, w_o_mem, w_ffn_gate, w_ffn_up, w_ffn_down):
    w = tiles(w_in, P)
    out = []
    for i in range(PAIRS):
        out += [w[4 * n + i] for n in (0, 1, 2, 4, 3, 5)]
        out += [w[24 + 4 * i + m] for m in range(4)]
    out += list(np.concatenate([tiles(w_up_a, P), tiles(w_up_b, P)], axis=2))
    out += list(tiles(w_out, P))
    out += list(tiles(w_q_mem, P))
    out += list(tiles(w_kv_mem, P))
    o = tiles(w_o_mem, P)
    out += [np.concatenate([o[2 * n], o[2 * n + 1]], axis=1) for n in range(KT // 2)]
    g, u = tiles(w_ffn_gate, P), tiles(w_ffn_up, P)

    def down(pair):
        rows = w_ffn_down[pair * 2 * P:(pair + 1) * 2 * P]
        return list(tiles(rows, HALF))

    out += [g[0], u[0], g[1], u[1]]
    for p in range(1, FPAIRS):
        out += [g[2 * p], *down(p - 1), u[2 * p], g[2 * p + 1], u[2 * p + 1]]
    out += down(FPAIRS - 1)
    return np.stack(out)


def constants(np):
    ident = np.eye(P, dtype=np.float32)
    rope = np.zeros((P, 2), np.float32)
    freq = (500000.0 ** (-np.arange(8) / 8)).astype(np.float32)
    for head in (0, HD):
        rope[head:head + 8, 0] = rope[head + 8:head + 16, 0] = freq
        rope[head:head + 8, 1], rope[head + 8:head + 16, 1] = -1.0, 1.0
    dist = (T - P + np.arange(P))[:, None] - np.arange(T)[None, :]
    count = np.zeros(dist.shape, np.int64)
    for window, dilation in ((128, 1), (512, 4), (2048, 16)):
        count += (dist >= 0) & (dist <= window) & (dist % dilation == 0)
    bias = np.where(count > 0, np.log(np.maximum(count, 1)) * HD ** 0.5, TINY).astype(np.float32)
    mask = np.where(np.arange(P)[:, None] > np.arange(P)[None, :], 0.0, TINY).astype(np.float32)
    return ident, rope, bias, mask


def kernel(**inputs):
    import numpy as np
    import concourse.bacc as bacc
    from concourse.bass_utils import run_bass_kernel_spmd as run

    a = {n: np.asarray(v) for n, v in inputs.items()}
    layer = {n: a[n][0] for n in a if n.startswith(("w_", "g_")) and n != "g_final"}
    gains = [layer["g_mix"], layer["g_mem_q"], layer["g_mem_kv"], layer["g_ffn"], a["g_final"]]
    ident, rope, bias, mask = constants(np)
    arrays = {
        "x_t": a["x"][0].T.reshape(KT, P, T),
        "mem_t": a["mem"][0].T.reshape(KT, P, NM).transpose(1, 0, 2),
        "positions": a["positions"][0],
        "gains": np.concatenate([g.reshape(KT, P).T for g in gains], axis=1),
        "weights": weight_stream(np, **{n: w for n, w in layer.items() if n.startswith("w_")}),
        "ident": ident, "rope": rope, "bias": bias, "mask": mask,
    }
    arrays = {n: np.ascontiguousarray(v) for n, v in arrays.items()}
    nc = bacc.Bacc("TRN2", target_bir_lowering=False, num_devices=1)
    args = [nc.dram_tensor(f"{n}_in", v.shape, mybir.dt.from_np(v.dtype), kind="ExternalInput").ap()
            for n, v in arrays.items()]
    out = nc.dram_tensor("out_t", (KT, P, T), F32, kind="ExternalOutput").ap()
    build(nc, *args, out)
    r = run(nc, [{f"{n}_in": v for n, v in arrays.items()}], core_ids=[0])
    return r.results[0]["out_t"].reshape(D, T).T[None]
```

```python
from contextlib import ExitStack

import concourse.bass as bass
from concourse import mybir

ALU = mybir.AluOpType
ACT = mybir.ActivationFunctionType
F32 = mybir.dt.float32
F32R = mybir.dt.float32r
I32 = mybir.dt.int32
AX_X = mybir.AxisListType.X

P = 128
T = 1024
D = 1024
KT = D // P
HALF = 512
NB = T // P
HD = 64
PAIRS = 4
NM = 256
MH = 4
FF = 2816
FPAIRS = FF // P // 2
EPS = 1e-6
EARLY_H = 5
TINY = -1.0e30
NEG_MAX = -3.0e38

TILES_IN = 10
N_TILES = PAIRS * TILES_IN + KT + KT + MH + 2 * MH + KT // 2 + 6 * FPAIRS

G_MIX, G_MEMQ, G_MEMKV, G_FFN, G_FINAL = (KT * n for n in range(5))

UNITS = 32
ORDER = ([(h, b) for b in range(NB) for h in range(2)]
         + [(h, b) for b in reversed(range(NB)) for h in range(2)])
LAG = 3
SLOTS = UNITS + 4


class Plan:

    def __init__(self, names, passes, transposes):
        self.names = names
        self.units = {n: 2 * k for k, n in enumerate(names)}
        self.tile = {n: k for k, n in enumerate(m for m in names if m[0] != "T")}
        self.fill = [[] for _ in range(SLOTS)]
        self.end = {}
        todo = [(n, half, p) for n in names for half in range(2) for p in (range(3) if n[0] != "T" else (None,))]
        t_slots = list(transposes)
        for s in range(SLOTS):
            left = passes[s]
            while todo and (left or todo[0][2] is None):
                n, half, p = todo[0]
                if p is None:
                    if t_slots[0] > s:
                        break
                    t_slots.pop(0)
                else:
                    left -= 1
                self.fill[s].append(todo.pop(0))
                if p in (2, None):
                    self.end[(n, half)] = s
        assert not todo and not t_slots
        self.after = {"dve": [[] for _ in range(SLOTS + 3)], "act": [[] for _ in range(SLOTS + 3)]}

        def then(engine, slot, *what):
            self.after[engine][slot].append(what)

        for (n, half), s in self.end.items():
            if n[0] == "T":
                then("act", s + 1, "v_hi", n, half)
                then("dve", s + 1, "v_lo", n, half)
            else:
                then("dve", s + 1, "read", n, half)
        for n in names:
            s = self.end[(n, 1)]
            if n in ("KB", "QB"):
                then("act", s + 2, "hi", n)
                then("dve", s + 3, "lo", n)
            elif n in ("QA", "KA"):
                then("act", s + 2, "swap", n)
                then("dve", s + 3, "rope", n)
                then("act", s + 4, "hi", n)
                then("dve", s + 5, "lo", n)
            elif n[0] == "G":
                then("act", min(s + 2, SLOTS), "store", n)


ROUND = Plan(("KB", "QB", "VB", "G0", "TB", "VA", "G1", "TA", "QA", "KA", "G2", "G3"),
             [2] * 10 + [1] * 4 + [0] + [1] * 4 + [2] * 4 + [0] + [2] * 12, (13, 15, 22, 24))
LAST = Plan(("KB", "QB", "VB", "TB", "G0", "G1", "G2", "G3"),
            [1] * 12 + [2] * 3 + [0] * 3 + [2] * 12 + [0] * 6, (16, 16))
LOAD_O = {max(LAST.end.values()) + 2 + n: [k for k in (2 * n, 2 * n + 1) if k < KT - 1] for n in range(4)}
ROUND_O = {min(LOAD_O) + 3 + k: k for k in range(4)}
RAW = {"QA": 0, "KA": 1, "VA": 2, "KB": 0, "QB": 1, "VB": 2, "G0": 0, "G1": 1, "G2": 0, "G3": 1}
SPLIT_NUMBER = {"KB": 3, "QB": 4, "QA": 5, "KA": 6, "TB": 3, "TA": 5}
HEAD_UNITS = 8
HEAD_TILES = 3


def blk(n, size=P):
    return slice(n * size, (n + 1) * size)


def build(nc, xT, memT, positions, gains, weights, ident_d, rope_d, bias_d, mask_d, outT):
    with ExitStack() as ctx:
        gates_d = nc.dram_tensor("gates_scratch", [2 * KT, P, T], F32, kind="Internal").ap()
        kv_d = nc.dram_tensor("memory_kv_scratch", [4, P, T], F32, kind="Internal").ap()
        o_d = nc.dram_tensor("o_scratch", [KT, P, T], F32, kind="Internal").ap()

        def sem(name):
            return ctx.enter_context(nc.semaphore(name))

        def keep(name, shape, dt):
            return ctx.enter_context(nc.sbuf_tensor(name, shape, dt))

        stage = keep("w_stage", [P, 2, KT * P], F32)
        w_hi = keep("w_hi", [P, 2, KT * P], F32R)
        w_lo = keep("w_lo", [P, 2, KT * P], F32R)
        n_hi = keep("n_hi", [P, KT, T], F32R)
        n_lo = keep("n_lo", [P, KT, T], F32R)
        rms = keep("rms", [P, T], F32)
        ident = keep("ident", [P, P], F32)
        mean_w = keep("mean_w", [P, P], F32)
        gain = keep("gain", [P, 5 * KT], F32)
        eps_col = keep("eps_col", [P, 1], F32)
        rope_c = keep("rope_c", [P, 2], F32)
        stat = keep("stat", [P, 4, 4], F32)

        def phase(*tensors):
            with ExitStack() as p:
                return [p.enter_context(nc.sbuf_tensor(n, s, d)) for n, s, d in tensors]

        (x_f, sq0, pos_i, ang, rnd, mem_f, mem_r, mg_hi, mg_lo) = phase(
            ("x_f", [P, KT, T], F32), ("sq0", [P, 2, T], F32), ("pos_i", [P, T], I32), ("ang", [P, T], F32),
            ("rnd", [P, 2, T], F32), ("mem_f", [P, KT, NM], F32), ("mem_r", [P, NM], F32),
            ("mg_hi", [P, KT, NM], F32R), ("mg_lo", [P, KT, NM], F32R))
        (_, vm_out, _, km_out) = phase(
            ("pad_x", [P, KT // 2, T], F32), ("vm_out", [P, 2, 2, MH * P], F32R),
            ("pad_k", [P, KT, T], F32), ("km_out", [P, 2, MH, NM], F32R))
        (sin_t, cos_t, qkA_q_hi, qkA_q_lo, qkA_k_hi, qkA_k_lo, qkB_q_hi, qkB_q_lo, qkB_k_hi,
         qkB_k_lo, vA, vB, pt, rows, e_row, r_row, raw, swap, bias_A, mask_B,
         o_low, o_sum) = phase(
            ("sin_m", [P, T], F32), ("cos_m", [P, T], F32),
            *[(f"qk{n}", [P, T], F32R) for n in range(8)],
            ("vA", [P, NB, 2, 2, HD], F32R), ("vB", [P, NB, 2, 2, HD], F32R),
            ("pt", [P, NB, 2, P], F32R),
            ("rows", [P, 4, T], F32), ("e_row", [P, 2, T], F32), ("r_row", [P, T], F32),
            ("raw", [P, 3, T], F32), ("swap", [P, T], F32),
            ("bias_A", [P, T], F32), ("mask_B", [P, P], F32),
            ("o_low", [HD, 2, P], F32), ("o_sum", [HD, 2, P], F32))
        qk = {"A": (qkA_q_hi, qkA_q_lo, qkA_k_hi, qkA_k_lo), "B": (qkB_q_hi, qkB_q_lo, qkB_k_hi, qkB_k_lo)}
        v_of = {"A": vA, "B": vB}
        (m_hi, m_lo, _, g_a, g_b, y_a, y_b) = phase(
            ("m_hi", [P, KT, T], F32R), ("m_lo", [P, KT, T], F32R), ("pad_g", [P, EARLY_H, T], F32),
            ("g_a", [P, 2, T], F32), ("g_b", [P, 2, T], F32),
            ("y_a", [P, 4, HALF], F32), ("y_b", [P, 2, HALF], F32))
        (_, h, sq, q_t) = phase(
            ("pad_m", [P, 2 * KT, T], F32), ("h", [P, KT, T], F32), ("sq", [P, T], F32), ("q_t", [P, T], F32))
        (qm_hi, qm_lo, km, vm, p_m, pm_hi, pm_lo) = phase(
            ("qm_hi", [P, MH, T], F32R), ("qm_lo", [P, MH, T], F32R),
            ("km", [P, 2, MH, NM], F32R), ("vm", [P, 2, 2, MH * P], F32R),
            ("p_m", [P, 3, 2, NM], F32), ("pm_hi", [P, 2, 2 * P], F32R), ("pm_lo", [P, 2, 2 * P], F32R))
        (a_hi, a_lo, g_f, u_f) = phase(
            ("a_hi", [P, 2, T], F32R), ("a_lo", [P, 2, T], F32R),
            ("g_f", [P, 2, T], F32), ("u_f", [P, 2, T], F32))

        ps = ctx.enter_context(nc.psum_tensor("ps", [P, 8, HALF], F32))
        ps_rows = ps[:, 2:4, :].rearrange("p b n -> p (b n)")
        ps_t = ps[:, 4:6, :].rearrange("p b n -> p (b n)")

        const_in, bias_in, pos_in = sem("const_in"), sem("bias_in"), sem("pos_in")
        tile_in = [sem(f"tile{k}_in") for k in range(KT)]
        w_in_s = [sem("w_stage0_in"), sem("w_stage1_in")]
        w_rounded, w_split, w_begun = sem("w_rounded"), sem("w_split"), sem("w_begun")
        bank_full, bank_free = sem("bank_full"), sem("bank_free")
        act_step, dve_step = sem("act_step"), sem("dve_step")
        squared, summed, mean_full, rms_raw, rms_ready = (
            sem("squared"), sem("summed"), sem("mean_full"), sem("rms_raw"), sem("rms_ready"))
        nhi_ready, nlo_ready = sem("nhi_ready"), sem("nlo_ready")
        ang_ready, sin_ready = sem("ang_ready"), sem("sin_ready")
        swap_in, rope_done = [sem("swap_q"), sem("swap_k")], sem("rope_done")
        qk_hi_s, qk_lo_s, vt_hi_s = sem("qk_hi"), sem("qk_lo"), sem("vt_hi")
        gate_out = [sem("gate_out0"), sem("gate_out1")]
        logits_full, logits_free = sem("logits_full"), sem("logits_free")
        max_ready, exp_ready, pA_ready, pB_ready = sem("max_ready"), sem("exp_ready"), sem("pA_ready"), sem("pB_ready")
        abs_ready, soft_ready, arg_ready = sem("abs_ready"), sem("soft_ready"), sem("arg_ready")
        pt_full, pt_hi_s, pt_lo_s, av_full = sem("pt_full"), sem("pt_hi_s"), sem("pt_lo_s"), sem("av_full")
        o_low_s, o_sum_s, o_out = sem("o_low_s"), sem("o_sum_s"), [sem("o_out0"), sem("o_out1")]
        o_hi_s, o_lo_s = sem("o_hi_s"), sem("o_lo_s")
        g_in, g_ready = [sem("g_in0"), sem("g_in1")], sem("g_ready")
        y_ready, m_hi_s, m_lo_s = sem("y_ready"), sem("m_hi_s"), sem("m_lo_s")
        mem_in, kv_out, kv_in = sem("mem_in"), sem("kv_out"), sem("kv_in")
        qm_hi_s, qm_lo_s = sem("qm_hi_s"), sem("qm_lo_s")
        msq, mmean, mrms_raw, mrms, mg_f, mg_hi_s, mg_lo_s = (
            sem("msq"), sem("mmean"), sem("mrms_raw"), sem("mrms"), sem("mg_f"), sem("mg_hi_s"), sem("mg_lo_s"))
        kv_full, kv_hi_s, kv_lo_s = sem("kv_full"), sem("kv_hi_s"), sem("kv_lo_s")
        ms_full, mx_ready, mp_exp, mr_ready, mp_ready = (
            sem("ms_full"), sem("mx_ready"), sem("mp_exp"), sem("mr_ready"), sem("mp_ready"))
        mt_full, mt_hi, mt_lo, mav_full, om_hi, om_lo = (
            sem("mt_full"), sem("mt_hi"), sem("mt_lo"), sem("mav_full"), sem("om_hi"), sem("om_lo"))
        silu_ready, hidden_ready, a_hi_s, a_lo_s = sem("silu_ready"), sem("hidden_ready"), sem("a_hi_s"), sem("a_lo_s")
        out_ready, out_done = sem("out_ready"), sem("out_done")

        B_MIX = 2
        B_ROUND = B_MIX + HEAD_UNITS
        BANKS_ROUND = 2 * len(ROUND.names)
        B_GATED = B_ROUND + (PAIRS - 1) * BANKS_ROUND + 2 * len(LAST.names)
        B_OUT = B_GATED + 4 * KT
        B_QM = B_OUT + 2 * KT
        B_OM = B_QM + 2 * MH
        B_FF = B_OM + 2 * KT
        B_FF_LOOP = B_FF + 8
        B_END = B_FF_LOOP + 24 * (FPAIRS - 1)
        W_MIX = 2 * MH
        W_GATED = W_MIX + PAIRS * TILES_IN
        W_OUT = W_GATED + KT
        W_QM = W_OUT + KT
        W_OM = W_QM + MH
        W_FF = W_OM + KT // 2
        W_FF_LOOP = W_FF + 4
        W_END = W_FF_LOOP + 6 * (FPAIRS - 1)
        assert W_END + 2 == N_TILES
        NORM_AT = KT + 5

        def apart(eng):
            eng.nop(nofuse=True)

        HU = NB // 2
        MU = MH * HU
        Q_PASSES = {HU * (t - 1) + slot: [(t, n // 3, n % 3) for n in ns]
                    for t in range(1, MH) for slot, ns in enumerate(((0, 1, 2), (3, 4), (5,)))}

        block = ctx.enter_context(nc.Block())

        @block.sync
        def _(sp):
            sp.dma_start(gain[:], gains).then_inc(const_in, 16)
            sp.dma_start(rope_c[:], rope_d).then_inc(const_in, 16)
            sp.dma_start(pos_i[:], positions.partition_broadcast(P)).then_inc(pos_in, 16)
            sp.dma_start(stage[:, 0, :], weights[0]).then_inc(w_in_s[0], 16)
            for k in range(0, KT, 2):
                sp.dma_start(x_f[:, k, :], xT[k]).then_inc(tile_in[k], 16)
                if k == 0:
                    sp.dma_start(stage[:, 1, :], weights[1]).then_inc(w_in_s[1], 16)
            sp.dma_start(ident[:], ident_d).then_inc(const_in, 16)
            with sp.Fori(1, N_TILES // 2) as i:
                for b in range(2):
                    sp.wait_ge(w_split, i * 2 + (b - 1))
                    src = weights[bass.ds(i * 2 + b, 1), :, :].rearrange("o p n -> p (o n)")
                    sp.dma_start(stage[:, b, :], src).then_inc(w_in_s[b], 16)

        @block.gpsimd
        def _(pool):
            def split(b, loaded, tile_free, number):
                pool.wait_ge(w_in_s[b], loaded)
                if tile_free is not None:
                    pool.wait_ge(w_begun, tile_free)
                apart(pool)
                pool.tensor_scalar(w_hi[:, b, :], stage[:, b, :], 1.0, 1.0, ALU.mult, ALU.mult).then_inc(w_rounded, 1)
                pool.wait_ge(w_rounded, number)
                pool.tensor_tensor(w_lo[:, b, :], stage[:, b, :], w_hi[:, b, :].bitcast(F32),
                                   ALU.subtract).then_inc(w_split, 1)

            for b in range(2):
                split(b, 16, None, b + 1)
            with pool.Fori(1, N_TILES // 2) as i:
                for b in range(2):
                    split(b, i * 16 + 16, i * 2 + b, i * 2 + (b + 1))
            for c in range(2 * KT):
                part = rms[:, blk(c // KT, HALF)]
                pool.wait_ge(squared, 3 * KT + c + 1)
                pool.wait_ge(summed, 3 * KT + c + 1)
                pool.tensor_tensor(part, part, sq[:, blk(c % 2, HALF)], ALU.add).then_inc(summed, 1)

        @block.tensor
        def _(pe):
            def passes(bank, units, mv_hi, mv_lo, which, ks, first, last):
                n = 0
                total = len(which) * len(ks)
                for p in which:
                    w = w_lo if p == 2 else w_hi
                    mv = mv_lo if p == 1 else mv_hi
                    for k in ks:
                        b, c = units(k)
                        ins = pe.matmul(bank, w[:, b, c:c + P], mv(k), start=(first and n == 0),
                                        stop=(last and n == total - 1))
                        if n == 0:
                            lead = ins
                        n += 1
                return lead, ins

            def begin_tile(number):
                pe.wait_ge(w_split, number)

            def product(bank, b, half, which=(0, 1, 2), hi=None, lo=None):
                hi, lo = hi or n_hi, lo or n_lo
                return passes(bank, lambda k: (b, k * P), lambda k: hi[:, k, blk(half, HALF)],
                              lambda k: lo[:, k, blk(half, HALF)], which, range(KT), which[0] == 0, which[-1] == 2)

            def mean(number, halves=range(2)):
                pe.wait_ge(summed, number)
                for half in halves:
                    pe.matmul(ps[:, 6 + half, :], mean_w[:], rms[:, blk(half, HALF)], start=True,
                              stop=True).then_inc(mean_full, 1)

            pe.wait_ge(msq, 1)
            pe.wait_ge(summed, 1)
            mem_sq = sq0[:].rearrange("p b n -> p (b n)")
            for k in range(KT):
                ins = pe.matmul(ps[:, 7, 0:NM], mean_w[:], mem_sq[:, blk(k, NM)], start=(k == 0), stop=(k == KT - 1))
            ins.then_inc(mmean, 1)
            pe.wait_ge(mg_lo_s, 1)
            for t in range(2 * MH):
                begin_tile(t + 1)
                if t >= 6:
                    pe.wait_ge(kv_lo_s, t - 5)
                bank = ps[:, 2 + t % 6, :]
                if t < MH:
                    lead, last = passes(bank[:, 0:NM], lambda k: (t % 2, k * P), lambda k: mg_hi[:, k, :],
                                        lambda k: mg_lo[:, k, :], (0, 1, 2), range(KT), True, True)
                else:
                    for mt in range(2):
                        n = 0
                        for a, w in ((mg_hi, w_hi), (mg_lo, w_hi), (mg_hi, w_lo)):
                            for k in range(KT):
                                last = pe.matmul(bank[:, blk(mt)], a[:, k, blk(mt)], w[:, t % 2, blk(k)],
                                                 start=(n == 0), stop=(n == 3 * KT - 1))
                                if mt == 0 and n == 0:
                                    lead = last
                                n += 1
                lead.then_inc(w_begun, 1)
                last.then_inc(kv_full, 1)

            pe.wait_ge(const_in, 48)
            pe.wait_ge(summed, KT + 1)
            for half in range(2):
                pe.matmul(ps[:, half, :], mean_w[:], rms[:, blk(half, HALF)], start=True, stop=True
                          ).then_inc(bank_full, 1)
            pe.wait_ge(nlo_ready, KT)
            pe.wait_ge(kv_lo_s, 2 * MH)

            def unit_pass(tile_number, buffer, half, p, banks_read):
                if p == 0:
                    if half == 0:
                        begin_tile(tile_number)
                    pe.wait_ge(bank_free, banks_read)
                lead, last = product(ps[:, half, :], buffer, half, (p,))
                if p == 0 and half == 0:
                    lead.then_inc(w_begun, 1)
                if p == 2:
                    last.then_inc(bank_full, 1)

            def v_transposes(first_bank, unit, half, v_read):
                pe.wait_ge(bank_free, first_bank + (unit - 1))
                pe.wait_ge(bank_free, v_read)
                for n in range(4):
                    ins = pe.transpose(ps[:, half, blk(n)], raw[:, 2, blk(half * 4 + n)], ident[:])
                ins.then_inc(bank_full, 1)

            def round_(i, plan):
                base = i * UNITS
                bank = i * BANKS_ROUND + B_ROUND

                def logits(u):
                    m = "AB"[u // 16]
                    hd, qb = ORDER[u]
                    q_hi, q_lo, k_hi, k_lo = qk[m]
                    if u == 0:
                        pe.wait_ge(qk_lo_s, i * 4 + 2)
                    if u == 16:
                        pe.wait_ge(qk_lo_s, i * 4 + 4)
                    if u:
                        pe.wait_ge(logits_free, base + u)
                    hs = slice(hd * HD, (hd + 1) * HD)
                    width = (qb + 1) * P
                    for c in range(0, width, HALF):
                        w = min(HALF, width - c)
                        for n, (a, b) in enumerate(((q_hi, k_hi), (q_hi, k_lo), (q_lo, k_hi))):
                            ins = pe.matmul(ps[:, 2 + c // HALF, 0:w], a[hs, blk(qb)], b[hs, c:c + w],
                                            start=(n == 0), stop=(n == 2))
                    ins.then_inc(logits_full, 1)

                def transposes(u):
                    if u < 16:
                        pe.wait_ge(pA_ready, i * 16 + (u + 1))
                    else:
                        pe.wait_ge(pB_ready, i * 16 + (u - 15))
                    if u:
                        pe.wait_ge(pt_lo_s, base + u)
                    for kb in range(ORDER[u][1] + 1):
                        ins = pe.transpose(ps_t[:, blk(kb)], rows[:, u % 4, blk(kb)], ident[:])
                    ins.then_inc(pt_full, 1)

                def attend(u):
                    hd, qb = ORDER[u]
                    v = v_of["AB"[u // 16]]
                    if u == 0:
                        pe.wait_ge(bank_free, bank)
                    if u == 16:
                        pe.wait_ge(bank_free, bank + (plan.units["TB"] + 2))
                    pe.wait_ge(pt_lo_s, base + (u + 1))
                    if u >= 2:
                        pe.wait_ge(o_sum_s, base + (u - 1))
                    for kb in range(qb + 1):
                        ins = pe.matmul(ps[:, 6 + u % 2, 0:2 * P], v[:, kb, hd, :, :].rearrange("p a d -> p (a d)"),
                                        pt[:, kb, :, :].rearrange("p a q -> p (a q)"), start=(kb == 0), stop=(kb == qb))
                    ins.then_inc(av_full, 1)

                for s in range(SLOTS):
                    if s < UNITS:
                        logits(s)
                    if 0 <= s - LAG - 1 < UNITS:
                        attend(s - LAG - 1)
                    if 0 <= s - LAG < UNITS:
                        transposes(s - LAG)
                    for name, half, p in plan.fill[s]:
                        unit = plan.units[name] + half
                        if p is None:
                            v_transposes(bank, unit, half, bank + (plan.units["V" + name[1]] + 2))
                        else:
                            tile = W_MIX + HEAD_TILES + plan.tile[name]
                            unit_pass(i * TILES_IN + (tile + 1), tile % 2, half, p, bank + (unit - 1))

            for tile in range(3):
                for half in range(2):
                    for p in range(3):
                        unit_pass(W_MIX + tile + 1, tile % 2, half, p, B_MIX + max(0, 2 * tile + half - 1))
            for half in range(2):
                v_transposes(B_MIX, 6 + half, half, B_MIX + 6)
            with pe.Fori(0, PAIRS - 1) as i:
                round_(i, ROUND)
            round_(PAIRS - 1, LAST)

            pe.wait_ge(o_lo_s, KT // 2)
            pe.wait_ge(bank_free, B_GATED)
            with pe.Fori(0, KT // 2) as i:
                for b in range(2):
                    begin_tile(i * 2 + (W_GATED + b + 1))
                    for c in range(4):
                        m, half = c // 2, c % 2
                        n = 4 * b + c
                        if c == 2:
                            pe.wait_ge(o_lo_s, KT)
                        pe.wait_ge(bank_free, i * 8 + (B_GATED + n - 3))
                        lead, last = passes(
                            ps[:, n % 4, :], lambda k: (b, k * P), lambda k: n_hi[:, k, blk(half, HALF)],
                            lambda k: n_lo[:, k, blk(half, HALF)], (0, 1, 2), range(4 * m, 4 * m + 4), True, True)
                        if c == 0:
                            lead.then_inc(w_begun, 1)
                        last.then_inc(bank_full, 1)

            pe.wait_ge(m_lo_s, 2 * KT)
            with pe.Fori(0, KT // 2) as i:
                for b in range(2):
                    begin_tile(i * 2 + (W_OUT + b + 1))
                    for half in range(2):
                        n = 2 * b + half
                        pe.wait_ge(bank_free, i * 4 + (B_OUT + n - 3))
                        lead, last = product(ps[:, n, :], b, half, hi=m_hi, lo=m_lo)
                        if half == 0:
                            lead.then_inc(w_begun, 1)
                        last.then_inc(bank_full, 1)

            pe.wait_ge(nlo_ready, 2 * KT)

            def q_pass(t, half, p):
                if p == 0:
                    if half == 0:
                        begin_tile(W_QM + t + 1)
                    pe.wait_ge(bank_free, B_QM + 2 * t + half - (1 if t else 3))
                lead, last = product(ps[:, half, :], t % 2, half, (p,))
                if p == 0 and half == 0:
                    lead.then_inc(w_begun, 1)
                if p == 2:
                    last.then_inc(bank_full, 1)

            for n in range(6):
                q_pass(0, n // 3, n % 3)
                if n == 2:
                    mean(2 * KT + 1)
            pe.wait_ge(bank_free, B_QM)
            pe.wait_ge(kv_in, 64)
            for s in range(MU + 3):
                if s < MU:
                    hd, qp = divmod(s, HU)
                    if qp == 0:
                        pe.wait_ge(qm_lo_s, hd + 1)
                    if s >= 2:
                        pe.wait_ge(mp_exp, s - 1)
                    for j in range(2):
                        for n, (a, b) in enumerate(((qm_hi, 0), (qm_hi, 1), (qm_lo, 0))):
                            ins = pe.matmul(ps[:, 2 + s % 2, blk(j, NM)], a[:, hd, blk(2 * qp + j)], km[:, b, hd, :],
                                            start=(n == 0), stop=(n == 2))
                    ins.then_inc(ms_full, 1)
                u = s - 3
                if 0 <= u < MU:
                    hd = u // HU
                    pe.wait_ge(mt_lo, u + 1)
                    if u == 0:
                        pe.wait_ge(rms_ready, 2)
                    if u >= 2:
                        pe.wait_ge(om_lo, u - 1)
                    n = 0
                    for a, b in ((0, pm_hi), (0, pm_lo), (1, pm_hi)):
                        for mt in range(2):
                            ins = pe.matmul(ps[:, 6 + u % 2, 0:2 * P], vm[:, a, mt, blk(hd)], b[:, mt, :],
                                            start=(n == 0), stop=(n == 5))
                            n += 1
                    ins.then_inc(mav_full, 1)
                u = s - 2
                if 0 <= u < MU:
                    pe.wait_ge(mp_ready, u + 1)
                    if u >= 2:
                        pe.wait_ge(mt_lo, u - 1)
                    for j in range(2):
                        for mt in range(2):
                            ins = pe.transpose(ps[:, 4 + u % 2, blk(2 * mt + j)], p_m[:, u % 3, j, blk(mt)], ident[:])
                    ins.then_inc(mt_full, 1)
                for t, half, p in Q_PASSES.get(s, ()):
                    q_pass(t, half, p)
            pe.wait_ge(bank_free, B_OM)
            pe.wait_ge(om_lo, MU)
            with pe.Fori(0, KT // 4) as i:
                for b in range(2):
                    begin_tile(i * 2 + (W_OM + b + 1))
                    for c in range(4):
                        n = 4 * b + c
                        pe.wait_ge(bank_free, i * 8 + (B_OM + n - 3))
                        lead, last = passes(
                            ps[:, n % 4, :], lambda k: (b, (4 * (c // 2) + k) * P),
                            lambda k: qm_hi[:, k, blk(c % 2, HALF)], lambda k: qm_lo[:, k, blk(c % 2, HALF)],
                            (0, 1, 2), range(4), True, True)
                        if c == 0:
                            lead.then_inc(w_begun, 1)
                        last.then_inc(bank_full, 1)

            def wide(b, start, ring_at):
                for half in range(2):
                    pe.wait_ge(bank_free, start + (half - 3))
                    lead, last = product(ps[:, ring_at + half, :], b, half)
                    if half == 0:
                        lead.then_inc(w_begun, 1)
                    last.then_inc(bank_full, 1)

            def down(tile, buffer, start, ring_at):
                for n in range(KT):
                    if n % 4 == 0:
                        begin_tile(tile + (n // 4 + 1))
                    b = (n // 4 + buffer) % 2
                    for half in range(2):
                        c = 2 * n + half
                        pe.wait_ge(bank_free, start + (c - 3))
                        lead, last = passes(
                            ps[:, (c + ring_at) % 4, :],
                            lambda k: (b, k * HALF + (n % 4) * P),
                            lambda k: a_hi[:, k, blk(half, HALF)], lambda k: a_lo[:, k, blk(half, HALF)],
                            (0, 1, 2), range(2), True, True)
                        if n % 4 == 0 and half == 0:
                            lead.then_inc(w_begun, 1)
                        last.then_inc(bank_full, 1)

            pe.wait_ge(nlo_ready, 3 * KT)
            for t in range(4):
                begin_tile(W_FF + t + 1)
                wide(t % 2, B_FF + 2 * t, (2 * t) % 4)
                if t == 0:
                    mean(3 * KT + 1)
            with pe.Fori(0, FPAIRS - 1) as i:
                tile, start = i * 6 + W_FF_LOOP, i * 24 + B_FF_LOOP
                begin_tile(tile + 1)
                wide(0, start, 0)
                pe.wait_ge(a_lo_s, i * 2 + 2)
                down(tile + 1, 1, start + 2, 2)
                for t in range(3, 6):
                    begin_tile(tile + (t + 1))
                    wide(t % 2, start + (12 + 2 * t), (12 + 2 * t) % 4)
            pe.wait_ge(a_lo_s, 2 * FPAIRS)
            begin_tile(W_END + 1)
            for c in range(2 * KT):
                if c == 4:
                    begin_tile(W_END + 2)
                half, n = divmod(c, KT)
                pe.wait_ge(bank_free, B_END + c - 3)
                lead, last = passes(
                    ps[:, c % 4, :], lambda k: (n // 4, k * HALF + (n % 4) * P),
                    lambda k: a_hi[:, k, blk(half, HALF)], lambda k: a_lo[:, k, blk(half, HALF)],
                    (0, 1, 2), range(2), True, True)
                if c in (0, 4):
                    lead.then_inc(w_begun, 1)
                last.then_inc(bank_full, 1)
                if c == KT + 3:
                    mean(4 * KT + 1, (0,))
            mean(5 * KT + 1, (1,))

        @block.scalar
        def _(act):
            steps = [0]

            def step(ins, base=0):
                steps[0] += 1
                ins.then_inc(act_step, 1)
                act.wait_ge(act_step, base + steps[0])

            act.dma_start(mem_f[:], memT).then_inc(mem_in, 16)
            for k in range(1, KT, 2):
                act.dma_start(x_f[:, k, :], xT[k]).then_inc(tile_in[k], 16)
            act.preload_act_table_set("natural_log_exp_and_others")

            def factors(number):
                if number == 1:
                    act.wait_ge(bank_free, B_MIX)
                else:
                    act.wait_ge(rms_raw, number - 1)
                step(act.activation(rms[:], rms[:], ACT.Ln))
                act.activation(rms[:], rms[:], ACT.Exp, scale=-0.5).then_inc(rms_ready, 1)

            def kv_hi(t):
                act.wait_ge(kv_full, t + 1)
                if t < MH:
                    act.activation(km_out[:, 0, t, :], ps[:, 2 + t % 6, 0:NM], ACT.Copy).then_inc(kv_hi_s, 1)
                else:
                    act.activation(vm_out[:, 0, :, blk(t - MH)],
                                   ps[:, 2 + t % 6, 0:NM].rearrange("p (m n) -> p m n", m=2), ACT.Copy
                                   ).then_inc(kv_hi_s, 1)

            act.wait_ge(mem_in, 16)
            act.activation(sq0[:].rearrange("p b n -> p (b n)"), mem_f[:].rearrange("p k n -> p (k n)"), ACT.Square
                           ).then_inc(msq, 1)
            act.wait_ge(const_in, 32)
            for k in range(KT):
                act.wait_ge(tile_in[k], 16)
                act.activation(n_hi[:, k, :], x_f[:, k, :], ACT.Copy, scale=gain[:, G_MIX + k:G_MIX + k + 1]
                               ).then_inc(nhi_ready, 1)
                if k == 0:
                    act.wait_ge(mrms_raw, 1)
                    step(act.activation(mem_r[:], mem_r[:], ACT.Ln))
                    act.activation(mem_r[:], mem_r[:], ACT.Exp, scale=-0.5).then_inc(mrms, 1)
                    act.wait_ge(mmean, 1)
                if k >= 2:
                    act.wait_ge(summed, k)
                act.activation(sq0[:, k % 2, :], x_f[:, k, :], ACT.Square).then_inc(squared, 1)
                if k == 0:
                    act.wait_ge(mg_f, 1)
                    act.activation(mg_hi[:], mem_f[:], ACT.Copy).then_inc(mg_hi_s, 1)
                if k >= KT - 2:
                    kv_hi(k - (KT - 2))
            act.wait_ge(nlo_ready, KT)
            for t in range(2, 2 * MH):
                kv_hi(t)
            factors(1)
            act.wait_ge(ang_ready, 1)
            act.activation(sin_t[:], rnd[:, 0, :], ACT.Sin).then_inc(sin_ready, 1)
            act.wait_ge(ang_ready, 2)
            act.activation(cos_t[:], rnd[:, 1, :], ACT.Sin).then_inc(sin_ready, 1)
            act.wait_ge(sin_ready, 2)
            act.wait_ge(kv_lo_s, 2 * MH)
            for a in range(2):
                act.dma_start(kv_d[a], km_out[:, a, :, :].rearrange("p h n -> p (h n)").bitcast(F32)).then_inc(kv_out, 16)
                act.dma_start(kv_d[2 + a], vm_out[:, a, :, :].rearrange("p m n -> p (m n)").bitcast(F32)).then_inc(kv_out, 16)
            act.wait_ge(kv_out, 64)
            act.dma_start(bias_A[:], bias_d).then_inc(bias_in, 16)
            act.dma_start(mask_B[:], mask_d).then_inc(bias_in, 16)
            act.preload_act_table_set("natural_log_exp_and_others")

            def swap_dma(n, src):
                for head in (0, HD):
                    for to, of in ((0, 8), (8, 0)):
                        act.dma_start(swap[head + to:head + to + 8, :], raw[head + of:head + of + 8, src, :]
                                      ).then_inc(swap_in[n], 16)

            def round_hi(name):
                m, which = name[1], name[0]
                act.activation(qk[m][0 if which == "Q" else 2][:], raw[:, RAW[name], :], ACT.Copy).then_inc(qk_hi_s, 1)

            def v_hi(m, half, bank_filled):
                act.wait_ge(bank_full, bank_filled)
                act.activation(v_of[m][:, blk(half, 4), :, 0, :],
                               ps[:, half, :].rearrange("p (n h d) -> p n h d", n=4, h=2), ACT.Copy
                               ).then_inc(vt_hi_s, 1)

            for n, name in enumerate(("QA", "KA")):
                act.wait_ge(bank_free, B_MIX + 2 * n + 2)
                swap_dma(n, n)
                act.wait_ge(rope_done, n + 1)
                round_hi(name)
            for half in range(2):
                v_hi("A", half, B_MIX + 6 + half + 1)

            def round_(i, plan):
                base = i * UNITS
                bank = i * BANKS_ROUND + B_ROUND
                for s in range(SLOTS + 2):
                    u = s
                    if 16 <= u < UNITS:
                        width = (ORDER[u][1] + 1) * P
                        act.wait_ge(logits_full, base + (u + 1))
                        act.activation(rows[:, u % 4, 0:width], ps_rows[:, 0:width], ACT.Copy, scale=HD ** -0.5
                                       ).then_inc(logits_free, 1)
                    u = s - LAG - 2
                    if 0 <= u < UNITS:
                        act.wait_ge(av_full, base + (u + 1))
                        if u >= 2:
                            act.wait_ge(o_sum_s, base + (u - 1))
                        act.activation(o_low[:, u % 2, :], ps[HD:P, 6 + u % 2, 0:P], ACT.Copy).then_inc(o_low_s, 1)
                    u = s - LAG
                    if 0 <= u < UNITS:
                        width = (ORDER[u][1] + 1) * P
                        act.wait_ge(pt_full, base + (u + 1))
                        act.activation(pt[:, 0:width // P, 0, :], ps_t[:, 0:width].rearrange("p (n q) -> p n q", q=P),
                                       ACT.Copy).then_inc(pt_hi_s, 1)
                    u = s - 2
                    if 16 <= u < UNITS:
                        row = rows[:, u % 4, 0:(ORDER[u][1] + 1) * P]
                        act.wait_ge(arg_ready, i * 16 + (u - 15))
                        act.activation(row, row, ACT.Exp).then_inc(pB_ready, 1)
                    u = s
                    if u < UNITS:
                        width = (ORDER[u][1] + 1) * P
                        if u < 16:
                            row = rows[:, u % 4, 0:width]
                            c = u % 4
                            act.wait_ge(max_ready, i * 16 + (u + 1))
                            act.activation(row, row, ACT.Exp, scale=HD ** -0.5, bias=stat[:, 1, c:c + 1],
                                           accum_out=stat[:, 2, c:c + 1]).then_inc(exp_ready, 1)
                        else:
                            e = e_row[:, u % 2, 0:width]
                            act.wait_ge(abs_ready, i * 16 + (u - 15))
                            act.activation(e, e, ACT.Exp).then_inc(act_step, 1)
                            act.wait_ge(act_step, i * 16 + (STEPS_ACT + u - 15))
                            act.activation(e, e, ACT.Ln, bias=1.0).then_inc(soft_ready, 1)
                    for what, name, *rest in plan.after["act"][s]:
                        unit = plan.units[name]
                        if what == "v_hi":
                            v_hi(name[1], rest[0], bank + (unit + rest[0] + 1))
                        elif what == "swap":
                            act.wait_ge(bank_free, bank + (unit + 2))
                            swap_dma(RAW[name], RAW[name])
                        elif what == "hi":
                            if name[1] == "A":
                                act.wait_ge(rope_done, i * 2 + (3 + RAW[name]))
                            else:
                                act.wait_ge(bank_free, bank + (unit + 2))
                            round_hi(name)
                        elif what == "store":
                            m = int(name[1])
                            act.wait_ge(bank_free, bank + (unit + 2))
                            act.dma_start(gates_d[bass.ds(i * 4 + m, 1), :, :].rearrange("o p n -> p (o n)"),
                                          raw[:, RAW[name], :]).then_inc(gate_out[m % 2], 16)
                    u = s - LAG - 3
                    if 0 <= u < UNITS:
                        store_o(i, u)
                    if plan is LAST and s in LOAD_O:
                        act.wait_ge(bank_full, B_GATED)
                        for b in range(2):
                            act.wait_ge(o_out[b], 16 + 16 * (UNITS // 2 * i + UNITS // 4))
                        for k in LOAD_O[s]:
                            act.dma_start(n_lo[:, k, :].bitcast(F32), o_d[k]).then_inc(tile_in[k], 16)
                    if plan is LAST and s in ROUND_O:
                        round_o(ROUND_O[s])

            def round_o(k):
                act.wait_ge(tile_in[k], 32)
                act.activation(n_hi[:, k, :], n_lo[:, k, :].bitcast(F32), ACT.Copy).then_inc(o_hi_s, 1)

            def store_o(i, u):
                hd, qb = ORDER[u]
                act.wait_ge(o_sum_s, i * UNITS + (u + 1))
                dst = o_d[bass.ds(i + 4 * (u // 16), 1), hd * HD:(hd + 1) * HD, blk(qb)].rearrange("o p n -> p (o n)")
                act.dma_start(dst, o_sum[:, u % 2, :]).then_inc(o_out[u % 2], 16)

            STEPS_ACT = steps[0]
            with act.Fori(0, PAIRS - 1) as i:
                round_(i, ROUND)
            round_(PAIRS - 1, LAST)
            steps[0] += PAIRS * 16

            def load_gates(j, b):
                for g, at in ((g_a, 0), (g_b, KT)):
                    act.dma_start(g[:, b, :], gates_d[bass.ds(j + at, 1), :, :].rearrange("o p n -> p (o n)")
                                  ).then_inc(g_in[b], 16)

            for b in range(2):
                act.wait_ge(o_out[b], PAIRS * UNITS // 2 * 16 + 16)
                act.wait_ge(gate_out[b], PAIRS * 2 * 16 + 16)
            act.dma_start(n_lo[:, KT - 1, :].bitcast(F32), o_d[KT - 1]).then_inc(tile_in[KT - 1], 16)
            load_gates(0, 0)
            load_gates(1, 1)
            for k in range(len(ROUND_O), KT):
                round_o(k)
            for k in range(EARLY_H):
                act.dma_start(h[:, k, :], xT[k]).then_inc(tile_in[k], 16)
            act.preload_act_table(ACT.Sigmoid)

            def gated(i, more):
                for b in range(2):
                    act.wait_ge(g_in[b], i * 32 + 32)
                    for g in (g_a, g_b):
                        act.activation(g[:, b, :], g[:, b, :], ACT.Sigmoid).then_inc(g_ready, 1)
                    for half in range(2):
                        act.wait_ge(y_ready, i * 4 + (2 * b + half + 1))
                        apart(act)
                        act.activation(m_hi[:, bass.ds(i * 2 + b, 1), blk(half, HALF)].rearrange("p o n -> p (o n)"),
                                       y_a[:, 2 * b + half, :], ACT.Copy).then_inc(m_hi_s, 1)
                    if more:
                        load_gates(i * 2 + (b + 2), b)

            with act.Fori(0, KT // 2 - 1) as i:
                gated(i, True)
            gated(KT // 2 - 1, False)

            act.wait_ge(y_ready, 2 * KT)
            act.wait_ge(m_lo_s, 2 * KT)
            for k in range(EARLY_H, KT):
                act.dma_start(h[:, k, :], xT[k]).then_inc(tile_in[k], 16)
            act.preload_act_table_set("natural_log_exp_and_others")

            def next_operand(j, number, g, banks):
                act.wait_ge(bank_free, banks)
                hj = h[:, j, :] if isinstance(j, int) else h[:, bass.ds(j, 1), :].rearrange("p o n -> p (o n)")
                nj = n_hi[:, j, :] if isinstance(j, int) else n_hi[:, bass.ds(j, 1), :].rearrange("p o n -> p (o n)")
                gj = gain[:, g + j:g + j + 1] if isinstance(j, int) else gain[:, bass.ds(j + g, 1)]
                apart(act)
                act.activation(nj, hj, ACT.Copy, scale=gj).then_inc(nhi_ready, 1)
                act.wait_ge(summed, number + (KT + 1))
                apart(act)
                act.activation(sq[:], hj, ACT.Square).then_inc(squared, 1)

            with act.Fori(0, KT // 2) as i:
                for b in range(2):
                    next_operand(i * 2 + b, i * 2 + b, G_MEMQ, i * 4 + (B_OUT + 2 * b + 2))

            act.wait_ge(bank_full, B_QM)
            for a in range(2):
                act.dma_start(km[:, a, :, :].rearrange("p h n -> p (h n)").bitcast(F32), kv_d[a]).then_inc(kv_in, 16)
                act.dma_start(vm[:, a, :, :].rearrange("p m n -> p (m n)").bitcast(F32), kv_d[2 + a]).then_inc(kv_in, 16)
            factors(2)

            def q_round(t):
                act.wait_ge(bank_free, B_QM + 2 * t + 2)
                act.activation(qm_hi[:, t, :], q_t[:], ACT.Copy).then_inc(qm_hi_s, 1)

            q_round(0)
            for s in range(MU + 4):
                if s < MU:
                    act.wait_ge(mx_ready, s + 1)
                    for j in range(2):
                        c = 2 * (s % 2) + j
                        ins = act.activation(p_m[:, s % 3, j, :], ps[:, 2 + s % 2, blk(j, NM)], ACT.Exp,
                                             scale=P ** -0.5, bias=stat[:, 1, c:c + 1], accum_out=stat[:, 2, c:c + 1])
                    ins.then_inc(mp_exp, 1)
                u = s - 2
                if 0 <= u < MU:
                    act.wait_ge(mt_full, u + 1)
                    act.activation(pm_hi[:], ps[:, 4 + u % 2, :].rearrange("p (m n) -> p m n", m=2), ACT.Copy
                                   ).then_inc(mt_hi, 1)
                u = s - 3
                if 0 <= u < MU:
                    hd, qp = divmod(u, HU)
                    act.wait_ge(mav_full, u + 1)
                    act.activation(qm_hi[:, hd, blk(qp, 2 * P)], ps[:, 6 + u % 2, 0:2 * P], ACT.Copy).then_inc(om_hi, 1)
                if s % HU == HU - 1 and s // HU + 1 < MH:
                    q_round(s // HU + 1)
            with act.Fori(0, KT // 4) as i:
                for b in range(4):
                    next_operand(i * 4 + b, i * 4 + (b + KT), G_FFN, i * 8 + (B_OM + 2 * b + 2))

            factors(3)
            act.preload_act_table(ACT.Silu)

            def hidden(f, gate_out_of_psum, number):
                act.wait_ge(bank_free, gate_out_of_psum)
                act.activation(g_f[:, f, :], g_f[:, f, :], ACT.Silu).then_inc(silu_ready, 1)
                act.wait_ge(hidden_ready, number)
                act.activation(a_hi[:, f, :], u_f[:, f, :], ACT.Copy).then_inc(a_hi_s, 1)

            for f in range(2):
                hidden(f, B_FF + 4 * f + 2, f + 1)
            with act.Fori(0, FPAIRS - 1) as i:
                for f in range(2):
                    hidden(f, i * 24 + (B_FF_LOOP + (2, 22)[f]), i * 2 + (f + 3))
            def last_factors(half):
                act.wait_ge(rms_raw, 3 + half)
                part = rms[:, blk(half, HALF)]
                step(act.activation(part, part, ACT.Ln))
                act.activation(part, part, ACT.Exp, scale=-0.5).then_inc(rms_ready, 1)

            def store(half, k):
                act.wait_ge(out_ready, half * KT + k + 1)
                act.dma_start(outT[k][:, blk(half, HALF)], h[:, k, blk(half, HALF)]).then_inc(out_done, 16)

            for c in range(2 * KT):
                half, j = divmod(c, KT)
                act.wait_ge(bank_free, B_END + c + 1)
                if c >= 2:
                    act.wait_ge(summed, 3 * KT + c)
                act.activation(sq[:, blk(c % 2, HALF)], h[:, j, blk(half, HALF)], ACT.Square).then_inc(squared, 1)
                if c == NORM_AT:
                    last_factors(0)
            for k in range(KT):
                store(0, k)
            last_factors(1)
            for k in range(KT):
                store(1, k)
            act.wait_ge(out_done, 32 * KT)

        @block.vector
        def _(dve):
            steps = [0]

            def step(ins, base=0):
                steps[0] += 1
                ins.then_inc(dve_step, 1)
                dve.wait_ge(dve_step, base + steps[0])

            def flat(ap):
                return ap.rearrange("p o n -> p (o n)")

            def raw_factors(number):
                dve.wait_ge(mean_full, 2 * number - 2)
                dve.tensor_scalar(rms[:], flat(ps[:, 6:8, :]), EPS, None, ALU.add).then_inc(rms_raw, 1)

            dve.memset(rms[:], 0.0)
            dve.memset(mean_w[:], 1.0 / D).then_inc(summed, 1)
            dve.wait_ge(summed, 1)
            dve.wait_ge(const_in, 32)
            dve.wait_ge(pos_in, 16)
            step(dve.tensor_copy(ang[:], pos_i[:]))
            step(dve.tensor_scalar(ang[:], ang[:], rope_c[:, 0:1], None, ALU.mult))
            big = 12582912.0
            step(dve.tensor_scalar(rnd[:, 0, :], ang[:], 0.15915494309189535, big, ALU.mult, ALU.add))
            step(dve.tensor_scalar(rnd[:, 0, :], rnd[:, 0, :], -big, None, ALU.add))
            for part in (6.28125, 0.0019350051879882812, 3.0199159819390456e-07):
                step(dve.scalar_tensor_tensor(ang[:], rnd[:, 0, :], -part, ang[:], ALU.mult, ALU.add))
            pi = 3.1415925
            step(dve.tensor_scalar(ang[:], ang[:], pi, -pi, ALU.min, ALU.max))
            def kv_lo(t):
                dve.wait_ge(kv_hi_s, t + 1)
                bank = ps[:, 2 + t % 6, 0:NM]
                if t < MH:
                    dve.tensor_tensor(km_out[:, 1, t, :], bank, km_out[:, 0, t, :].bitcast(F32), ALU.subtract
                                      ).then_inc(kv_lo_s, 1)
                else:
                    c = blk(t - MH)
                    dve.tensor_tensor(vm_out[:, 1, :, c], bank.rearrange("p (m n) -> p m n", m=2),
                                      vm_out[:, 0, :, c].bitcast(F32), ALU.subtract).then_inc(kv_lo_s, 1)

            for k in range(KT):
                if k == 0:
                    dve.wait_ge(mmean, 1)
                    dve.tensor_scalar(mem_r[:], ps[:, 7, 0:NM], EPS, None, ALU.add).then_inc(mrms_raw, 1)
                dve.wait_ge(nhi_ready, k + 1)
                dve.scalar_tensor_tensor(n_lo[:, k, :], x_f[:, k, :], gain[:, G_MIX + k:G_MIX + k + 1],
                                         n_hi[:, k, :].bitcast(F32), ALU.mult, ALU.subtract).then_inc(nlo_ready, 1)
                if k == 0:
                    dve.wait_ge(mrms, 1)
                    for m in range(KT):
                        last = dve.scalar_tensor_tensor(mem_f[:, m, :], mem_f[:, m, :],
                                                        gain[:, G_MEMKV + m:G_MEMKV + m + 1], mem_r[:],
                                                        ALU.mult, ALU.mult)
                    last.then_inc(mg_f, 1)
                dve.wait_ge(squared, k + 1)
                if k:
                    dve.wait_ge(summed, k + 1)
                dve.tensor_tensor(rms[:], rms[:], sq0[:, k % 2, :], ALU.add).then_inc(summed, 1)
                if k == 0:
                    dve.wait_ge(mg_f, 1)
                    dve.wait_ge(mg_hi_s, 1)
                    dve.tensor_tensor(mg_lo[:], mem_f[:], mg_hi[:].bitcast(F32), ALU.subtract).then_inc(mg_lo_s, 1)
                if k >= KT - 2:
                    kv_lo(k - (KT - 2))
            for t in range(2, 2 * MH):
                kv_lo(t)
            dve.wait_ge(bank_full, 2)
            for half in range(2):
                dve.tensor_scalar(rms[:, blk(half, HALF)], ps[:, half, :], EPS, None, ALU.add).then_inc(bank_free, 1)
            step(dve.scalar_tensor_tensor(rnd[:, 1, :], ang[:], -1.0, ang[:], ALU.mult, ALU.max))
            dve.tensor_scalar(rnd[:, 0, :], ang[:], rope_c[:, 1:2], None, ALU.mult).then_inc(ang_ready, 1)
            dve.tensor_scalar(rnd[:, 1, :], rnd[:, 1, :], -1.0, pi / 2, ALU.mult, ALU.add).then_inc(ang_ready, 1)
            dve.wait_ge(sin_ready, 2)
            step(dve.memset(swap[:], 0.0))
            for b in range(2):
                dve.memset(o_sum[:, b, :], 0.0).then_inc(o_out[b], 16)
                dve.memset(raw[:, b, 0:1], 0.0).then_inc(gate_out[b], 16)
            for b in range(2):
                dve.wait_ge(gate_out[b], 16)
            dve.wait_ge(bias_in, 32)
            dve.wait_ge(rms_ready, 1)

            def read_out(name, half, bank_unit):
                dve.wait_ge(bank_full, bank_unit + 1)
                dve.tensor_tensor(raw[:, RAW[name], blk(half, HALF)], ps[:, half, :], rms[:, blk(half, HALF)],
                                  ALU.mult).then_inc(bank_free, 1)

            def lo_part(name, number, filled):
                dst, hi = qk[name[1]][1 if name[0] == "Q" else 3], qk[name[1]][0 if name[0] == "Q" else 2]
                dve.wait_ge(bank_free, filled)
                dve.wait_ge(qk_hi_s, number)
                dve.tensor_tensor(dst[:], raw[:, RAW[name], :], hi[:].bitcast(F32), ALU.subtract).then_inc(qk_lo_s, 1)

            def rope(src, swapped, follow):
                dve.wait_ge(swap_in[src], swapped)
                follow(dve.tensor_tensor(swap[:], swap[:], sin_t[:], ALU.mult))
                follow(dve.tensor_tensor(raw[:, src, :], raw[:, src, :], cos_t[:], ALU.mult))
                dve.tensor_tensor(raw[:, src, :], raw[:, src, :], swap[:], ALU.add).then_inc(rope_done, 1)

            def v_lo(m, half, number):
                v = v_of[m]
                dve.wait_ge(vt_hi_s, number)
                dve.tensor_tensor(v[:, blk(half, 4), :, 1, :],
                                  ps[:, half, :].rearrange("p (n h d) -> p n h d", n=4, h=2),
                                  v[:, blk(half, 4), :, 0, :].bitcast(F32), ALU.subtract).then_inc(bank_free, 1)

            read_out("QA", 0, B_MIX)
            read_out("QA", 1, B_MIX + 1)
            read_out("KA", 0, B_MIX + 2)
            rope(0, 64, step)
            read_out("KA", 1, B_MIX + 3)
            lo_part("QA", 1, B_MIX + 2)
            read_out("VA", 0, B_MIX + 4)
            rope(1, 64, step)
            read_out("VA", 1, B_MIX + 5)
            lo_part("KA", 2, B_MIX + 4)
            for half in range(2):
                v_lo("A", half, half + 1)

            def o_rest(k):
                dve.wait_ge(o_hi_s, k + 1)
                dve.tensor_tensor(n_lo[:, k, :], n_lo[:, k, :].bitcast(F32), n_hi[:, k, :].bitcast(F32),
                                  ALU.subtract).then_inc(o_lo_s, 1)

            def round_(i, plan, links):
                base = i * UNITS
                bank = i * BANKS_ROUND + B_ROUND
                local = [0]

                def link(ins):
                    local[0] += 1
                    ins.then_inc(dve_step, 1)
                    dve.wait_ge(dve_step, i * LINKS + (steps[0] + local[0]))

                for s in range(SLOTS + 2):
                    u = s
                    if u < UNITS:
                        width = (ORDER[u][1] + 1) * P
                        row = rows[:, u % 4, 0:width]
                        c = u % 4
                        if u < 16:
                            dve.wait_ge(logits_full, base + (u + 1))
                            apart(dve)
                            dve.tensor_tensor_reduce(
                                out=row, in0=ps_rows[:, 0:width], in1=bias_A[:, T - width:T], scale=1.0,
                                scalar=NEG_MAX, op0=ALU.add, op1=ALU.max, accum_out=stat[:, 0, c:c + 1]
                            ).then_inc(logits_free, 1)
                            dve.wait_ge(logits_free, base + (u + 1))
                            dve.tensor_scalar(stat[:, 1, c:c + 1], stat[:, 0, c:c + 1], -HD ** -0.5, None, ALU.mult
                                              ).then_inc(max_ready, 1)
                        else:
                            dve.wait_ge(logits_free, base + (u + 1))
                            link(dve.tensor_tensor(row[:, width - P:width], row[:, width - P:width], mask_B[:], ALU.add))
                            dve.scalar_tensor_tensor(e_row[:, u % 2, 0:width], row, -1.0, row, ALU.mult, ALU.min
                                                     ).then_inc(abs_ready, 1)
                    u = s - LAG - 2
                    if 0 <= u < UNITS:
                        dve.wait_ge(o_low_s, base + (u + 1))
                        dve.wait_ge(o_out[u % 2], i * (UNITS // 2 * 16) + (u // 2 + 1) * 16)
                        o = o_sum[:, u % 2, :]
                        link(dve.tensor_tensor(o, ps[0:HD, 6 + u % 2, 0:P], o_low[:, u % 2, :], ALU.add))
                        dve.tensor_tensor(o, o, ps[0:HD, 6 + u % 2, P:2 * P], ALU.add).then_inc(o_sum_s, 1)
                    u = s - LAG
                    if 0 <= u < UNITS:
                        width = (ORDER[u][1] + 1) * P
                        dve.wait_ge(pt_hi_s, base + (u + 1))
                        nb = width // P
                        dve.tensor_tensor(pt[:, 0:nb, 1, :], ps_t[:, 0:width].rearrange("p (n q) -> p n q", q=P),
                                          pt[:, 0:nb, 0, :].bitcast(F32), ALU.subtract).then_inc(pt_lo_s, 1)
                    u = s - 1
                    if 0 <= u < 16:
                        width = (ORDER[u][1] + 1) * P
                        c = u % 4
                        dve.wait_ge(exp_ready, i * 16 + (u + 1))
                        link(dve.reciprocal(stat[:, 3, c:c + 1], stat[:, 2, c:c + 1]))
                        row = rows[:, u % 4, 0:width]
                        dve.tensor_scalar(row, row, stat[:, 3, c:c + 1], None, ALU.mult).then_inc(pA_ready, 1)
                    if 16 <= u < UNITS:
                        width = (ORDER[u][1] + 1) * P
                        row, c_row, e = rows[:, u % 4, 0:width], r_row[:, 0:width], e_row[:, u % 2, 0:width]
                        if u > 16:
                            dve.wait_ge(arg_ready, i * 16 + (u - 16))
                        link(dve.tensor_scalar(c_row, row, 0.0, None, ALU.max))
                        dve.wait_ge(soft_ready, i * 16 + (u - 15))
                        link(dve.tensor_tensor_scan(c_row[:, ::-1], c_row[:, ::-1], e[:, ::-1], 0.0, ALU.add, ALU.add))
                        dve.tensor_tensor(row, row, c_row, ALU.subtract).then_inc(arg_ready, 1)
                    for what, name, *rest in plan.after["dve"][s]:
                        unit = plan.units[name]
                        if what == "v_lo":
                            v_lo(name[1], rest[0], i * 4 + (SPLIT_NUMBER[name] + rest[0]))
                        elif what == "rope":
                            rope(RAW[name], i * 64 + 128, link)
                        elif what == "lo":
                            lo_part(name, i * 4 + SPLIT_NUMBER[name], bank + (unit + 2))
                        elif what == "read":
                            if rest[0] == 0 and name[0] == "G" and (plan is ROUND or name in ("G0", "G1")):
                                split_of = {"G0": "KB", "G1": "QB", "G2": "QA", "G3": "KA"}[name]
                                dve.wait_ge(qk_lo_s, i * 4 + SPLIT_NUMBER[split_of])
                            if rest[0] == 0 and name in ("KB", "QB"):
                                dve.wait_ge(gate_out[RAW[name]], i * 32 + 16)
                            if rest[0] == 0 and name in (("QA", "KA") if plan is ROUND else ("G2", "G3")):
                                dve.wait_ge(gate_out[RAW[name]], i * 32 + 32)
                            read_out(name, rest[0], bank + (unit + rest[0]))
                    if plan is LAST and s - 1 in ROUND_O:
                        o_rest(ROUND_O[s - 1])
                assert local[0] == links

            LINKS = UNITS + 16 + 3 * 16 + 4
            with dve.Fori(0, PAIRS - 1) as i:
                round_(i, ROUND, LINKS)
            round_(PAIRS - 1, LAST, LINKS - 4)
            steps[0] += PAIRS * LINKS - 4

            for k in range(SLOTS + 1 - min(ROUND_O), KT):
                o_rest(k)

            def column(t, j):
                return t[:, j, :] if isinstance(j, int) else flat(t[:, bass.ds(j, 1), :])

            with dve.Fori(0, KT // 2) as i:
                for b in range(2):
                    j = i * 2 + b
                    dve.wait_ge(g_ready, i * 4 + (2 * b + 2))
                    for c in range(4):
                        m, half = c // 2, c % 2
                        n = 4 * b + c
                        ya, yb = y_a[:, 2 * b + half, :], y_b[:, half, :]
                        dve.wait_ge(bank_full, i * 8 + (B_GATED + n + 1))
                        dve.tensor_tensor((ya, yb)[m], ps[:, n % 4, :], (g_a, g_b)[m][:, b, blk(half, HALF)], ALU.mult
                                          ).then_inc(bank_free, 1)
                        if m == 0:
                            continue
                        dve.wait_ge(bank_free, i * 8 + (B_GATED + n + 1))
                        dve.tensor_tensor(ya, ya, yb, ALU.add).then_inc(y_ready, 1)
                        dve.wait_ge(m_hi_s, i * 4 + (2 * b + half + 1))
                        hi = flat(m_hi[:, bass.ds(j, 1), blk(half, HALF)])
                        lo = flat(m_lo[:, bass.ds(j, 1), blk(half, HALF)])
                        dve.tensor_tensor(lo, ya, hi.bitcast(F32), ALU.subtract).then_inc(m_lo_s, 1)

            def add_product(j, bank, start):
                for half in range(2):
                    dve.wait_ge(bank_full, start + (half + 1))
                    hj = (h[:, j, blk(half, HALF)] if isinstance(j, int)
                          else flat(h[:, bass.ds(j, 1), blk(half, HALF)]))
                    dve.tensor_tensor(hj, ps[:, bank + half, :], hj, ALU.add).then_inc(bank_free, 1)

            def next_operand(j, number, g, start):
                dve.wait_ge(bank_free, start + 2)
                dve.wait_ge(nhi_ready, number + (KT + 1))
                gj = gain[:, bass.ds(j + g, 1)]
                dve.scalar_tensor_tensor(column(n_lo, j), column(h, j), gj, column(n_hi, j).bitcast(F32),
                                         ALU.mult, ALU.subtract).then_inc(nlo_ready, 1)
                dve.wait_ge(squared, number + (KT + 1))
                dve.wait_ge(summed, number + (KT + 1))
                dve.tensor_tensor(rms[:], rms[:], sq[:], ALU.add).then_inc(summed, 1)

            def out_pair(i):
                for b in range(2):
                    start = i * 4 + (B_OUT + 2 * b)
                    add_product(i * 2 + b, 2 * b, start)
                    next_operand(i * 2 + b, i * 2 + b, G_MEMQ, start)

            step(dve.memset(rms[:], 0.0))
            for k in range(EARLY_H):
                dve.wait_ge(tile_in[k], 48)
            with dve.Fori(0, EARLY_H // 2) as i:
                out_pair(i)
            for k in range(EARLY_H, KT):
                dve.wait_ge(tile_in[k], 48)
            with dve.Fori(EARLY_H // 2, KT // 2) as i:
                out_pair(i)

            raw_factors(2)
            dve.wait_ge(rms_ready, 2)

            def q_read(t, half):
                n = 2 * t + half
                if t and half == 0:
                    dve.wait_ge(qm_lo_s, t)
                dve.wait_ge(bank_full, B_QM + n + 1)
                dve.tensor_tensor(q_t[:, blk(half, HALF)], ps[:, half, :], rms[:, blk(half, HALF)], ALU.mult
                                  ).then_inc(bank_free, 1)

            def q_split(t):
                dve.wait_ge(bank_free, B_QM + 2 * t + 2)
                dve.wait_ge(qm_hi_s, t + 1)
                dve.tensor_tensor(qm_lo[:, t, :], q_t[:], qm_hi[:, t, :].bitcast(F32), ALU.subtract).then_inc(qm_lo_s, 1)

            q_read(0, 0)
            q_read(0, 1)
            q_split(0)
            for s in range(MU + 4):
                t = s // HU + 1
                if s < MU:
                    c = slice(2 * (s % 2), 2 * (s % 2) + 2)
                    dve.wait_ge(ms_full, s + 1)
                    step(dve.reduce_max(stat[:, 0, c], ps[:, 2 + s % 2, :].rearrange("p (j n) -> p j n", j=2), AX_X))
                    dve.tensor_scalar(stat[:, 1, c], stat[:, 0, c], -P ** -0.5, None, ALU.mult).then_inc(mx_ready, 1)
                if s % HU == HU - 1 and t < MH:
                    q_read(t, 1)
                u = s - 1
                if 0 <= u < MU:
                    c = 2 * (u % 2)
                    dve.wait_ge(mp_exp, u + 1)
                    dve.reciprocal(stat[:, 3, c:c + 2], stat[:, 2, c:c + 2]).then_inc(mr_ready, 1)
                    dve.wait_ge(mr_ready, u + 1)
                    for j in range(2):
                        ins = dve.tensor_scalar(p_m[:, u % 3, j, :], p_m[:, u % 3, j, :], stat[:, 3, c + j:c + j + 1],
                                                None, ALU.mult)
                    ins.then_inc(mp_ready, 1)
                u = s - 2
                if 0 <= u < MU:
                    dve.wait_ge(mt_hi, u + 1)
                    dve.tensor_tensor(pm_lo[:], ps[:, 4 + u % 2, :].rearrange("p (m n) -> p m n", m=2),
                                      pm_hi[:].bitcast(F32), ALU.subtract).then_inc(mt_lo, 1)
                u = s - 3
                if 0 <= u < MU:
                    hd, qp = divmod(u, HU)
                    dve.wait_ge(om_hi, u + 1)
                    dve.tensor_tensor(qm_lo[:, hd, blk(qp, 2 * P)], ps[:, 6 + u % 2, 0:2 * P],
                                      qm_hi[:, hd, blk(qp, 2 * P)].bitcast(F32), ALU.subtract).then_inc(om_lo, 1)
                if t < MH and s % HU == 1:
                    q_read(t, 0)
                if t < MH and s % HU == HU - 1:
                    q_split(t)
            step(dve.memset(rms[:], 0.0))
            with dve.Fori(0, KT // 4) as i:
                for b in range(4):
                    start = i * 8 + (B_OM + 2 * b)
                    add_product(i * 4 + b, (2 * b) % 4, start)
                    next_operand(i * 4 + b, i * 4 + (b + KT), G_FFN, start)

            raw_factors(3)
            dve.wait_ge(rms_ready, 3)

            def half_out(dst, unit, bank):
                for half in range(2):
                    dve.wait_ge(bank_full, unit + (half + 1))
                    dve.tensor_tensor(dst[:, blk(half, HALF)], ps[:, bank + half, :], rms[:, blk(half, HALF)],
                                      ALU.mult).then_inc(bank_free, 1)

            def hidden(f, unit, bank, number):
                half_out(u_f[:, f, :], unit, bank)
                dve.wait_ge(bank_free, unit + 2)
                dve.wait_ge(silu_ready, number)
                dve.tensor_tensor(u_f[:, f, :], u_f[:, f, :], g_f[:, f, :], ALU.mult).then_inc(hidden_ready, 1)
                dve.wait_ge(a_hi_s, number)
                dve.tensor_tensor(a_lo[:, f, :], u_f[:, f, :], a_hi[:, f, :].bitcast(F32), ALU.subtract
                                  ).then_inc(a_lo_s, 1)

            for f in range(2):
                half_out(g_f[:, f, :], B_FF + 4 * f, 0)
                hidden(f, B_FF + 4 * f + 2, 2, f + 1)
            with dve.Fori(0, FPAIRS - 1) as i:
                start = i * 24 + B_FF_LOOP
                half_out(g_f[:, 0, :], start, 0)
                for n in range(KT):
                    add_product(n, (2 * n + 2) % 4, start + (2 + 2 * n))
                hidden(0, start + 18, 2, i * 2 + 3)
                half_out(g_f[:, 1, :], start + 20, 0)
                hidden(1, start + 22, 2, i * 2 + 4)

            step(dve.memset(rms[:], 0.0))

            def last_add(c):
                half, j = divmod(c, KT)
                dve.wait_ge(bank_full, B_END + c + 1)
                hj = h[:, j, blk(half, HALF)]
                dve.tensor_tensor(hj, ps[:, c % 4, :], hj, ALU.add).then_inc(bank_free, 1)

            def last_raw(half):
                dve.wait_ge(mean_full, 5 + half)
                dve.tensor_scalar(rms[:, blk(half, HALF)], ps[:, 6 + half, :], EPS, None, ALU.add).then_inc(rms_raw, 1)

            def last_norm(half, ks):
                dve.wait_ge(rms_ready, 4 + half)
                for k in ks:
                    hk = h[:, k, blk(half, HALF)]
                    dve.scalar_tensor_tensor(hk, hk, gain[:, G_FINAL + k:G_FINAL + k + 1], rms[:, blk(half, HALF)],
                                             ALU.mult, ALU.mult).then_inc(out_ready, 1)

            for c in range(2 * KT):
                last_add(c)
                if c == NORM_AT:
                    last_raw(0)
            last_norm(0, range(KT))
            last_raw(1)
            last_norm(1, range(KT))


def tiles(w, cols):
    k, n = w.shape
    return w.reshape(k // P, P, n // cols, cols).transpose(2, 1, 0, 3).reshape(n // cols, P, k // P * cols)


def weight_stream(np, w_in, w_up_a, w_up_b, w_out, w_q_mem, w_kv_mem, w_o_mem, w_ffn_gate, w_ffn_up, w_ffn_down):
    w = tiles(w_in, P)
    out = list(tiles(w_kv_mem, P))
    place = {"QA": 0, "KA": 4, "VA": 8, "QB": 12, "KB": 16, "VB": 20}
    out += [w[place[n]] for n in ("QA", "KA", "VA")]
    for i in range(PAIRS):
        for n in (ROUND if i < PAIRS - 1 else LAST).names:
            if n[0] == "G":
                out.append(w[24 + 4 * i + int(n[1])])
            elif n[0] != "T":
                out.append(w[place[n] + (i + 1 if n[1] == "A" else i)])
    out += list(np.concatenate([tiles(w_up_a, P), tiles(w_up_b, P)], axis=2))
    out += list(tiles(w_out, P))
    out += list(tiles(w_q_mem, P))
    o = tiles(w_o_mem, P)
    out += [np.concatenate([o[2 * n], o[2 * n + 1]], axis=1) for n in range(KT // 2)]
    g, u = tiles(w_ffn_gate, P), tiles(w_ffn_up, P)

    def down(pair):
        rows = w_ffn_down[pair * 2 * P:(pair + 1) * 2 * P]
        return list(tiles(rows, HALF))

    out += [g[0], u[0], g[1], u[1]]
    for p in range(1, FPAIRS):
        out += [g[2 * p], *down(p - 1), u[2 * p], g[2 * p + 1], u[2 * p + 1]]
    out += down(FPAIRS - 1)
    return np.stack(out)


def constants(np):
    ident = np.eye(P, dtype=np.float32)
    rope = np.zeros((P, 2), np.float32)
    freq = (500000.0 ** (-np.arange(8) / 8)).astype(np.float32)
    for head in (0, HD):
        rope[head:head + 8, 0] = rope[head + 8:head + 16, 0] = freq
        rope[head:head + 8, 1], rope[head + 8:head + 16, 1] = -1.0, 1.0
    dist = (T - P + np.arange(P))[:, None] - np.arange(T)[None, :]
    count = np.zeros(dist.shape, np.int64)
    for window, dilation in ((128, 1), (512, 4), (2048, 16)):
        count += (dist >= 0) & (dist <= window) & (dist % dilation == 0)
    bias = np.where(count > 0, np.log(np.maximum(count, 1)) * HD ** 0.5, TINY).astype(np.float32)
    mask = np.where(np.arange(P)[:, None] > np.arange(P)[None, :], 0.0, TINY).astype(np.float32)
    return ident, rope, bias, mask


def kernel(**inputs):
    import numpy as np
    import concourse.bacc as bacc
    from concourse.bass_utils import run_bass_kernel_spmd as run

    a = {n: np.asarray(v) for n, v in inputs.items()}
    layer = {n: a[n][0] for n in a if n.startswith(("w_", "g_")) and n != "g_final"}
    gains = [layer["g_mix"], layer["g_mem_q"], layer["g_mem_kv"], layer["g_ffn"], a["g_final"]]
    ident, rope, bias, mask = constants(np)
    arrays = {
        "x_t": a["x"][0].T.reshape(KT, P, T),
        "mem_t": a["mem"][0].T.reshape(KT, P, NM).transpose(1, 0, 2),
        "positions": a["positions"][0],
        "gains": np.concatenate([g.reshape(KT, P).T for g in gains], axis=1),
        "weights": weight_stream(np, **{n: w for n, w in layer.items() if n.startswith("w_")}),
        "ident": ident, "rope": rope, "bias": bias, "mask": mask,
    }
    arrays = {n: np.ascontiguousarray(v) for n, v in arrays.items()}
    nc = bacc.Bacc("TRN2", target_bir_lowering=False, num_devices=1)
    args = [nc.dram_tensor(f"{n}_in", v.shape, mybir.dt.from_np(v.dtype), kind="ExternalInput").ap()
            for n, v in arrays.items()]
    out = nc.dram_tensor("out_t", (KT, P, T), F32, kind="ExternalOutput").ap()
    build(nc, *args, out)
    r = run(nc, [{f"{n}_in": v for n, v in arrays.items()}], core_ids=[0])
    return r.results[0]["out_t"].reshape(D, T).T[None]
```

```python
from contextlib import ExitStack

import concourse.bass as bass
from concourse import mybir

ALU = mybir.AluOpType
ACT = mybir.ActivationFunctionType
F32 = mybir.dt.float32
F32R = mybir.dt.float32r
I32 = mybir.dt.int32
AX_X = mybir.AxisListType.X

P = 128
T = 1024
D = 1024
KT = D // P
HALF = 512
NB = T // P
HD = 64
PAIRS = 4
NM = 256
MH = 4
FF = 2816
FPAIRS = FF // P // 2
EPS = 1e-6
EARLY_H = 5
TINY = -1.0e30
NEG_MAX = -3.0e38

TILES_IN = 10
N_TILES = PAIRS * TILES_IN + KT + KT + MH + 2 * MH + KT // 2 + 6 * FPAIRS

G_MIX, G_MEMQ, G_MEMKV, G_FFN, G_FINAL = (KT * n for n in range(5))

UNITS = 32
ORDER = ([(h, b) for b in range(NB) for h in range(2)]
         + [(h, b) for b in reversed(range(NB)) for h in range(2)])
LAG = 3
SLOTS = UNITS + 4


class Plan:

    def __init__(self, names, passes, transposes):
        self.names = names
        self.units = {n: 2 * k for k, n in enumerate(names)}
        self.tile = {n: k for k, n in enumerate(names)}
        self.fill = [[] for _ in range(SLOTS)]
        self.end = {}
        todo = [(n, half, p) for n in names for half in range(2) for p in range(3)]
        assert len(passes) == SLOTS and sum(passes) == len(todo)
        for s in range(SLOTS):
            for _ in range(passes[s]):
                n, half, p = todo.pop(0)
                self.fill[s].append((n, half, p))
                self.end[(n, half)] = s
            for n, at in transposes.items():
                if s in (at, at + 1):
                    self.fill[s].append((n, s - at, None))
                    self.end[(n, s - at)] = s
        self.after = {"dve": [[] for _ in range(SLOTS + 3)], "act": [[] for _ in range(SLOTS + 3)]}

        def then(engine, slot, *what):
            self.after[engine][slot].append(what)

        for n in names:
            s = self.end[(n, 1)]
            if n in ("KB", "QB"):
                then("act", s + 2, "hi", n)
                then("dve", s + 3, "lo", n)
            elif n in ("QA", "KA"):
                then("act", s + 2, "swap", n)
                then("dve", s + 3, "rope", n, 0, 1)
                then("dve", s + 4, "rope", n, 2)
                then("act", s + 5, "hi", n)
                then("dve", s + 6, "lo", n)
            elif n[0] == "G":
                then("act", min(s + 2, SLOTS), "store", n)
        for (n, half), s in self.end.items():
            if n[0] == "T":
                then("act", s + 1, "v_hi", n, half)
                then("dve", s + 1, "v_lo", n, half)
            else:
                then("dve", s + 1, "read", n, half)
        for work in self.after["dve"]:
            work.sort(key=lambda w: w[0] == "rope")


ROUND = Plan(("VB", "KB", "QB", "G0", "G1", "G2", "QA", "KA", "VA", "G3"),
             [2] * 9 + [1] * 9 + [2] * 4 + [1] + [2] * 12 + [0], {"TB": 4, "TA": 34})
LAST = Plan(("VB", "KB", "QB", "G0", "G1", "G2", "G3"),
            [2] * 6 + [1] * 12 + [2] * 7 + [1] * 4 + [0] * 7, {"TB": 4})
LOAD_O = {max(LAST.end.values()) + 2 + n: [k for k in (2 * n, 2 * n + 1) if k < KT - 1] for n in range(4)}
ROUND_O = {min(LOAD_O) + 3 + k: k for k in range(4)}
RAW = {"QA": 0, "KA": 1, "VA": 2, "KB": 0, "QB": 1, "VB": 2, "G0": 0, "G1": 1, "G2": 0, "G3": 1}
SPLIT_NUMBER = {"KB": 3, "QB": 4, "QA": 5, "KA": 6, "TB": 3, "TA": 5}
HEAD_TILES = 3
HEAD_UNITS = 2 * HEAD_TILES


def blk(n, size=P):
    return slice(n * size, (n + 1) * size)


def build(nc, xT, memT, positions, gains, weights, ident_d, rope_d, bias_d, mask_d, outT):
    with ExitStack() as ctx:
        gates_d = nc.dram_tensor("gates_scratch", [2 * KT, P, T], F32, kind="Internal").ap()
        kv_d = nc.dram_tensor("memory_kv_scratch", [4, P, T], F32, kind="Internal").ap()
        o_d = nc.dram_tensor("o_scratch", [KT, P, T], F32, kind="Internal").ap()

        def sem(name):
            return ctx.enter_context(nc.semaphore(name))

        def keep(name, shape, dt):
            return ctx.enter_context(nc.sbuf_tensor(name, shape, dt))

        stage = keep("w_stage", [P, 2, KT * P], F32)
        w_hi = keep("w_hi", [P, 2, KT * P], F32R)
        w_lo = keep("w_lo", [P, 2, KT * P], F32R)
        n_hi = keep("n_hi", [P, KT, T], F32R)
        n_lo = keep("n_lo", [P, KT, T], F32R)
        rms = keep("rms", [P, T], F32)
        ident = keep("ident", [P, P], F32)
        mean_w = keep("mean_w", [P, P], F32)
        gain = keep("gain", [P, 5 * KT], F32)
        rope_c = keep("rope_c", [P, 2], F32)
        r_col = keep("r_col", [P, 2], F32)
        stat = keep("stat", [P, 4, 4], F32)

        def phase(*tensors):
            with ExitStack() as p:
                return [p.enter_context(nc.sbuf_tensor(n, s, d)) for n, s, d in tensors]

        (x_f, sq0, pos_i, ang, rnd, mem_f, mem_r, mg_hi, mg_lo, mem_sq, k_f) = phase(
            ("x_f", [P, KT, T], F32), ("sq0", [P, 2, T], F32), ("pos_i", [P, T], I32), ("ang", [P, T], F32),
            ("rnd", [P, 2, T], F32), ("mem_f", [P, KT, NM], F32), ("mem_r", [P, NM], F32),
            ("mg_hi", [P, KT, NM], F32R), ("mg_lo", [P, KT, NM], F32R), ("mem_sq", [P, KT, NM], F32),
            ("k_f", [P, NM], F32))
        (_, vm_out, _, km_out) = phase(
            ("pad_x", [P, KT // 2, T], F32), ("vm_out", [P, 2, 2, MH * P], F32R),
            ("pad_k", [P, KT, T], F32), ("km_out", [P, 2, MH, NM], F32R))
        (sin_t, cos_t, qkA_q_hi, qkA_q_lo, qkA_k_hi, qkA_k_lo, qkB_q_hi, qkB_q_lo, qkB_k_hi,
         qkB_k_lo, vA, vB, pt, rows, e_row, r_row, raw, swap, bias_A, mask_B,
         o_low, o_sum) = phase(
            ("sin_m", [P, T], F32), ("cos_m", [P, T], F32),
            *[(f"qk{n}", [P, T], F32R) for n in range(8)],
            ("vA", [P, NB, 2, 2, HD], F32R), ("vB", [P, NB, 2, 2, HD], F32R),
            ("pt", [P, NB, 2, P], F32R),
            ("rows", [P, 4, T], F32), ("e_row", [P, 2, T], F32), ("r_row", [P, T], F32),
            ("raw", [P, 3, T], F32), ("swap", [P, T], F32),
            ("bias_A", [P, T], F32), ("mask_B", [P, P], F32),
            ("o_low", [HD, 2, P], F32), ("o_sum", [P, 2, P], F32))
        qk = {"A": (qkA_q_hi, qkA_q_lo, qkA_k_hi, qkA_k_lo), "B": (qkB_q_hi, qkB_q_lo, qkB_k_hi, qkB_k_lo)}
        v_of = {"A": vA, "B": vB}

        def o_of(u):
            lower = HD * (u // 2 % 2)
            return o_sum[lower:lower + HD, u % 2, :]

        (m_hi, m_lo, _, g_a, g_b, y_a, y_b) = phase(
            ("m_hi", [P, KT, T], F32R), ("m_lo", [P, KT, T], F32R), ("pad_g", [P, EARLY_H, T], F32),
            ("g_a", [P, 2, T], F32), ("g_b", [P, 2, T], F32),
            ("y_a", [P, 4, HALF], F32), ("y_b", [P, 2, HALF], F32))
        (_, h, sq, q_t) = phase(
            ("pad_m", [P, 2 * KT, T], F32), ("h", [P, KT, T], F32), ("sq", [P, T], F32), ("q_t", [P, T], F32))
        (qm_hi, qm_lo, km, vm, p_m, pm_hi, pm_lo) = phase(
            ("qm_hi", [P, MH, T], F32R), ("qm_lo", [P, MH, T], F32R),
            ("km", [P, 2, MH, NM], F32R), ("vm", [P, 2, 2, MH * P], F32R),
            ("p_m", [P, 3, 2, NM], F32), ("pm_hi", [P, 2, 2, 2 * P], F32R), ("pm_lo", [P, 2, 2, 2 * P], F32R))
        (a_hi, a_lo, g_f, u_f) = phase(
            ("a_hi", [P, 2, T], F32R), ("a_lo", [P, 2, T], F32R),
            ("g_f", [P, 2, T], F32), ("u_f", [P, 2, T], F32))

        ps = ctx.enter_context(nc.psum_tensor("ps", [P, 8, HALF], F32))
        ps_rows = ps[:, 2:4, :].rearrange("p b n -> p (b n)")
        ps_t = ps[:, 4:6, :].rearrange("p b n -> p (b n)")

        const_in, ident_in, bias_in, pos_in = sem("const_in"), sem("ident_in"), sem("bias_in"), sem("pos_in")
        tile_in = [sem(f"tile{k}_in") for k in range(KT)]
        w_in_s = [sem("w_stage0_in"), sem("w_stage1_in")]
        w_rounded, w_split, w_begun = sem("w_rounded"), sem("w_split"), sem("w_begun")
        bank_full, bank_free = sem("bank_full"), sem("bank_free")
        act_step, dve_step = sem("act_step"), sem("dve_step")
        squared, summed, mean_full, rms_raw, rms_ready = (
            sem("squared"), sem("summed"), sem("mean_full"), sem("rms_raw"), sem("rms_ready"))
        nhi_ready, nlo_ready = sem("nhi_ready"), sem("nlo_ready")
        ang_ready, sin_ready = sem("ang_ready"), sem("sin_ready")
        swap_in, rope_done = [sem("swap_q"), sem("swap_k")], sem("rope_done")
        qk_hi_s, qk_lo_s = sem("qk_hi"), sem("qk_lo")
        vt_full, vt_hi_s, vt_lo_s = sem("vt_full"), sem("vt_hi"), sem("vt_lo")
        gate_out = [sem("gate_out0"), sem("gate_out1")]
        logits_full, logits_free = sem("logits_full"), sem("logits_free")
        max_ready, exp_ready, pA_ready, pB_ready = sem("max_ready"), sem("exp_ready"), sem("pA_ready"), sem("pB_ready")
        abs_ready, soft_ready, arg_ready = sem("abs_ready"), sem("soft_ready"), sem("arg_ready")
        pt_full, pt_hi_s, pt_lo_s, av_full = sem("pt_full"), sem("pt_hi_s"), sem("pt_lo_s"), sem("av_full")
        o_low_s, o_sum_s, o_out = sem("o_low_s"), sem("o_sum_s"), [sem(f"o_out{n}") for n in range(4)]
        o_hi_s, o_lo_s = sem("o_hi_s"), sem("o_lo_s")
        g_in, g_ready = [sem("g_in0"), sem("g_in1")], sem("g_ready")
        y_ready, m_hi_s, m_lo_s = sem("y_ready"), sem("m_hi_s"), sem("m_lo_s")
        mem_in, kv_out, kv_in = sem("mem_in"), sem("kv_out"), sem("kv_in")
        qm_hi_s, qm_lo_s = sem("qm_hi_s"), sem("qm_lo_s")
        msq, mmean, mrms_raw, mrms, mg_hi_s, mg_lo_s = (
            sem("msq"), sem("mmean"), sem("mrms_raw"), sem("mrms"), sem("mg_hi_s"), sem("mg_lo_s"))
        r_col_full, r_col_ready, k_f_ready = sem("r_col_full"), sem("r_col_ready"), sem("k_f_ready")
        kv_full, kv_hi_s, kv_lo_s = sem("kv_full"), sem("kv_hi_s"), sem("kv_lo_s")
        ms_full, mx_ready, mp_exp, mr_ready, mp_ready = (
            sem("ms_full"), sem("mx_ready"), sem("mp_exp"), sem("mr_ready"), sem("mp_ready"))
        mt_full, mt_hi, mt_lo, mav_full, om_hi, om_lo = (
            sem("mt_full"), sem("mt_hi"), sem("mt_lo"), sem("mav_full"), sem("om_hi"), sem("om_lo"))
        silu_ready, hidden_ready, a_hi_s, a_lo_s = sem("silu_ready"), sem("hidden_ready"), sem("a_hi_s"), sem("a_lo_s")
        out_ready, out_done = sem("out_ready"), sem("out_done")

        B_MIX = 2
        B_ROUND = B_MIX + HEAD_UNITS
        BANKS_ROUND = 2 * len(ROUND.names)
        B_GATED = B_ROUND + (PAIRS - 1) * BANKS_ROUND + 2 * len(LAST.names)
        B_OUT = B_GATED + 4 * KT
        B_QM = B_OUT + 2 * KT
        B_OM = B_QM + 2 * MH
        B_FF = B_OM + 2 * KT
        B_FF_LOOP = B_FF + 8
        B_END = B_FF_LOOP + 24 * (FPAIRS - 1)
        W_MIX = 2 * MH
        W_GATED = W_MIX + PAIRS * TILES_IN
        W_OUT = W_GATED + KT
        W_QM = W_OUT + KT
        W_OM = W_QM + MH
        W_FF = W_OM + KT // 2
        W_FF_LOOP = W_FF + 4
        W_END = W_FF_LOOP + 6 * (FPAIRS - 1)
        assert W_END + 2 == N_TILES
        NORM_AT = KT + 5

        def apart(eng):
            eng.nop(nofuse=True)

        HU = NB // 2
        MU = MH * HU
        Q_PASSES = {HU * (t - 1) + slot: [(t, n // 3, n % 3) for n in ns]
                    for t in range(2, MH) for slot, ns in enumerate(((0, 1, 2), (3, 4, 5)))}
        Q_PASSES[0] = [(1, 1, 0), (1, 1, 1)]
        Q_PASSES[1] = [(1, 1, 2)]

        KEYS_AT = (4, 5, 7)

        block = ctx.enter_context(nc.Block())

        @block.sync
        def _(sp):
            sp.dma_start(gain[:], gains).then_inc(const_in, 16)
            sp.dma_start(rope_c[:], rope_d).then_inc(const_in, 16)
            sp.dma_start(pos_i[:], positions.partition_broadcast(P)).then_inc(pos_in, 16)
            sp.dma_start(stage[:, 0, :], weights[0]).then_inc(w_in_s[0], 16)
            for k in range(0, KT, 2):
                sp.dma_start(x_f[:, k, :], xT[k]).then_inc(tile_in[k], 16)
                if k == 0:
                    sp.dma_start(stage[:, 1, :], weights[1]).then_inc(w_in_s[1], 16)
            sp.dma_start(ident[:], ident_d).then_inc(ident_in, 16)
            sp.dma_start(bias_A[:], bias_d).then_inc(bias_in, 16)
            sp.dma_start(mask_B[:], mask_d).then_inc(bias_in, 16)
            with sp.Fori(1, N_TILES // 2) as i:
                for b in range(2):
                    sp.wait_ge(w_split, i * 2 + (b - 1))
                    src = weights[bass.ds(i * 2 + b, 1), :, :].rearrange("o p n -> p (o n)")
                    sp.dma_start(stage[:, b, :], src).then_inc(w_in_s[b], 16)

        @block.gpsimd
        def _(pool):
            def split(b, loaded, tile_free, number):
                pool.wait_ge(w_in_s[b], loaded)
                if tile_free is not None:
                    pool.wait_ge(w_begun, tile_free)
                apart(pool)
                pool.tensor_scalar(w_hi[:, b, :], stage[:, b, :], 1.0, 1.0, ALU.mult, ALU.mult).then_inc(w_rounded, 1)
                pool.wait_ge(w_rounded, number)
                pool.tensor_tensor(w_lo[:, b, :], stage[:, b, :], w_hi[:, b, :].bitcast(F32),
                                   ALU.subtract).then_inc(w_split, 1)

            for b in range(2):
                split(b, 16, None, b + 1)
            with pool.Fori(1, N_TILES // 2) as i:
                for b in range(2):
                    split(b, i * 16 + 16, i * 2 + b, i * 2 + (b + 1))
            for c in range(2 * KT):
                part = rms[:, blk(c // KT, HALF)]
                pool.wait_ge(squared, 3 * KT + c + 1)
                pool.wait_ge(summed, 3 * KT + c + 1)
                pool.tensor_tensor(part, part, sq[:, blk(c % 2, HALF)], ALU.add).then_inc(summed, 1)

        @block.tensor
        def _(pe):
            def passes(bank, units, mv_hi, mv_lo, which, ks, first, last, wait=None):
                n = 0
                total = len(which) * len(ks)
                for p in which:
                    w = w_lo if p == 2 else w_hi
                    mv = mv_lo if p == 1 else mv_hi
                    for k in ks:
                        if wait and p != 2 and k in (ks[0], ks[-1]):
                            made, count = wait[p]
                            pe.wait_ge(made, count + (k == ks[-1]))
                        b, c = units(k)
                        ins = pe.matmul(bank, w[:, b, c:c + P], mv(k), start=(first and n == 0),
                                        stop=(last and n == total - 1))
                        if n == 0:
                            lead = ins
                        n += 1
                return lead, ins

            def begin_tile(number):
                pe.wait_ge(w_split, number)

            def product(bank, b, half, which=(0, 1, 2), hi=None, lo=None, wait=None):
                hi, lo = hi or n_hi, lo or n_lo
                return passes(bank, lambda k: (b, k * P), lambda k: hi[:, k, blk(half, HALF)],
                              lambda k: lo[:, k, blk(half, HALF)], which, range(KT), which[0] == 0,
                              len(which) == 3 or which[-1] == 2, wait)

            def mean(number, halves=range(2)):
                pe.wait_ge(summed, number)
                for half in halves:
                    pe.matmul(ps[:, 6 + half, :], mean_w[:], rms[:, blk(half, HALF)], start=True,
                              stop=True).then_inc(mean_full, 1)

            pe.wait_ge(mg_lo_s, KT)
            for t in range(2 * MH):
                begin_tile(t + 1)
                if t == 1:
                    pe.wait_ge(msq, 1)
                    pe.wait_ge(summed, 1)
                    for k in range(KT):
                        ins = pe.matmul(ps[:, 7, 0:NM], mean_w[:], mem_sq[:, k, :], start=(k == 0), stop=(k == KT - 1))
                    ins.then_inc(mmean, 1)
                if t == MH:
                    pe.wait_ge(mrms, 1)
                    pe.wait_ge(ident_in, 16)
                    for mt in range(2):
                        ins = pe.transpose(ps[:, 1, blk(mt)], mem_r[:, blk(mt)], ident[:])
                    ins.then_inc(r_col_full, 1)
                if t == MH + 2:
                    pe.wait_ge(r_col_ready, 1)
                    pe.wait_ge(kv_lo_s, 2)
                    pe.wait_ge(summed, KT + 1)
                    for half in range(2):
                        pe.matmul(ps[:, half, :], mean_w[:], rms[:, blk(half, HALF)], start=True, stop=True
                                  ).then_inc(bank_full, 1)
                if t < MH:
                    lead, last = passes(ps[:, 2 + t, 0:NM], lambda k: (t % 2, k * P), lambda k: mg_hi[:, k, :],
                                        lambda k: mg_lo[:, k, :], (0, 1, 2), range(KT), True, True)
                    last.then_inc(kv_full, 1)
                else:
                    first = t % 2 == 0
                    for mt in range(2):
                        item = MH + (t - MH) // 2 * 2 + mt
                        n = 0
                        for a, w in ((mg_hi, w_hi), (mg_lo, w_hi), (mg_hi, w_lo)):
                            for k in range(KT // 2):
                                last = pe.matmul(ps[:, 2 + item % 6, 0:NM], a[:, k + (0 if first else KT // 2), blk(mt)],
                                                 w[:, t % 2, blk(k, NM)], start=(first and n == 0),
                                                 stop=(not first and n == 3 * KT // 2 - 1))
                                if mt == 0 and n == 0:
                                    lead = last
                                n += 1
                        if not first:
                            last.then_inc(kv_full, 1)
                lead.then_inc(w_begun, 1)

            pe.wait_ge(nlo_ready, KT)

            def unit_pass(tile_number, buffer, half, p, banks_read):
                if p == 0:
                    if half == 0:
                        begin_tile(tile_number)
                    pe.wait_ge(bank_free, banks_read)
                lead, last = product(ps[:, half, :], buffer, half, (p,))
                if p == 0 and half == 0:
                    lead.then_inc(w_begun, 1)
                if p == 2:
                    last.then_inc(bank_full, 1)

            def v_transposes(half, number, v_read):
                if number is not None:
                    pe.wait_ge(vt_lo_s, number)
                pe.wait_ge(bank_free, v_read)
                for n in range(4):
                    ins = pe.transpose(ps[:, 5, blk(n)], raw[:, 2, blk(half * 4 + n)], ident[:])
                ins.then_inc(vt_full, 1)

            def round_(i, plan):
                base = i * UNITS
                bank = i * BANKS_ROUND + B_ROUND

                def logits(u):
                    m = "AB"[u // 16]
                    hd, qb = ORDER[u]
                    q_hi, q_lo, k_hi, k_lo = qk[m]
                    if u == 0:
                        pe.wait_ge(qk_lo_s, i * 4 + 2)
                    if u == 16:
                        pe.wait_ge(qk_lo_s, i * 4 + 4)
                    if u:
                        pe.wait_ge(logits_free, base + u)
                    hs = slice(hd * HD, (hd + 1) * HD)
                    width = (qb + 1) * P
                    for c in range(0, width, HALF):
                        w = min(HALF, width - c)
                        for n, (a, b) in enumerate(((q_hi, k_hi), (q_hi, k_lo), (q_lo, k_hi))):
                            ins = pe.matmul(ps[:, 2 + c // HALF, 0:w], a[hs, blk(qb)], b[hs, c:c + w],
                                            start=(n == 0), stop=(n == 2))
                    ins.then_inc(logits_full, 1)

                def transposes(u):
                    if u < 16:
                        pe.wait_ge(pA_ready, i * 16 + (u + 1))
                    else:
                        pe.wait_ge(pB_ready, i * 16 + (u - 15))
                    if u:
                        pe.wait_ge(pt_lo_s, base + u)
                    if u == NB:
                        pe.wait_ge(vt_lo_s, i * 4 + 4)
                    for kb in range(ORDER[u][1] + 1):
                        ins = pe.transpose(ps_t[:, blk(kb)], rows[:, u % 4, blk(kb)], ident[:])
                    ins.then_inc(pt_full, 1)

                def attend(u):
                    hd, qb = ORDER[u]
                    v = v_of["AB"[u // 16]]
                    if u == 0:
                        pe.wait_ge(vt_lo_s, i * 4 + 2)
                    if u == 16:
                        pe.wait_ge(vt_lo_s, i * 4 + 4)
                    pe.wait_ge(pt_lo_s, base + (u + 1))
                    if u >= 2:
                        pe.wait_ge(o_sum_s, base + (u - 1))
                    for kb in range(qb + 1):
                        ins = pe.matmul(ps[:, 6 + u % 2, 0:2 * P], v[:, kb, hd, :, :].rearrange("p a d -> p (a d)"),
                                        pt[:, kb, :, :].rearrange("p a q -> p (a q)"), start=(kb == 0), stop=(kb == qb))
                    ins.then_inc(av_full, 1)

                for s in range(SLOTS):
                    if s < UNITS:
                        logits(s)
                    if 0 <= s - LAG - 1 < UNITS:
                        attend(s - LAG - 1)
                    if 0 <= s - LAG < UNITS:
                        transposes(s - LAG)
                    for name, half, p in plan.fill[s]:
                        if p is None:
                            v_transposes(half, i * 4 + (SPLIT_NUMBER[name] + half - 1),
                                         bank + (plan.units["V" + name[1]] + 2))
                        else:
                            unit = plan.units[name] + half
                            tile = W_MIX + HEAD_TILES + plan.tile[name]
                            unit_pass(i * TILES_IN + (tile + 1), tile % 2, half, p, bank + (unit - 1))

            for tile in range(3):
                for half in range(2):
                    for p in range(3):
                        unit_pass(W_MIX + tile + 1, tile % 2, half, p, B_MIX + max(0, 2 * tile + half - 1))
            pe.wait_ge(kv_lo_s, 2 * MH)
            for half in range(2):
                v_transposes(half, None if half == 0 else 1, B_MIX + 6)
            with pe.Fori(0, PAIRS - 1) as i:
                round_(i, ROUND)
            round_(PAIRS - 1, LAST)

            pe.wait_ge(o_lo_s, KT // 2)
            pe.wait_ge(bank_free, B_GATED)
            with pe.Fori(0, KT // 2) as i:
                for b in range(2):
                    begin_tile(i * 2 + (W_GATED + b + 1))
                    for c in range(4):
                        m, half = c // 2, c % 2
                        n = 4 * b + c
                        if c == 2:
                            pe.wait_ge(o_lo_s, KT)
                        pe.wait_ge(bank_free, i * 8 + (B_GATED + n - 3))
                        lead, last = passes(
                            ps[:, n % 4, :], lambda k: (b, k * P), lambda k: n_hi[:, k, blk(half, HALF)],
                            lambda k: n_lo[:, k, blk(half, HALF)], (0, 1, 2), range(4 * m, 4 * m + 4), True, True)
                        if c == 0:
                            lead.then_inc(w_begun, 1)
                        last.then_inc(bank_full, 1)

            with pe.Fori(0, KT // 2) as i:
                for b in range(2):
                    begin_tile(i * 2 + (W_OUT + b + 1))
                    for half in range(2):
                        n = 2 * b + half
                        pe.wait_ge(bank_free, i * 4 + (B_OUT + n - 3))
                        if n == 0:
                            lead, last = product(ps[:, n, :], b, half, (0, 2, 1), m_hi, m_lo,
                                                 ((m_hi_s, 2 * KT - 2), (m_lo_s, 2 * KT - 2)))
                        else:
                            pe.wait_ge(m_lo_s, 2 * KT)
                            lead, last = product(ps[:, n, :], b, half, hi=m_hi, lo=m_lo)
                        if half == 0:
                            lead.then_inc(w_begun, 1)
                        last.then_inc(bank_full, 1)

            def q_pass(t, half, which, wait=None):
                p = which[0]
                if p == 0:
                    if half == 0:
                        begin_tile(W_QM + t + 1)
                    pe.wait_ge(bank_free, B_QM + 2 * t + half - (1 if t else 3))
                lead, last = product(ps[:, half, :], t % 2, half, which, wait=wait)
                if p == 0 and half == 0:
                    lead.then_inc(w_begun, 1)
                if len(which) == 3 or p == 2:
                    last.then_inc(bank_full, 1)

            q_pass(0, 0, (0, 2, 1), ((nhi_ready, 2 * KT - 1), (nlo_ready, 2 * KT - 1)))
            mean(2 * KT + 1)
            q_pass(0, 1, (0, 1, 2))
            q_pass(1, 0, (0, 1, 2))
            pe.wait_ge(bank_free, B_QM)
            pe.wait_ge(kv_in, 64)
            for s in range(MU + 3):
                if s < MU:
                    hd, qp = divmod(s, HU)
                    if qp == 0:
                        pe.wait_ge(qm_lo_s, hd + 1)
                    if s >= 2:
                        pe.wait_ge(mp_exp, s - 1)
                    for j in range(2):
                        for n, (a, b) in enumerate(((qm_hi, 0), (qm_hi, 1), (qm_lo, 0))):
                            ins = pe.matmul(ps[:, 2 + s % 2, blk(j, NM)], a[:, hd, blk(2 * qp + j)], km[:, b, hd, :],
                                            start=(n == 0), stop=(n == 2))
                    ins.then_inc(ms_full, 1)
                u = s - 2
                if 0 <= u < MU:
                    pe.wait_ge(mp_ready, u + 1)
                    if u >= 2:
                        pe.wait_ge(mt_lo, u - 1)
                    for j in range(2):
                        for mt in range(2):
                            ins = pe.transpose(ps[:, 4 + u % 2, blk(2 * mt + j)], p_m[:, u % 3, j, blk(mt)], ident[:])
                    ins.then_inc(mt_full, 1)
                u = s - 3
                if 0 <= u < MU:
                    hd = u // HU
                    pe.wait_ge(mt_lo, u + 1)
                    if u == 0:
                        pe.wait_ge(rms_ready, 2)
                    if u >= 2:
                        pe.wait_ge(om_lo, u - 1)
                    n = 0
                    for a, b in ((0, pm_hi), (0, pm_lo), (1, pm_hi)):
                        for mt in range(2):
                            ins = pe.matmul(ps[:, 6 + u % 2, 0:2 * P], vm[:, a, mt, blk(hd)], b[:, u % 2, mt, :],
                                            start=(n == 0), stop=(n == 5))
                            n += 1
                    ins.then_inc(mav_full, 1)
                for t, half, p in Q_PASSES.get(s, ()):
                    q_pass(t, half, (p,))
            pe.wait_ge(bank_free, B_OM)
            pe.wait_ge(om_lo, MU)
            with pe.Fori(0, KT // 4) as i:
                for b in range(2):
                    begin_tile(i * 2 + (W_OM + b + 1))
                    for c in range(4):
                        n = 4 * b + c
                        pe.wait_ge(bank_free, i * 8 + (B_OM + n - 3))
                        lead, last = passes(
                            ps[:, n % 4, :], lambda k: (b, (4 * (c // 2) + k) * P),
                            lambda k: qm_hi[:, k, blk(c % 2, HALF)], lambda k: qm_lo[:, k, blk(c % 2, HALF)],
                            (0, 1, 2), range(4), True, True)
                        if c == 0:
                            lead.then_inc(w_begun, 1)
                        last.then_inc(bank_full, 1)

            def wide(b, start, ring_at, wait=None):
                for half in range(2):
                    pe.wait_ge(bank_free, start + (half - 3))
                    if wait and half == 0:
                        lead, last = product(ps[:, ring_at + half, :], b, half, (0, 2, 1), wait=wait)
                    else:
                        lead, last = product(ps[:, ring_at + half, :], b, half)
                    if half == 0:
                        lead.then_inc(w_begun, 1)
                    last.then_inc(bank_full, 1)

            def down(tile, buffer, start, ring_at):
                for n in range(KT):
                    if n % 4 == 0:
                        begin_tile(tile + (n // 4 + 1))
                    b = (n // 4 + buffer) % 2
                    for half in range(2):
                        c = 2 * n + half
                        pe.wait_ge(bank_free, start + (c - 3))
                        lead, last = passes(
                            ps[:, (c + ring_at) % 4, :],
                            lambda k: (b, k * HALF + (n % 4) * P),
                            lambda k: a_hi[:, k, blk(half, HALF)], lambda k: a_lo[:, k, blk(half, HALF)],
                            (0, 1, 2), range(2), True, True)
                        if n % 4 == 0 and half == 0:
                            lead.then_inc(w_begun, 1)
                        last.then_inc(bank_full, 1)

            for t in range(4):
                begin_tile(W_FF + t + 1)
                wide(t % 2, B_FF + 2 * t, (2 * t) % 4,
                     ((nhi_ready, 3 * KT - 1), (nlo_ready, 3 * KT - 1)) if t == 0 else None)
                if t == 0:
                    mean(3 * KT + 1)
            with pe.Fori(0, FPAIRS - 1) as i:
                tile, start = i * 6 + W_FF_LOOP, i * 24 + B_FF_LOOP
                begin_tile(tile + 1)
                wide(0, start, 0)
                pe.wait_ge(a_lo_s, i * 2 + 2)
                down(tile + 1, 1, start + 2, 2)
                for t in range(3, 6):
                    begin_tile(tile + (t + 1))
                    wide(t % 2, start + (12 + 2 * t), (12 + 2 * t) % 4)
            def last_down(c, ks, last):
                half, n = divmod(c, KT)
                return passes(ps[:, c % 4, :], lambda k: (n // 4, k * HALF + (n % 4) * P),
                              lambda k: a_hi[:, k, blk(half, HALF)], lambda k: a_lo[:, k, blk(half, HALF)],
                              (0, 1, 2), ks, 0 in ks, last)

            begin_tile(W_END + 1)
            pe.wait_ge(a_lo_s, 2 * FPAIRS - 1)
            for c in range(4):
                pe.wait_ge(bank_free, B_END + c - 3)
                lead, _ = last_down(c, (0,), False)
                if c == 0:
                    lead.then_inc(w_begun, 1)
            pe.wait_ge(a_lo_s, 2 * FPAIRS)
            for c in range(2 * KT):
                if c < 4:
                    _, last = last_down(c, (1,), True)
                else:
                    if c == 4:
                        begin_tile(W_END + 2)
                    pe.wait_ge(bank_free, B_END + c - 3)
                    lead, last = last_down(c, range(2), True)
                    if c == 4:
                        lead.then_inc(w_begun, 1)
                last.then_inc(bank_full, 1)
                if c == KT + 3:
                    mean(4 * KT + 1, (0,))
            mean(5 * KT + 1, (1,))

        @block.scalar
        def _(act):
            steps = [0]

            def step(ins):
                steps[0] += 1
                ins.then_inc(act_step, 1)
                act.wait_ge(act_step, steps[0])

            act.dma_start(mem_f[:], memT).then_inc(mem_in, 16)
            for k in range(1, KT, 2):
                act.dma_start(x_f[:, k, :], xT[k]).then_inc(tile_in[k], 16)
            act.preload_act_table_set("natural_log_exp_and_others")

            def factors(number):
                if number == 1:
                    act.wait_ge(bank_free, B_MIX)
                else:
                    act.wait_ge(rms_raw, number - 1)
                step(act.activation(rms[:], rms[:], ACT.Ln))
                act.activation(rms[:], rms[:], ACT.Exp, scale=-0.5).then_inc(rms_ready, 1)

            def kv_hi(t):
                if t < MH:
                    act.wait_ge(k_f_ready, t + 1)
                    act.activation(km_out[:, 0, t, :], k_f[:], ACT.Copy).then_inc(kv_hi_s, 1)
                else:
                    pair, mt = divmod(t - MH, 2)
                    act.wait_ge(kv_full, t + 1)
                    act.wait_ge(r_col_ready, 1)
                    act.activation(vm_out[:, 0, mt, blk(pair, NM)], ps[:, 2 + t % 6, 0:NM], ACT.Copy,
                                   scale=r_col[:, mt:mt + 1]).then_inc(kv_hi_s, 1)

            act.wait_ge(mem_in, 16)
            act.wait_ge(const_in, 32)
            for k in range(KT):
                act.activation(mg_hi[:, k, :], mem_f[:, k, :], ACT.Copy, scale=gain[:, G_MEMKV + k:G_MEMKV + k + 1]
                               ).then_inc(mg_hi_s, 1)
            act.activation(mem_sq[:], mem_f[:], ACT.Square).then_inc(msq, 1)
            for k in range(KT):
                act.wait_ge(tile_in[k], 16)
                act.activation(n_hi[:, k, :], x_f[:, k, :], ACT.Copy, scale=gain[:, G_MIX + k:G_MIX + k + 1]
                               ).then_inc(nhi_ready, 1)
                if k >= 2:
                    act.wait_ge(summed, k)
                act.activation(sq0[:, k % 2, :], x_f[:, k, :], ACT.Square).then_inc(squared, 1)
                if k == 3:
                    act.wait_ge(mrms_raw, 1)
                    step(act.activation(mem_r[:], mem_r[:], ACT.Ln))
                    act.activation(mem_r[:], mem_r[:], ACT.Exp, scale=-0.5).then_inc(mrms, 1)
                if k in KEYS_AT:
                    kv_hi(KEYS_AT.index(k))
            kv_hi(len(KEYS_AT))
            act.wait_ge(nlo_ready, KT)
            act.wait_ge(ang_ready, 1)
            act.activation(sin_t[:], rnd[:, 0, :], ACT.Sin).then_inc(sin_ready, 1)
            act.wait_ge(ang_ready, 2)
            act.activation(cos_t[:], rnd[:, 1, :], ACT.Sin).then_inc(sin_ready, 1)
            act.preload_act_table_set("natural_log_exp_and_others")
            for t in range(len(KEYS_AT) + 1, 2 * MH):
                kv_hi(t)
            factors(1)
            act.wait_ge(kv_lo_s, 2 * MH)
            for a in range(2):
                act.dma_start(kv_d[a], km_out[:, a, :, :].rearrange("p h n -> p (h n)").bitcast(F32)).then_inc(kv_out, 16)
                act.dma_start(kv_d[2 + a], vm_out[:, a, :, :].rearrange("p m n -> p (m n)").bitcast(F32)).then_inc(kv_out, 16)
            act.wait_ge(kv_out, 64)

            def swap_dma(n, src):
                for head in (0, HD):
                    for to, of in ((0, 8), (8, 0)):
                        act.dma_start(swap[head + to:head + to + 8, :], raw[head + of:head + of + 8, src, :]
                                      ).then_inc(swap_in[n], 16)

            def round_hi(name):
                m, which = name[1], name[0]
                act.activation(qk[m][0 if which == "Q" else 2][:], raw[:, RAW[name], :], ACT.Copy).then_inc(qk_hi_s, 1)

            def v_hi(m, half, number):
                act.wait_ge(vt_full, number)
                act.activation(v_of[m][:, blk(half, 4), :, 0, :],
                               ps[:, 5, :].rearrange("p (n h d) -> p n h d", n=4, h=2), ACT.Copy
                               ).then_inc(vt_hi_s, 1)

            for n, name in enumerate(("QA", "KA")):
                act.wait_ge(bank_free, B_MIX + 2 * n + 2)
                swap_dma(n, n)
                act.wait_ge(rope_done, n + 1)
                round_hi(name)
            for half in range(2):
                v_hi("A", half, half + 1)

            def round_(i, plan):
                base = i * UNITS
                bank = i * BANKS_ROUND + B_ROUND
                for s in range(SLOTS + 2):
                    u = s
                    if 16 <= u < UNITS:
                        width = (ORDER[u][1] + 1) * P
                        act.wait_ge(logits_full, base + (u + 1))
                        act.activation(rows[:, u % 4, 0:width], ps_rows[:, 0:width], ACT.Copy, scale=HD ** -0.5
                                       ).then_inc(logits_free, 1)
                    u = s - LAG - 2
                    if 0 <= u < UNITS:
                        act.wait_ge(av_full, base + (u + 1))
                        if u >= 2:
                            act.wait_ge(o_sum_s, base + (u - 1))
                        act.activation(o_low[:, u % 2, :], ps[HD:P, 6 + u % 2, 0:P], ACT.Copy).then_inc(o_low_s, 1)
                    u = s - LAG
                    if 0 <= u < UNITS:
                        width = (ORDER[u][1] + 1) * P
                        act.wait_ge(pt_full, base + (u + 1))
                        act.activation(pt[:, 0:width // P, 0, :], ps_t[:, 0:width].rearrange("p (n q) -> p n q", q=P),
                                       ACT.Copy).then_inc(pt_hi_s, 1)
                    u = s - 2
                    if 16 <= u < UNITS:
                        row = rows[:, u % 4, 0:(ORDER[u][1] + 1) * P]
                        act.wait_ge(arg_ready, i * 16 + (u - 15))
                        act.activation(row, row, ACT.Exp).then_inc(pB_ready, 1)
                    u = s
                    if u < UNITS:
                        width = (ORDER[u][1] + 1) * P
                        if u < 16:
                            row = rows[:, u % 4, 0:width]
                            c = u % 4
                            act.wait_ge(max_ready, i * 16 + (u + 1))
                            act.activation(row, row, ACT.Exp, scale=HD ** -0.5, bias=stat[:, 1, c:c + 1],
                                           accum_out=stat[:, 2, c:c + 1]).then_inc(exp_ready, 1)
                        else:
                            e = e_row[:, u % 2, 0:width]
                            act.wait_ge(abs_ready, i * 16 + (u - 15))
                            act.activation(e, e, ACT.Exp).then_inc(act_step, 1)
                            act.wait_ge(act_step, i * 16 + (STEPS_ACT + u - 15))
                            act.activation(e, e, ACT.Ln, bias=1.0).then_inc(soft_ready, 1)
                    for what, name, *rest in plan.after["act"][s]:
                        unit = plan.units.get(name)
                        if what == "v_hi":
                            v_hi(name[1], rest[0], i * 4 + (SPLIT_NUMBER[name] + rest[0]))
                        elif what == "swap":
                            act.wait_ge(bank_free, bank + (unit + 2))
                            if name == "KA":
                                act.wait_ge(rope_done, i * 2 + 3)
                            swap_dma(RAW[name], RAW[name])
                        elif what == "hi":
                            if name[1] == "A":
                                act.wait_ge(rope_done, i * 2 + (3 + RAW[name]))
                            else:
                                act.wait_ge(bank_free, bank + (unit + 2))
                            round_hi(name)
                        elif what == "store":
                            m = int(name[1])
                            act.wait_ge(bank_free, bank + (unit + 2))
                            act.dma_start(gates_d[bass.ds(i * 4 + m, 1), :, :].rearrange("o p n -> p (o n)"),
                                          raw[:, RAW[name], :]).then_inc(gate_out[m % 2], 16)
                    u = s - LAG - 3
                    if 0 <= u < UNITS:
                        store_o(i, u)
                    if plan is LAST and s in LOAD_O:
                        act.wait_ge(bank_full, B_GATED)
                        for b in range(4):
                            act.wait_ge(o_out[b], 16 + 16 * (UNITS // 4 * i + UNITS // 8))
                        for k in LOAD_O[s]:
                            act.dma_start(n_lo[:, k, :].bitcast(F32), o_d[k]).then_inc(tile_in[k], 16)
                    if plan is LAST and s in ROUND_O:
                        round_o(ROUND_O[s])

            def round_o(k):
                act.wait_ge(tile_in[k], 32)
                act.activation(n_hi[:, k, :], n_lo[:, k, :].bitcast(F32), ACT.Copy).then_inc(o_hi_s, 1)

            def store_o(i, u):
                hd, qb = ORDER[u]
                act.wait_ge(o_sum_s, i * UNITS + (u + 1))
                dst = o_d[bass.ds(i + 4 * (u // 16), 1), hd * HD:(hd + 1) * HD, blk(qb)].rearrange("o p n -> p (o n)")
                act.dma_start(dst, o_of(u)).then_inc(o_out[u % 4], 16)

            STEPS_ACT = steps[0]
            with act.Fori(0, PAIRS - 1) as i:
                round_(i, ROUND)
            round_(PAIRS - 1, LAST)
            steps[0] += PAIRS * 16

            def load_gates(j, b):
                for g, at in ((g_a, 0), (g_b, KT)):
                    act.dma_start(g[:, b, :], gates_d[bass.ds(j + at, 1), :, :].rearrange("o p n -> p (o n)")
                                  ).then_inc(g_in[b], 16)

            for b in range(4):
                act.wait_ge(o_out[b], PAIRS * UNITS // 4 * 16 + 16)
            for b in range(2):
                act.wait_ge(gate_out[b], PAIRS * 2 * 16 + 16)
            act.dma_start(n_lo[:, KT - 1, :].bitcast(F32), o_d[KT - 1]).then_inc(tile_in[KT - 1], 16)
            load_gates(0, 0)
            load_gates(1, 1)
            for k in range(len(ROUND_O), KT):
                round_o(k)
            for k in range(EARLY_H):
                act.dma_start(h[:, k, :], xT[k]).then_inc(tile_in[k], 16)
            act.preload_act_table(ACT.Sigmoid)

            def gated(i, more):
                for b in range(2):
                    act.wait_ge(g_in[b], i * 32 + 32)
                    for g in (g_a, g_b):
                        act.activation(g[:, b, :], g[:, b, :], ACT.Sigmoid).then_inc(g_ready, 1)
                    for half in range(2):
                        act.wait_ge(y_ready, i * 4 + (2 * b + half + 1))
                        apart(act)
                        act.activation(m_hi[:, bass.ds(i * 2 + b, 1), blk(half, HALF)].rearrange("p o n -> p (o n)"),
                                       y_a[:, 2 * b + half, :], ACT.Copy).then_inc(m_hi_s, 1)
                    if more:
                        load_gates(i * 2 + (b + 2), b)

            with act.Fori(0, KT // 2 - 1) as i:
                gated(i, True)
            gated(KT // 2 - 1, False)

            act.wait_ge(y_ready, 2 * KT)
            act.wait_ge(m_lo_s, 2 * KT)
            for k in range(EARLY_H, KT):
                act.dma_start(h[:, k, :], xT[k]).then_inc(tile_in[k], 16)
            act.preload_act_table_set("natural_log_exp_and_others")

            def next_operand(j, number, g, banks):
                act.wait_ge(bank_free, banks)
                hj = h[:, j, :] if isinstance(j, int) else h[:, bass.ds(j, 1), :].rearrange("p o n -> p (o n)")
                nj = n_hi[:, j, :] if isinstance(j, int) else n_hi[:, bass.ds(j, 1), :].rearrange("p o n -> p (o n)")
                gj = gain[:, g + j:g + j + 1] if isinstance(j, int) else gain[:, bass.ds(j + g, 1)]
                apart(act)
                act.activation(nj, hj, ACT.Copy, scale=gj).then_inc(nhi_ready, 1)
                act.wait_ge(summed, number + (KT + 1))
                apart(act)
                act.activation(sq[:], hj, ACT.Square).then_inc(squared, 1)

            with act.Fori(0, KT // 2) as i:
                for b in range(2):
                    next_operand(i * 2 + b, i * 2 + b, G_MEMQ, i * 4 + (B_OUT + 2 * b + 2))

            act.wait_ge(bank_full, B_QM)
            for a in range(2):
                act.dma_start(km[:, a, :, :].rearrange("p h n -> p (h n)").bitcast(F32), kv_d[a]).then_inc(kv_in, 16)
                act.dma_start(vm[:, a, :, :].rearrange("p m n -> p (m n)").bitcast(F32), kv_d[2 + a]).then_inc(kv_in, 16)
            factors(2)

            def q_round(t):
                act.wait_ge(bank_free, B_QM + 2 * t + 2)
                act.activation(qm_hi[:, t, :], q_t[:], ACT.Copy).then_inc(qm_hi_s, 1)

            q_round(0)
            for s in range(MU + 4):
                if s < MU:
                    act.wait_ge(mx_ready, s + 1)
                    for j in range(2):
                        c = 2 * (s % 2) + j
                        ins = act.activation(p_m[:, s % 3, j, :], ps[:, 2 + s % 2, blk(j, NM)], ACT.Exp,
                                             scale=P ** -0.5, bias=stat[:, 1, c:c + 1], accum_out=stat[:, 2, c:c + 1])
                    ins.then_inc(mp_exp, 1)
                u = s - 2
                if 0 <= u < MU:
                    act.wait_ge(mt_full, u + 1)
                    if u >= 2:
                        act.wait_ge(mav_full, u - 1)
                    act.activation(pm_hi[:, u % 2, :, :], ps[:, 4 + u % 2, :].rearrange("p (m n) -> p m n", m=2), ACT.Copy
                                   ).then_inc(mt_hi, 1)
                u = s - 3
                if 0 <= u < MU:
                    hd, qp = divmod(u, HU)
                    act.wait_ge(mav_full, u + 1)
                    act.activation(qm_hi[:, hd, blk(qp, 2 * P)], ps[:, 6 + u % 2, 0:2 * P], ACT.Copy).then_inc(om_hi, 1)
                if s % HU == 2 and s // HU + 1 < MH:
                    q_round(s // HU + 1)
            with act.Fori(0, KT // 4) as i:
                for b in range(4):
                    next_operand(i * 4 + b, i * 4 + (b + KT), G_FFN, i * 8 + (B_OM + 2 * b + 2))

            factors(3)
            act.preload_act_table(ACT.Silu)

            def hidden(f, gate_out_of_psum, number):
                act.wait_ge(bank_free, gate_out_of_psum)
                act.activation(g_f[:, f, :], g_f[:, f, :], ACT.Silu).then_inc(silu_ready, 1)
                act.wait_ge(hidden_ready, number)
                act.activation(a_hi[:, f, :], u_f[:, f, :], ACT.Copy).then_inc(a_hi_s, 1)

            for f in range(2):
                hidden(f, B_FF + 4 * f + 2, f + 1)
            with act.Fori(0, FPAIRS - 1) as i:
                for f in range(2):
                    hidden(f, i * 24 + (B_FF_LOOP + (2, 22)[f]), i * 2 + (f + 3))
            act.preload_act_table_set("natural_log_exp_and_others")

            def last_factors(half):
                act.wait_ge(rms_raw, 3 + half)
                part = rms[:, blk(half, HALF)]
                step(act.activation(part, part, ACT.Ln))
                act.activation(part, part, ACT.Exp, scale=-0.5).then_inc(rms_ready, 1)

            def store(half, k):
                act.wait_ge(out_ready, half * KT + k + 1)
                act.dma_start(outT[k][:, blk(half, HALF)], h[:, k, blk(half, HALF)]).then_inc(out_done, 16)

            for c in range(2 * KT):
                half, j = divmod(c, KT)
                act.wait_ge(bank_free, B_END + c + 1)
                if c >= 2:
                    act.wait_ge(summed, 3 * KT + c)
                act.activation(sq[:, blk(c % 2, HALF)], h[:, j, blk(half, HALF)], ACT.Square).then_inc(squared, 1)
                if c == NORM_AT:
                    last_factors(0)
            for k in range(KT):
                store(0, k)
            last_factors(1)
            for k in range(KT):
                store(1, k)
            act.wait_ge(out_done, 32 * KT)

        @block.vector
        def _(dve):
            steps = [0]

            def step(ins):
                steps[0] += 1
                ins.then_inc(dve_step, 1)
                dve.wait_ge(dve_step, steps[0])

            def flat(ap):
                return ap.rearrange("p o n -> p (o n)")

            def raw_factors(number):
                dve.wait_ge(mean_full, 2 * number - 2)
                dve.tensor_scalar(rms[:], flat(ps[:, 6:8, :]), EPS, None, ALU.add).then_inc(rms_raw, 1)

            dve.memset(rms[:], 0.0)
            dve.memset(mean_w[:], 1.0 / D).then_inc(summed, 1)
            dve.wait_ge(summed, 1)
            dve.wait_ge(const_in, 32)
            for k in range(KT):
                dve.wait_ge(mg_hi_s, k + 1)
                dve.scalar_tensor_tensor(mg_lo[:, k, :], mem_f[:, k, :], gain[:, G_MEMKV + k:G_MEMKV + k + 1],
                                         mg_hi[:, k, :].bitcast(F32), ALU.mult, ALU.subtract).then_inc(mg_lo_s, 1)
            dve.wait_ge(pos_in, 16)
            step(dve.tensor_copy(ang[:], pos_i[:]))
            step(dve.tensor_scalar(ang[:], ang[:], rope_c[:, 0:1], None, ALU.mult))
            big = 12582912.0
            step(dve.tensor_scalar(rnd[:, 0, :], ang[:], 0.15915494309189535, big, ALU.mult, ALU.add))
            step(dve.tensor_scalar(rnd[:, 0, :], rnd[:, 0, :], -big, None, ALU.add))
            for part in (6.28125, 0.0019350051879882812, 3.0199159819390456e-07):
                step(dve.scalar_tensor_tensor(ang[:], rnd[:, 0, :], -part, ang[:], ALU.mult, ALU.add))
            pi = 3.1415925
            step(dve.tensor_scalar(ang[:], ang[:], pi, -pi, ALU.min, ALU.max))
            def kv_lo(t):
                bank = ps[:, 2 + t % 6, 0:NM]
                if t < MH:
                    dve.wait_ge(kv_full, t + 1)
                    if t:
                        dve.wait_ge(kv_lo_s, t)
                    else:
                        dve.wait_ge(mrms, 1)
                    dve.tensor_tensor(k_f[:], bank, mem_r[:], ALU.mult).then_inc(k_f_ready, 1)
                    dve.wait_ge(k_f_ready, t + 1)
                    dve.wait_ge(kv_hi_s, t + 1)
                    dve.tensor_tensor(km_out[:, 1, t, :], k_f[:], km_out[:, 0, t, :].bitcast(F32), ALU.subtract
                                      ).then_inc(kv_lo_s, 1)
                    return
                pair, mt = divmod(t - MH, 2)
                dve.wait_ge(kv_hi_s, t + 1)
                dve.scalar_tensor_tensor(vm_out[:, 1, mt, blk(pair, NM)], bank, r_col[:, mt:mt + 1],
                                         vm_out[:, 0, mt, blk(pair, NM)].bitcast(F32), ALU.mult, ALU.subtract
                                         ).then_inc(kv_lo_s, 1)

            for k in range(KT):
                dve.wait_ge(nhi_ready, k + 1)
                dve.scalar_tensor_tensor(n_lo[:, k, :], x_f[:, k, :], gain[:, G_MIX + k:G_MIX + k + 1],
                                         n_hi[:, k, :].bitcast(F32), ALU.mult, ALU.subtract).then_inc(nlo_ready, 1)
                dve.wait_ge(squared, k + 1)
                if k:
                    dve.wait_ge(summed, k + 1)
                dve.tensor_tensor(rms[:], rms[:], sq0[:, k % 2, :], ALU.add).then_inc(summed, 1)
                if k == 2:
                    dve.wait_ge(mmean, 1)
                    dve.tensor_scalar(mem_r[:], ps[:, 7, 0:NM], EPS, None, ALU.add).then_inc(mrms_raw, 1)
                if k in KEYS_AT:
                    kv_lo(KEYS_AT.index(k))
            dve.wait_ge(r_col_full, 1)
            for mt in range(2):
                ins = dve.tensor_copy(r_col[:, mt:mt + 1], ps[:, 1, mt * P:mt * P + 1])
            ins.then_inc(r_col_ready, 1)
            dve.wait_ge(r_col_ready, 1)
            kv_lo(len(KEYS_AT))
            step(dve.scalar_tensor_tensor(rnd[:, 1, :], ang[:], -1.0, ang[:], ALU.mult, ALU.max))
            dve.tensor_scalar(rnd[:, 0, :], ang[:], rope_c[:, 1:2], None, ALU.mult).then_inc(ang_ready, 1)
            dve.tensor_scalar(rnd[:, 1, :], rnd[:, 1, :], -1.0, pi / 2, ALU.mult, ALU.add).then_inc(ang_ready, 1)
            for t in range(len(KEYS_AT) + 1, 2 * MH):
                kv_lo(t)
            dve.wait_ge(bank_full, 2)
            for half in range(2):
                dve.tensor_scalar(rms[:, blk(half, HALF)], ps[:, half, :], EPS, None, ALU.add).then_inc(bank_free, 1)
            dve.wait_ge(sin_ready, 2)
            step(dve.memset(swap[:], 0.0))
            for b in range(4):
                dve.memset(o_of(b), 0.0).then_inc(o_out[b], 16)
            for b in range(2):
                dve.memset(raw[:, b, 0:1], 0.0).then_inc(gate_out[b], 16)
            for b in range(2):
                dve.wait_ge(gate_out[b], 16)
            dve.wait_ge(rms_ready, 1)

            def read_out(name, half, bank_unit):
                dve.wait_ge(bank_full, bank_unit + 1)
                dve.tensor_tensor(raw[:, RAW[name], blk(half, HALF)], ps[:, half, :], rms[:, blk(half, HALF)],
                                  ALU.mult).then_inc(bank_free, 1)

            def lo_part(name, number, filled):
                dst, hi = qk[name[1]][1 if name[0] == "Q" else 3], qk[name[1]][0 if name[0] == "Q" else 2]
                dve.wait_ge(bank_free, filled)
                dve.wait_ge(qk_hi_s, number)
                dve.tensor_tensor(dst[:], raw[:, RAW[name], :], hi[:].bitcast(F32), ALU.subtract).then_inc(qk_lo_s, 1)

            def rope(src, swapped, follow, parts=range(3)):
                x = raw[:, src, :]
                if 0 in parts:
                    dve.wait_ge(swap_in[src], swapped)
                    follow(dve.tensor_tensor(swap[:], swap[:], sin_t[:], ALU.mult))
                if 1 in parts:
                    follow(dve.tensor_tensor(x, x, cos_t[:], ALU.mult))
                if 2 in parts:
                    dve.tensor_tensor(x, x, swap[:], ALU.add).then_inc(rope_done, 1)

            def v_lo(m, half, number):
                v = v_of[m]
                dve.wait_ge(vt_hi_s, number)
                dve.tensor_tensor(v[:, blk(half, 4), :, 1, :],
                                  ps[:, 5, :].rearrange("p (n h d) -> p n h d", n=4, h=2),
                                  v[:, blk(half, 4), :, 0, :].bitcast(F32), ALU.subtract).then_inc(vt_lo_s, 1)

            read_out("QA", 0, B_MIX)
            read_out("QA", 1, B_MIX + 1)
            read_out("KA", 0, B_MIX + 2)
            rope(0, 64, step)
            read_out("KA", 1, B_MIX + 3)
            lo_part("QA", 1, B_MIX + 2)
            read_out("VA", 0, B_MIX + 4)
            rope(1, 64, step)
            read_out("VA", 1, B_MIX + 5)
            lo_part("KA", 2, B_MIX + 4)
            for half in range(2):
                v_lo("A", half, half + 1)

            def o_rest(k):
                dve.wait_ge(o_hi_s, k + 1)
                dve.tensor_tensor(n_lo[:, k, :], n_lo[:, k, :].bitcast(F32), n_hi[:, k, :].bitcast(F32),
                                  ALU.subtract).then_inc(o_lo_s, 1)

            def round_(i, plan, links):
                base = i * UNITS
                bank = i * BANKS_ROUND + B_ROUND
                local = [0]

                def link(ins):
                    local[0] += 1
                    ins.then_inc(dve_step, 1)
                    dve.wait_ge(dve_step, i * LINKS + (steps[0] + local[0]))

                for s in range(SLOTS + 2):
                    u = s
                    if u < UNITS:
                        width = (ORDER[u][1] + 1) * P
                        row = rows[:, u % 4, 0:width]
                        c = u % 4
                        if u < 16:
                            dve.wait_ge(logits_full, base + (u + 1))
                            apart(dve)
                            dve.tensor_tensor_reduce(
                                out=row, in0=ps_rows[:, 0:width], in1=bias_A[:, T - width:T], scale=1.0,
                                scalar=NEG_MAX, op0=ALU.add, op1=ALU.max, accum_out=stat[:, 0, c:c + 1]
                            ).then_inc(logits_free, 1)
                            dve.wait_ge(logits_free, base + (u + 1))
                            dve.tensor_scalar(stat[:, 1, c:c + 1], stat[:, 0, c:c + 1], -HD ** -0.5, None, ALU.mult
                                              ).then_inc(max_ready, 1)
                        else:
                            dve.wait_ge(logits_free, base + (u + 1))
                            link(dve.tensor_tensor(row[:, width - P:width], row[:, width - P:width], mask_B[:], ALU.add))
                            dve.scalar_tensor_tensor(e_row[:, u % 2, 0:width], row, -1.0, row, ALU.mult, ALU.min
                                                     ).then_inc(abs_ready, 1)
                    u = s - LAG - 2
                    if 0 <= u < UNITS:
                        dve.wait_ge(o_low_s, base + (u + 1))
                        o = o_low[:, u % 2, :]
                        link(dve.tensor_tensor(o, ps[0:HD, 6 + u % 2, 0:P], o, ALU.add))
                        dve.wait_ge(o_out[u % 4], i * (UNITS // 4 * 16) + (u // 4 + 1) * 16)
                        dve.tensor_tensor(o_of(u), o, ps[0:HD, 6 + u % 2, P:2 * P], ALU.add).then_inc(o_sum_s, 1)
                    u = s - LAG
                    if 0 <= u < UNITS:
                        width = (ORDER[u][1] + 1) * P
                        dve.wait_ge(pt_hi_s, base + (u + 1))
                        nb = width // P
                        dve.tensor_tensor(pt[:, 0:nb, 1, :], ps_t[:, 0:width].rearrange("p (n q) -> p n q", q=P),
                                          pt[:, 0:nb, 0, :].bitcast(F32), ALU.subtract).then_inc(pt_lo_s, 1)
                    u = s - 1
                    if 0 <= u < 16:
                        width = (ORDER[u][1] + 1) * P
                        c = u % 4
                        dve.wait_ge(exp_ready, i * 16 + (u + 1))
                        link(dve.reciprocal(stat[:, 3, c:c + 1], stat[:, 2, c:c + 1]))
                        row = rows[:, u % 4, 0:width]
                        dve.tensor_scalar(row, row, stat[:, 3, c:c + 1], None, ALU.mult).then_inc(pA_ready, 1)
                    if 16 <= u < UNITS:
                        width = (ORDER[u][1] + 1) * P
                        row, c_row, e = rows[:, u % 4, 0:width], r_row[:, 0:width], e_row[:, u % 2, 0:width]
                        if u > 16:
                            dve.wait_ge(arg_ready, i * 16 + (u - 16))
                        link(dve.tensor_scalar(c_row, row, 0.0, None, ALU.max))
                        dve.wait_ge(soft_ready, i * 16 + (u - 15))
                        link(dve.tensor_tensor_scan(c_row[:, ::-1], c_row[:, ::-1], e[:, ::-1], 0.0, ALU.add, ALU.add))
                        dve.tensor_tensor(row, row, c_row, ALU.subtract).then_inc(arg_ready, 1)
                    for what, name, *rest in plan.after["dve"][s]:
                        unit = plan.units.get(name)
                        if what == "v_lo":
                            v_lo(name[1], rest[0], i * 4 + (SPLIT_NUMBER[name] + rest[0]))
                        elif what == "rope":
                            rope(RAW[name], i * 64 + 128, link, rest)
                        elif what == "lo":
                            lo_part(name, i * 4 + SPLIT_NUMBER[name], bank + (unit + 2))
                        elif what == "read":
                            split = {"KB": 1, "QB": 2, "G0": 3, "G1": 4, "G3": 6 if plan is ROUND else None}.get(name)
                            stored = {"KB": 1, "QB": 1, "G2": 2, "QA": 3, "KA": 2,
                                      "G3": 2 if plan is LAST else None}.get(name)
                            if rest[0] == 0 and split:
                                dve.wait_ge(qk_lo_s, i * 4 + split)
                            if rest[0] == 0 and stored:
                                dve.wait_ge(gate_out[RAW[name]], i * 32 + 16 * stored)
                            read_out(name, rest[0], bank + (unit + rest[0]))
                    if plan is LAST and s - 1 in ROUND_O:
                        o_rest(ROUND_O[s - 1])
                assert local[0] == links

            LINKS = UNITS + 16 + 3 * 16 + 4
            dve.wait_ge(bias_in, 32)
            with dve.Fori(0, PAIRS - 1) as i:
                round_(i, ROUND, LINKS)
            round_(PAIRS - 1, LAST, LINKS - 4)
            steps[0] += PAIRS * LINKS - 4

            for k in range(SLOTS + 1 - min(ROUND_O), KT):
                o_rest(k)

            def column(t, j):
                return t[:, j, :] if isinstance(j, int) else flat(t[:, bass.ds(j, 1), :])

            with dve.Fori(0, KT // 2) as i:
                for b in range(2):
                    j = i * 2 + b
                    dve.wait_ge(g_ready, i * 4 + (2 * b + 2))
                    for c in range(4):
                        m, half = c // 2, c % 2
                        n = 4 * b + c
                        ya, yb = y_a[:, 2 * b + half, :], y_b[:, half, :]
                        dve.wait_ge(bank_full, i * 8 + (B_GATED + n + 1))
                        dve.tensor_tensor((ya, yb)[m], ps[:, n % 4, :], (g_a, g_b)[m][:, b, blk(half, HALF)], ALU.mult
                                          ).then_inc(bank_free, 1)
                        if m == 0:
                            continue
                        dve.wait_ge(bank_free, i * 8 + (B_GATED + n + 1))
                        dve.tensor_tensor(ya, ya, yb, ALU.add).then_inc(y_ready, 1)
                        dve.wait_ge(m_hi_s, i * 4 + (2 * b + half + 1))
                        hi = flat(m_hi[:, bass.ds(j, 1), blk(half, HALF)])
                        lo = flat(m_lo[:, bass.ds(j, 1), blk(half, HALF)])
                        dve.tensor_tensor(lo, ya, hi.bitcast(F32), ALU.subtract).then_inc(m_lo_s, 1)

            def add_product(j, bank, start):
                for half in range(2):
                    dve.wait_ge(bank_full, start + (half + 1))
                    hj = (h[:, j, blk(half, HALF)] if isinstance(j, int)
                          else flat(h[:, bass.ds(j, 1), blk(half, HALF)]))
                    dve.tensor_tensor(hj, ps[:, bank + half, :], hj, ALU.add).then_inc(bank_free, 1)

            def next_operand(j, number, g, start):
                dve.wait_ge(bank_free, start + 2)
                dve.wait_ge(nhi_ready, number + (KT + 1))
                gj = gain[:, bass.ds(j + g, 1)]
                dve.scalar_tensor_tensor(column(n_lo, j), column(h, j), gj, column(n_hi, j).bitcast(F32),
                                         ALU.mult, ALU.subtract).then_inc(nlo_ready, 1)
                dve.wait_ge(squared, number + (KT + 1))
                dve.wait_ge(summed, number + (KT + 1))
                dve.tensor_tensor(rms[:], rms[:], sq[:], ALU.add).then_inc(summed, 1)

            def out_pair(i):
                for b in range(2):
                    start = i * 4 + (B_OUT + 2 * b)
                    add_product(i * 2 + b, 2 * b, start)
                    next_operand(i * 2 + b, i * 2 + b, G_MEMQ, start)

            step(dve.memset(rms[:], 0.0))
            for k in range(EARLY_H):
                dve.wait_ge(tile_in[k], 48)
            with dve.Fori(0, EARLY_H // 2) as i:
                out_pair(i)
            for k in range(EARLY_H, KT):
                dve.wait_ge(tile_in[k], 48)
            with dve.Fori(EARLY_H // 2, KT // 2) as i:
                out_pair(i)

            raw_factors(2)
            dve.wait_ge(rms_ready, 2)

            def q_read(t, half):
                n = 2 * t + half
                if t and half == 0:
                    dve.wait_ge(qm_lo_s, t)
                dve.wait_ge(bank_full, B_QM + n + 1)
                dve.tensor_tensor(q_t[:, blk(half, HALF)], ps[:, half, :], rms[:, blk(half, HALF)], ALU.mult
                                  ).then_inc(bank_free, 1)

            def q_split(t):
                dve.wait_ge(bank_free, B_QM + 2 * t + 2)
                dve.wait_ge(qm_hi_s, t + 1)
                dve.tensor_tensor(qm_lo[:, t, :], q_t[:], qm_hi[:, t, :].bitcast(F32), ALU.subtract).then_inc(qm_lo_s, 1)

            q_read(0, 0)
            q_read(0, 1)
            q_split(0)
            for s in range(MU + 4):
                t = s // HU + 1
                if s < MU:
                    c = slice(2 * (s % 2), 2 * (s % 2) + 2)
                    dve.wait_ge(ms_full, s + 1)
                    step(dve.reduce_max(stat[:, 0, c], ps[:, 2 + s % 2, :].rearrange("p (j n) -> p j n", j=2), AX_X))
                    dve.tensor_scalar(stat[:, 1, c], stat[:, 0, c], -P ** -0.5, None, ALU.mult).then_inc(mx_ready, 1)
                if s % HU == 2 and t < MH:
                    q_read(t, 1)
                u = s - 1
                if 0 <= u < MU:
                    c = 2 * (u % 2)
                    dve.wait_ge(mp_exp, u + 1)
                    dve.reciprocal(stat[:, 3, c:c + 2], stat[:, 2, c:c + 2]).then_inc(mr_ready, 1)
                    dve.wait_ge(mr_ready, u + 1)
                    for j in range(2):
                        ins = dve.tensor_scalar(p_m[:, u % 3, j, :], p_m[:, u % 3, j, :], stat[:, 3, c + j:c + j + 1],
                                                None, ALU.mult)
                    ins.then_inc(mp_ready, 1)
                u = s - 2
                if 0 <= u < MU:
                    dve.wait_ge(mt_hi, u + 1)
                    dve.tensor_tensor(pm_lo[:, u % 2, :, :], ps[:, 4 + u % 2, :].rearrange("p (m n) -> p m n", m=2),
                                      pm_hi[:, u % 2, :, :].bitcast(F32), ALU.subtract).then_inc(mt_lo, 1)
                u = s - 3
                if 0 <= u < MU:
                    hd, qp = divmod(u, HU)
                    dve.wait_ge(om_hi, u + 1)
                    dve.tensor_tensor(qm_lo[:, hd, blk(qp, 2 * P)], ps[:, 6 + u % 2, 0:2 * P],
                                      qm_hi[:, hd, blk(qp, 2 * P)].bitcast(F32), ALU.subtract).then_inc(om_lo, 1)
                if t < MH and s % HU == 1:
                    q_read(t, 0)
                if t < MH and s % HU == 2:
                    q_split(t)
            step(dve.memset(rms[:], 0.0))
            with dve.Fori(0, KT // 4) as i:
                for b in range(4):
                    start = i * 8 + (B_OM + 2 * b)
                    add_product(i * 4 + b, (2 * b) % 4, start)
                    next_operand(i * 4 + b, i * 4 + (b + KT), G_FFN, start)

            raw_factors(3)
            dve.wait_ge(rms_ready, 3)

            def half_out(dst, unit, bank):
                for half in range(2):
                    dve.wait_ge(bank_full, unit + (half + 1))
                    dve.tensor_tensor(dst[:, blk(half, HALF)], ps[:, bank + half, :], rms[:, blk(half, HALF)],
                                      ALU.mult).then_inc(bank_free, 1)

            def hidden(f, unit, bank, number):
                half_out(u_f[:, f, :], unit, bank)
                dve.wait_ge(bank_free, unit + 2)
                dve.wait_ge(silu_ready, number)
                dve.tensor_tensor(u_f[:, f, :], u_f[:, f, :], g_f[:, f, :], ALU.mult).then_inc(hidden_ready, 1)
                dve.wait_ge(a_hi_s, number)
                dve.tensor_tensor(a_lo[:, f, :], u_f[:, f, :], a_hi[:, f, :].bitcast(F32), ALU.subtract
                                  ).then_inc(a_lo_s, 1)

            for f in range(2):
                half_out(g_f[:, f, :], B_FF + 4 * f, 0)
                hidden(f, B_FF + 4 * f + 2, 2, f + 1)
            with dve.Fori(0, FPAIRS - 1) as i:
                start = i * 24 + B_FF_LOOP
                half_out(g_f[:, 0, :], start, 0)
                for n in range(KT):
                    add_product(n, (2 * n + 2) % 4, start + (2 + 2 * n))
                hidden(0, start + 18, 2, i * 2 + 3)
                half_out(g_f[:, 1, :], start + 20, 0)
                hidden(1, start + 22, 2, i * 2 + 4)

            step(dve.memset(rms[:], 0.0))

            def last_add(c):
                half, j = divmod(c, KT)
                dve.wait_ge(bank_full, B_END + c + 1)
                hj = h[:, j, blk(half, HALF)]
                dve.tensor_tensor(hj, ps[:, c % 4, :], hj, ALU.add).then_inc(bank_free, 1)

            def last_raw(half):
                dve.wait_ge(mean_full, 5 + half)
                dve.tensor_scalar(rms[:, blk(half, HALF)], ps[:, 6 + half, :], EPS, None, ALU.add).then_inc(rms_raw, 1)

            def last_norm(half, ks):
                dve.wait_ge(rms_ready, 4 + half)
                for k in ks:
                    hk = h[:, k, blk(half, HALF)]
                    dve.scalar_tensor_tensor(hk, hk, gain[:, G_FINAL + k:G_FINAL + k + 1], rms[:, blk(half, HALF)],
                                             ALU.mult, ALU.mult).then_inc(out_ready, 1)

            for c in range(2 * KT):
                last_add(c)
                if c == NORM_AT:
                    last_raw(0)
            last_norm(0, range(KT))
            last_raw(1)
            last_norm(1, range(KT))


def tiles(w, cols):
    k, n = w.shape
    return w.reshape(k // P, P, n // cols, cols).transpose(2, 1, 0, 3).reshape(n // cols, P, k // P * cols)


def weight_stream(np, w_in, w_up_a, w_up_b, w_out, w_q_mem, w_kv_mem, w_o_mem, w_ffn_gate, w_ffn_up, w_ffn_down):
    w = tiles(w_in, P)
    out = list(tiles(w_kv_mem[:, :MH * P], P))
    values = w_kv_mem[:, MH * P:]
    first, second = (tiles(values[n:n + D // 2], NM) for n in (0, D // 2))
    for f, g in zip(first, second):
        out += [f, g]
    place = {"QA": 0, "KA": 4, "VA": 8, "QB": 12, "KB": 16, "VB": 20}
    out += [w[place[n]] for n in ("QA", "KA", "VA")]
    for i in range(PAIRS):
        for n in (ROUND if i < PAIRS - 1 else LAST).names:
            if n[0] == "G":
                out.append(w[24 + 4 * i + int(n[1])])
            else:
                out.append(w[place[n] + (i + 1 if n[1] == "A" else i)])
    out += list(np.concatenate([tiles(w_up_a, P), tiles(w_up_b, P)], axis=2))
    out += list(tiles(w_out, P))
    out += list(tiles(w_q_mem, P))
    o = tiles(w_o_mem, P)
    out += [np.concatenate([o[2 * n], o[2 * n + 1]], axis=1) for n in range(KT // 2)]
    g, u = tiles(w_ffn_gate, P), tiles(w_ffn_up, P)

    def down(pair):
        rows = w_ffn_down[pair * 2 * P:(pair + 1) * 2 * P]
        return list(tiles(rows, HALF))

    out += [g[0], u[0], g[1], u[1]]
    for p in range(1, FPAIRS):
        out += [g[2 * p], *down(p - 1), u[2 * p], g[2 * p + 1], u[2 * p + 1]]
    out += down(FPAIRS - 1)
    return np.stack(out)


def constants(np):
    ident = np.eye(P, dtype=np.float32)
    rope = np.zeros((P, 2), np.float32)
    freq = (500000.0 ** (-np.arange(8) / 8)).astype(np.float32)
    for head in (0, HD):
        rope[head:head + 8, 0] = rope[head + 8:head + 16, 0] = freq
        rope[head:head + 8, 1], rope[head + 8:head + 16, 1] = -1.0, 1.0
    dist = (T - P + np.arange(P))[:, None] - np.arange(T)[None, :]
    count = np.zeros(dist.shape, np.int64)
    for window, dilation in ((128, 1), (512, 4), (2048, 16)):
        count += (dist >= 0) & (dist <= window) & (dist % dilation == 0)
    bias = np.where(count > 0, np.log(np.maximum(count, 1)) * HD ** 0.5, TINY).astype(np.float32)
    mask = np.where(np.arange(P)[:, None] > np.arange(P)[None, :], 0.0, TINY).astype(np.float32)
    return ident, rope, bias, mask


def kernel(**inputs):
    import numpy as np
    import concourse.bacc as bacc
    from concourse.bass_utils import run_bass_kernel_spmd as run

    a = {n: np.asarray(v) for n, v in inputs.items()}
    layer = {n: a[n][0] for n in a if n.startswith(("w_", "g_")) and n != "g_final"}
    gains = [layer["g_mix"], layer["g_mem_q"], layer["g_mem_kv"], layer["g_ffn"], a["g_final"]]
    ident, rope, bias, mask = constants(np)
    arrays = {
        "x_t": a["x"][0].T.reshape(KT, P, T),
        "mem_t": a["mem"][0].T.reshape(KT, P, NM).transpose(1, 0, 2),
        "positions": a["positions"][0],
        "gains": np.concatenate([g.reshape(KT, P).T for g in gains], axis=1),
        "weights": weight_stream(np, **{n: w for n, w in layer.items() if n.startswith("w_")}),
        "ident": ident, "rope": rope, "bias": bias, "mask": mask,
    }
    arrays = {n: np.ascontiguousarray(v) for n, v in arrays.items()}
    nc = bacc.Bacc("TRN2", target_bir_lowering=False, num_devices=1)
    args = [nc.dram_tensor(f"{n}_in", v.shape, mybir.dt.from_np(v.dtype), kind="ExternalInput").ap()
            for n, v in arrays.items()]
    out = nc.dram_tensor("out_t", (KT, P, T), F32, kind="ExternalOutput").ap()
    build(nc, *args, out)
    r = run(nc, [{f"{n}_in": v for n, v in arrays.items()}], core_ids=[0])
    return r.results[0]["out_t"].reshape(D, T).T[None]
```
